# Optimizing a Trainium2 kernel written in Bass

```python
import math
import jax, jax.numpy as jnp
from jax import lax
import numpy as np

D_MODEL = 1024
BATCH = 1
SEQ = 256
DEPTH = 1

MOBA_HEADS = 8
MOBA_HEAD_DIM = 64
MOBA_WIDTH = MOBA_HEADS * MOBA_HEAD_DIM
MOBA_ROT_DIM = MOBA_HEAD_DIM // 4
MOBA_BLOCK = 256
MOBA_TOPK = 3
MOBA_Q_CHUNK = 128
MLA_HEADS = 8
MLA_NOPE = 64
MLA_ROPE = 32
MLA_V = 64
MLA_Q_LORA = 384
MLA_KV_LORA = 256
MLA_WIDTH = MLA_HEADS * MLA_V
MLA_Q_BLOCK = 128
ROPE_THETA = 500000.0
D_FF = 4 * D_MODEL
EPS = 1e-6
IN_WIDTH = 3 * MOBA_WIDTH + MLA_Q_LORA + MLA_KV_LORA + MLA_ROPE + 2 * D_MODEL


def _rms_norm(x, g):
    xf = x.astype(jnp.float32)
    y = xf * lax.rsqrt(jnp.mean(xf * xf, axis=-1, keepdims=True) + EPS)
    return (y * g.astype(jnp.float32)).astype(x.dtype)

def _split_cols(t, widths):
    out, start = [], 0
    for w in widths:
        out.append(t[..., start:start + w])
        start += w
    return out

def _rope(x, positions):
    r = x.shape[-1]
    half = r // 2
    inv_freq = ROPE_THETA ** (-jnp.arange(half, dtype=jnp.float32) * (2.0 / r))
    ang = positions.astype(jnp.float32)[..., None] * inv_freq
    cos = jnp.cos(ang)[:, :, None, :]
    sin = jnp.sin(ang)[:, :, None, :]
    xf = x.astype(jnp.float32)
    x1, x2 = xf[..., :half], xf[..., half:]
    return jnp.concatenate([x1 * cos - x2 * sin, x2 * cos + x1 * sin], axis=-1).astype(x.dtype)

def _partial_rope(x, positions):
    return jnp.concatenate([_rope(x[..., :MOBA_ROT_DIM], positions), x[..., MOBA_ROT_DIM:]], axis=-1)

def _moba_attention(q, k, v):
    B, S, H, Dh = q.shape
    nb = -(-S // MOBA_BLOCK)
    pad = nb * MOBA_BLOCK - S
    topk = min(MOBA_TOPK, nb)
    n_chunks = S // MOBA_Q_CHUNK
    scale = Dh ** -0.5
    qt = jnp.transpose(q, (0, 2, 1, 3))
    kp = jnp.pad(jnp.transpose(k, (0, 2, 1, 3)), ((0, 0), (0, 0), (0, pad), (0, 0)))
    vp = jnp.pad(jnp.transpose(v, (0, 2, 1, 3)), ((0, 0), (0, 0), (0, pad), (0, 0)))
    kb = kp.reshape(B, H, nb, MOBA_BLOCK, Dh)
    vb = vp.reshape(B, H, nb, MOBA_BLOCK, Dh)
    kmean = jnp.mean(kb.astype(jnp.float32), axis=3)
    head_idx = jnp.arange(H)[:, None, None]

    def per_batch(args):
        qb, kbb, vbb, kmb = args

        def per_chunk(c):
            q0 = c * MOBA_Q_CHUNK
            qc = lax.dynamic_slice_in_dim(qb, q0, MOBA_Q_CHUNK, axis=1)
            own = q0 // MOBA_BLOCK
            gate = jnp.einsum('hqd,hnd->hqn', qc.astype(jnp.float32), kmb)
            gate = jnp.where(jnp.arange(nb)[None, None, :] < own, gate, -jnp.inf)
            _, idx = lax.top_k(gate, topk)
            valid = jnp.arange(topk) < own
            kg = kbb[head_idx, idx]
            vg = vbb[head_idx, idx]
            s_past = jnp.einsum('hqd,hqnkd->hqnk', qc, kg).astype(jnp.float32) * scale
            s_past = jnp.where(valid[None, None, :, None], s_past, -jnp.inf)
            s_past = s_past.reshape(H, MOBA_Q_CHUNK, topk * MOBA_BLOCK)
            k_own = lax.dynamic_index_in_dim(kbb, own, axis=1, keepdims=False)
            v_own = lax.dynamic_index_in_dim(vbb, own, axis=1, keepdims=False)
            s_own = jnp.einsum('hqd,hkd->hqk', qc, k_own).astype(jnp.float32) * scale
            qpos = q0 + jnp.arange(MOBA_Q_CHUNK)
            kpos = own * MOBA_BLOCK + jnp.arange(MOBA_BLOCK)
            s_own = jnp.where(kpos[None, None, :] <= qpos[None, :, None], s_own, -jnp.inf)
            p = jax.nn.softmax(jnp.concatenate([s_past, s_own], axis=-1), axis=-1).astype(v.dtype)
            p_past = p[..., :topk * MOBA_BLOCK].reshape(H, MOBA_Q_CHUNK, topk, MOBA_BLOCK)
            p_own = p[..., topk * MOBA_BLOCK:]
            return (jnp.einsum('hqnk,hqnkd->hqd', p_past, vg)
                    + jnp.einsum('hqk,hkd->hqd', p_own, v_own))

        outs = lax.map(per_chunk, jnp.arange(n_chunks))
        return jnp.transpose(outs, (1, 0, 2, 3)).reshape(H, S, Dh)

    o = lax.map(per_batch, (qt, kb, vb, kmean))
    return jnp.transpose(o, (0, 2, 1, 3))

def _mla_attention(q_nope, q_rope, k_nope, k_rope, v):
    S = q_nope.shape[1]
    scale = (MLA_NOPE + MLA_ROPE) ** -0.5
    outs = []
    for c in range(S // MLA_Q_BLOCK):
        q0, q1 = c * MLA_Q_BLOCK, (c + 1) * MLA_Q_BLOCK
        s = (jnp.einsum('bqhd,bkhd->bhqk', q_nope[:, q0:q1], k_nope[:, :q1])
             + jnp.einsum('bqhr,bkr->bhqk', q_rope[:, q0:q1], k_rope[:, :q1]))
        s = s.astype(jnp.float32) * scale
        mask = jnp.arange(q1)[None, :] <= (q0 + jnp.arange(MLA_Q_BLOCK))[:, None]
        s = jnp.where(mask[None, None], s, -jnp.inf)
        p = jax.nn.softmax(s, axis=-1).astype(v.dtype)
        outs.append(jnp.einsum('bhqk,bkhd->bqhd', p, v[:, :q1]))
    return jnp.concatenate(outs, axis=1)

def first_inputs(seed: int = 0) -> dict:
    key = jax.random.key(seed)
    ks = jax.random.split(key, 20)
    f32 = jnp.float32

    def w(k, shape, fan_in):
        return jax.random.normal(k, shape, f32) * (fan_in ** -0.5)

    def gain(k, n):
        return 1.0 + 0.1 * jax.random.normal(k, (DEPTH, n), f32)

    x = jax.random.normal(ks[0], (BATCH, SEQ, D_MODEL), f32)
    offsets = jax.random.randint(ks[1], (BATCH, 1), 0, 4096)
    positions = (offsets + jnp.arange(SEQ)[None, :]).astype(jnp.int32)
    return {
        "x": x,
        "positions": positions,
        "g_pre_mix": gain(ks[2], D_MODEL),
        "w_in": w(ks[3], (DEPTH, D_MODEL, IN_WIDTH), D_MODEL),
        "b_gate": 0.01 * jax.random.normal(ks[4], (DEPTH, 2 * D_MODEL), f32),
        "g_q_norm": gain(ks[5], MLA_Q_LORA),
        "w_uq": w(ks[6], (DEPTH, MLA_Q_LORA, MLA_HEADS * (MLA_NOPE + MLA_ROPE)), MLA_Q_LORA),
        "g_kv_norm": gain(ks[7], MLA_KV_LORA),
        "w_ukv": w(ks[8], (DEPTH, MLA_KV_LORA, MLA_HEADS * (MLA_NOPE + MLA_V)), MLA_KV_LORA),
        "w_branch_a": w(ks[9], (DEPTH, MOBA_WIDTH, D_MODEL), MOBA_WIDTH),
        "w_branch_b": w(ks[10], (DEPTH, MLA_WIDTH, D_MODEL), MLA_WIDTH),
        "w_out": w(ks[11], (DEPTH, D_MODEL, D_MODEL), D_MODEL),
        "g_post_mix": gain(ks[12], D_MODEL),
        "g_pre_mlp": gain(ks[13], D_MODEL),
        "w_up": w(ks[14], (DEPTH, D_MODEL, D_FF), D_MODEL),
        "w_down": w(ks[15], (DEPTH, D_FF, D_MODEL), D_FF),
        "g_post_mlp": gain(ks[16], D_MODEL),
    }

def first_block(x, positions, g_pre_mix, w_in, b_gate, g_q_norm, w_uq, g_kv_norm, w_ukv,
              w_branch_a, w_branch_b, w_out, g_post_mix, g_pre_mlp, w_up, w_down, g_post_mlp):
    B, S, _ = x.shape
    for l in range(DEPTH):
        h = _rms_norm(x, g_pre_mix[l])
        proj = h @ w_in[l]
        qa, ka, va, c_q, c_kv, k_r, gate_logits = _split_cols(
            proj, [MOBA_WIDTH, MOBA_WIDTH, MOBA_WIDTH, MLA_Q_LORA, MLA_KV_LORA, MLA_ROPE, 2 * D_MODEL])
        qa = _partial_rope(qa.reshape(B, S, MOBA_HEADS, MOBA_HEAD_DIM), positions)
        ka = _partial_rope(ka.reshape(B, S, MOBA_HEADS, MOBA_HEAD_DIM), positions)
        va = va.reshape(B, S, MOBA_HEADS, MOBA_HEAD_DIM)
        o_a = _moba_attention(qa, ka, va).reshape(B, S, MOBA_WIDTH) @ w_branch_a[l]
        q = (_rms_norm(c_q, g_q_norm[l]) @ w_uq[l]).reshape(B, S, MLA_HEADS, MLA_NOPE + MLA_ROPE)
        q_nope = q[..., :MLA_NOPE]
        q_rope = _rope(q[..., MLA_NOPE:], positions)
        kv = (_rms_norm(c_kv, g_kv_norm[l]) @ w_ukv[l]).reshape(B, S, MLA_HEADS, MLA_NOPE + MLA_V)
        k_nope, v_b = kv[..., :MLA_NOPE], kv[..., MLA_NOPE:]
        k_rope = _rope(k_r[:, :, None, :], positions)[:, :, 0, :]
        o_b = _mla_attention(q_nope, q_rope, k_nope, k_rope, v_b).reshape(B, S, MLA_WIDTH) @ w_branch_b[l]
        gates = jax.nn.sigmoid((gate_logits + b_gate[l]).astype(jnp.float32)).astype(x.dtype)
        merged = gates[..., :D_MODEL] * o_a + gates[..., D_MODEL:] * o_b
        x = x + _rms_norm(merged @ w_out[l], g_post_mix[l])
        h2 = _rms_norm(x, g_pre_mlp[l])
        m = jnp.square(jax.nn.relu(h2 @ w_up[l])) @ w_down[l]
        x = x + _rms_norm(m, g_post_mlp[l])
    return x


DEPTH_2 = 2

N_MIXERS = 2

HG_HEADS = 8
HG_DK = D_MODEL // HG_HEADS
HG_DV = D_MODEL // HG_HEADS
HG_KDIM = HG_HEADS * HG_DK
HG_VDIM = HG_HEADS * HG_DV
HG_CHUNK = 64
N_HGRN = (DEPTH_2 + 1) // 2

LRU_WIDTH = D_MODEL
LRU_BLOCKS = 4
LRU_BW = LRU_WIDTH // LRU_BLOCKS
CONV_WIDTH = 4
LRU_C = 8.0
N_LRU = DEPTH_2 // 2

D_FF_2 = ((8 * D_MODEL // 3 + 255) // 256) * 256


def rmsnorm(x, w):
    xf = x.astype(jnp.float32)
    y = xf * lax.rsqrt(jnp.mean(xf * xf, axis=-1, keepdims=True) + EPS) * w.astype(jnp.float32)
    return y.astype(x.dtype)

def hgrn2_mixer(h, w_in, lb, norm_w, w_out):
    B, S, _ = h.shape
    C = HG_CHUNK
    nc = S // C
    proj = h @ w_in
    q, fl, v, g = jnp.split(proj, [HG_KDIM, 2 * HG_KDIM, 2 * HG_KDIM + HG_VDIM], axis=-1)
    q = jax.nn.silu(q.astype(jnp.float32))
    fl = fl.astype(jnp.float32)
    lbv = lb.astype(jnp.float32)
    log_f = jnp.logaddexp(jnp.log(lbv), jnp.log1p(-lbv) + jax.nn.log_sigmoid(fl))
    k = (1.0 - lbv) * jax.nn.sigmoid(-fl)

    def to_chunks(t, d):
        return t.reshape(B, nc, C, HG_HEADS, d).transpose(1, 0, 3, 2, 4)

    qc = to_chunks(q, HG_DK)
    kc = to_chunks(k, HG_DK)
    vc = to_chunks(v.astype(jnp.float32), HG_DV)
    bc = jnp.cumsum(to_chunks(log_f, HG_DK), axis=3)
    causal = jnp.tril(jnp.ones((C, C), dtype=bool))[:, :, None]

    def step(state, inp):
        qb, kb, vb, bb = inp
        rel = bb[:, :, :, None, :] - bb[:, :, None, :, :]
        decay = jnp.exp(jnp.where(causal, rel, -jnp.inf))
        scores = jnp.einsum('bhtk,bhtsk,bhsk->bhts', qb, decay, kb)
        o = jnp.einsum('bhts,bhsv->bhtv', scores, vb) + jnp.einsum('bhtk,bhkv->bhtv', qb * jnp.exp(bb), state)
        b_last = bb[:, :, -1, :]
        state = jnp.exp(b_last)[..., None] * state + jnp.einsum(
            'bhsk,bhsv->bhkv', kb * jnp.exp(b_last[:, :, None, :] - bb), vb)
        return state, o

    s0 = jnp.zeros((B, HG_HEADS, HG_DK, HG_DV), jnp.float32)
    _, oc = lax.scan(step, s0, (qc, kc, vc, bc))
    o = oc.transpose(1, 0, 3, 2, 4).reshape(B, S, HG_HEADS, HG_DV)
    o = o * lax.rsqrt(jnp.mean(o * o, axis=-1, keepdims=True) + EPS) * norm_w.astype(jnp.float32)
    o = o.reshape(B, S, HG_VDIM) * jax.nn.silu(g.astype(jnp.float32))
    return o.astype(h.dtype) @ w_out

def rglru_mixer(h, w_in, conv_w, conv_b, wa, ba, wx, bx, lam, w_out):
    B, S, _ = h.shape
    proj = h @ w_in
    y, u = jnp.split(proj, [LRU_WIDTH], axis=-1)
    y = jax.nn.gelu(y.astype(jnp.float32))
    u = u.astype(jnp.float32)
    u_pad = jnp.pad(u, ((0, 0), (CONV_WIDTH - 1, 0), (0, 0)))
    cw = conv_w.astype(jnp.float32)
    uc = conv_b.astype(jnp.float32)
    for tap in range(CONV_WIDTH):
        uc = uc + u_pad[:, tap:tap + S, :] * cw[tap]
    ub = uc.reshape(B, S, LRU_BLOCKS, LRU_BW)
    r = jax.nn.sigmoid(jnp.einsum('bsnc,ncd->bsnd', ub, wa.astype(jnp.float32)).reshape(B, S, LRU_WIDTH)
                       + ba.astype(jnp.float32))
    ig = jax.nn.sigmoid(jnp.einsum('bsnc,ncd->bsnd', ub, wx.astype(jnp.float32)).reshape(B, S, LRU_WIDTH)
                        + bx.astype(jnp.float32))
    log_a = -LRU_C * r * jax.nn.softplus(-lam.astype(jnp.float32))
    a = jnp.exp(log_a)
    b_in = jnp.sqrt(-jnp.expm1(2.0 * log_a)) * (ig * uc)

    def combine(left, right):
        a1, b1 = left
        a2, b2 = right
        return a1 * a2, a2 * b1 + b2

    _, hs = lax.associative_scan(combine, (a, b_in), axis=1)
    return (hs * y).astype(h.dtype) @ w_out

def swiglu(h, w_in, w_out):
    gate, up = jnp.split(h @ w_in, [D_FF_2], axis=-1)
    return (jax.nn.silu(gate) * up) @ w_out

def second_inputs(seed: int = 0) -> dict:
    key = jax.random.key(seed)
    ks = jax.random.split(key, 24)
    f32 = jnp.float32
    D = D_MODEL

    def nrm(k, shape, fan_in):
        return jax.random.normal(k, shape, f32) * (fan_in ** -0.5)

    x = jax.random.normal(ks[0], (BATCH, SEQ, D), f32)
    norm_mix = 1.0 + 0.02 * jax.random.normal(ks[1], (DEPTH_2, D), f32)
    norm_ffn = 1.0 + 0.02 * jax.random.normal(ks[2], (DEPTH_2, D), f32)
    norm_final = 1.0 + 0.02 * jax.random.normal(ks[3], (D,), f32)

    hgrn_w_in = nrm(ks[4], (N_HGRN, D, 2 * HG_KDIM + 2 * HG_VDIM), D)
    hgrn_lb = 0.1 * jax.random.normal(ks[5], (N_HGRN + 1, HG_KDIM), f32)
    hgrn_norm = 1.0 + 0.02 * jax.random.normal(ks[6], (N_HGRN, HG_DV), f32)
    hgrn_w_out = nrm(ks[7], (N_HGRN, HG_VDIM, D), HG_VDIM)

    lru_w_in = nrm(ks[8], (N_LRU, D, 2 * LRU_WIDTH), D)
    lru_conv_w = nrm(ks[9], (N_LRU, CONV_WIDTH, LRU_WIDTH), CONV_WIDTH)
    lru_conv_b = 0.01 * jax.random.normal(ks[10], (N_LRU, LRU_WIDTH), f32)
    lru_wa = nrm(ks[11], (N_LRU, LRU_BLOCKS, LRU_BW, LRU_BW), LRU_BW)
    lru_ba = 0.01 * jax.random.normal(ks[12], (N_LRU, LRU_WIDTH), f32)
    lru_wx = nrm(ks[13], (N_LRU, LRU_BLOCKS, LRU_BW, LRU_BW), LRU_BW)
    lru_bx = 0.01 * jax.random.normal(ks[14], (N_LRU, LRU_WIDTH), f32)
    a0 = jax.random.uniform(ks[15], (N_LRU, LRU_WIDTH), f32, 0.9, 0.999)
    s = a0 ** (1.0 / LRU_C)
    lru_lambda = jnp.log(s) - jnp.log1p(-s)
    lru_w_out = nrm(ks[16], (N_LRU, LRU_WIDTH, D), LRU_WIDTH)

    ffn_w_in = nrm(ks[17], (DEPTH_2, D, 2 * D_FF_2), D)
    ffn_w_out = nrm(ks[18], (DEPTH_2, D_FF_2, D), D_FF_2)

    return {"x": x, "norm_mix": norm_mix, "norm_ffn": norm_ffn, "norm_final": norm_final,
            "hgrn_w_in": hgrn_w_in, "hgrn_lb": hgrn_lb, "hgrn_norm": hgrn_norm, "hgrn_w_out": hgrn_w_out,
            "lru_w_in": lru_w_in, "lru_conv_w": lru_conv_w, "lru_conv_b": lru_conv_b,
            "lru_wa": lru_wa, "lru_ba": lru_ba, "lru_wx": lru_wx, "lru_bx": lru_bx,
            "lru_lambda": lru_lambda, "lru_w_out": lru_w_out,
            "ffn_w_in": ffn_w_in, "ffn_w_out": ffn_w_out}

def second_block(x, norm_mix, norm_ffn, norm_final, hgrn_w_in, hgrn_lb, hgrn_norm, hgrn_w_out,
              lru_w_in, lru_conv_w, lru_conv_b, lru_wa, lru_ba, lru_wx, lru_bx, lru_lambda, lru_w_out,
              ffn_w_in, ffn_w_out):
    lb_all = jnp.cumsum(jax.nn.softmax(hgrn_lb.astype(jnp.float32), axis=0), axis=0)
    for l in range(DEPTH_2):
        j = l // N_MIXERS
        hn = rmsnorm(x, norm_mix[l])
        if l % N_MIXERS == 0:
            mix = hgrn2_mixer(hn, hgrn_w_in[j], lb_all[j], hgrn_norm[j], hgrn_w_out[j])
        else:
            mix = rglru_mixer(hn, lru_w_in[j], lru_conv_w[j], lru_conv_b[j], lru_wa[j], lru_ba[j],
                              lru_wx[j], lru_bx[j], lru_lambda[j], lru_w_out[j])
        x = x + mix
        x = x + swiglu(rmsnorm(x, norm_ffn[l]), ffn_w_in[l], ffn_w_out[l])
    return rmsnorm(x, norm_final)


def setup_inputs(seed=0):
    out = dict(first_inputs(seed))
    for name, value in second_inputs(seed + 1).items():
        if name != "x":
            out[name + "_2"] = value
    return out


def reference(
    x, positions, g_pre_mix, w_in, b_gate, g_q_norm, w_uq, g_kv_norm, w_ukv, w_branch_a,
    w_branch_b, w_out, g_post_mix, g_pre_mlp, w_up, w_down, g_post_mlp, norm_mix_2, norm_ffn_2,
    norm_final_2, hgrn_w_in_2, hgrn_lb_2, hgrn_norm_2, hgrn_w_out_2, lru_w_in_2, lru_conv_w_2,
    lru_conv_b_2, lru_wa_2, lru_ba_2, lru_wx_2, lru_bx_2, lru_lambda_2, lru_w_out_2, ffn_w_in_2,
    ffn_w_out_2,
):
    x = first_block(
        x, positions, g_pre_mix, w_in, b_gate, g_q_norm, w_uq, g_kv_norm, w_ukv, w_branch_a,
        w_branch_b, w_out, g_post_mix, g_pre_mlp, w_up, w_down, g_post_mlp,
    )
    return second_block(
        x, norm_mix_2, norm_ffn_2, norm_final_2, hgrn_w_in_2, hgrn_lb_2, hgrn_norm_2,
        hgrn_w_out_2, lru_w_in_2, lru_conv_w_2, lru_conv_b_2, lru_wa_2, lru_ba_2, lru_wx_2,
        lru_bx_2, lru_lambda_2, lru_w_out_2, ffn_w_in_2, ffn_w_out_2,
    )


_drawn_inputs = setup_inputs


def setup_inputs(seed=0):
    import zlib

    import numpy as np

    out = dict(_drawn_inputs(seed))
    spreads = {}
    factors = {'b_gate': 8.0,
     'norm_mix_2': 3.044,
     'norm_ffn_2': 4.676,
     'norm_final_2': 8.176,
     'hgrn_lb_2': 8.0,
     'hgrn_norm_2': 7.107,
     'lru_conv_b_2': 14.922,
     'lru_ba_2': 64.0,
     'lru_bx_2': 64.0}
    for name, (base, spread) in spreads.items():
        noise = np.random.default_rng([zlib.crc32(name.encode()), seed]).standard_normal(out[name].shape)
        drawn = base * np.exp(spread * noise) if base else spread * noise
        out[name] = __import__('jax').numpy.asarray(drawn.astype(out[name].dtype))
    for name, factor in factors.items():
        out[name] = (out[name] * factor).astype(out[name].dtype)
    return out
```

```python
import numpy as np
import concourse.bass as bass
from concourse import mybir
from contextlib import ExitStack

F32 = mybir.dt.float32
F32R = mybir.dt.float32r
I32 = mybir.dt.int32
U8 = mybir.dt.uint8
ALU = mybir.AluOpType
ACT = mybir.ActivationFunctionType
AX = mybir.AxisListType.X

EPS = 1e-6
TWO_PI = 2.0 * np.pi
PI_1 = 6.28125
PI_2 = 0.00193500518798828125
PI_3 = float(TWO_PI - PI_1 - PI_2)
MAGIC = 12582912.0

C_LB0, C_LB1, C_CONVB, C_BA, C_BX, C_LAM, C_CONVW, C_N = 0, 8, 16, 24, 32, 40, 48, 80
R_PRE_MIX, R_POST_MIX, R_PRE_MLP, R_POST_MLP = 0, 1024, 2048, 3072
R_MIX0, R_MIX1, R_FFN0, R_FFN1, R_FINAL = 4096, 5120, 6144, 7168, 8192
R_BGATE, R_HNORM, R_QN, R_KVN, R_N = 9216, 11264, 12288, 12672, 12928


def chunk_list():
    out = []

    def a_type(name, col, width, kt, group):
        for k in range(0, kt, group):
            out.append((("a", name, col, width, k, min(group, kt - k)), width * min(group, kt - k)))

    def s_type(pairs, kt):
        out.append((("s", tuple(pairs), kt), 128 * kt * len(pairs)))

    for col, width in ((0, 512), (512, 512), (1024, 512), (1536, 384), (1920, 288)):
        a_type("w_in", col, width, 8, 4)
    for n in range(4):
        a_type("w_in", 2208 + 512 * n, 512, 8, 4)
    a_type("w_uq", 0, 384, 3, 3)
    a_type("w_uq", 384, 384, 3, 3)
    a_type("w_ukv", 0, 512, 2, 2)
    a_type("w_ukv", 512, 512, 2, 2)
    for n in range(2):
        a_type("w_branch_a", 512 * n, 512, 4, 4)
        a_type("w_branch_b", 512 * n, 512, 4, 4)
    for n in range(2):
        a_type("w_out", 512 * n, 512, 8, 4)

    def mlp(up, down, units):
        for j in range(units + 1):
            if j < units:
                for u in up(j):
                    s_type(u, 8)
            if j:
                out.append((("d", down, j - 1), 2048))

    mlp(lambda j: [[("w_up", 2 * j), ("w_up", 2 * j + 1)]], "w_down", 16)
    for h in range(8):
        s_type([("hgrn_w_in", h), ("hgrn_w_in", 8 + h)], 8)
    for n in range(4):
        a_type("hgrn_w_in", 2048 + 512 * n, 512, 8, 4)
    for n in range(2):
        a_type("hgrn_w_out", 512 * n, 512, 8, 4)
    mlp(lambda j: [[("ffn_in0", f), ("ffn_in0", 22 + f)] for f in (2 * j, 2 * j + 1)], "ffn_out0", 11)
    for f in range(8):
        s_type([("lru_w_in", f), ("lru_w_in", 8 + f)], 8)
    for n in range(0, 4, 2):
        out.append((("g", n), 2048))
    for n in range(2):
        a_type("lru_w_out", 512 * n, 512, 8, 4)
    mlp(lambda j: [[("ffn_in1", f), ("ffn_in1", 22 + f)] for f in (2 * j, 2 * j + 1)], "ffn_out1", 11)
    return out


def lay_chunk(w, key):
    if key[0] == "a":
        _, name, col, width, k, n = key
        return w[name][128 * k:128 * (k + n), col:col + width].reshape(n, 128, width).transpose(1, 0, 2)
    if key[0] == "s":
        _, pairs, kt = key
        return np.concatenate([w[name][:, 128 * f:128 * f + 128].reshape(kt, 128, 128).transpose(1, 0, 2)
                               for name, f in pairs], axis=1)
    if key[0] == "d":
        _, name, j = key
        return w[name][256 * j:256 * j + 256].reshape(2, 128, 1024).transpose(1, 0, 2)
    n = key[1]
    return np.concatenate([w[name][m].reshape(2, 128, 256).transpose(1, 0, 2)
                           for m in (n, n + 1) for name in ("lru_wa", "lru_wx")], axis=1)


def program(nc, x_d, pos_d, w_d, cols_d, rows_d, const_d, out_d):
    NRAW, NHL = 3, 4
    ENG = ("pe", "act", "dve", "pool", "sp")
    chunks = chunk_list()
    offs = np.concatenate([[0], np.cumsum([128 * wd for _, wd in chunks])]).tolist()

    ctx = ExitStack()
    with ctx:
        def sb(name, shape, dt=F32):
            return ctx.enter_context(nc.sbuf_tensor(name, shape, dt))

        raw = sb("raw", [128, NRAW, 2048])
        wH = sb("wH", [128, NHL, 2048], F32R)
        wL = sb("wL", [128, NHL, 2048], F32R)
        xr = sb("xr", [128, 2, 1024])
        xn = sb("xn", [128, 2, 1024])
        aH = sb("aH", [128, 8, 256], F32R)
        aL = sb("aL", [128, 8, 256], F32R)
        RR = sb("RR", [128, 4608], F32R)
        bc = sb("bc", [128, 1024])
        ident = sb("ident", [128, 128])
        amask = sb("amask", [128, 384])
        hmask = sb("hmask", [128, 8, 128], U8)
        cols = sb("cols", [128, C_N])
        st = sb("st", [128, 256])
        consts = sb("consts", [128, 32])
        FF = sb("FF", [128, 14848])
        ps = ctx.enter_context(nc.psum_tensor("ps", [128, 8, 512], F32))

        sems = {e: ctx.enter_context(nc.semaphore(f"s_{e}")) for e in ENG}
        for n in range(NRAW):
            sems[f"raw{n}"] = ctx.enter_context(nc.semaphore(f"s_raw{n}"))
        for n in ("in", "bc", "bg", "out"):
            sems[n] = ctx.enter_context(nc.semaphore(f"s_{n}"))
        queue = {e: [] for e in ENG}
        count = {s: 0 for s in sems}
        seen = {e: {} for e in ENG}

        def wait(e, after):
            for t in after:
                if t is None:
                    continue
                s, v = t
                if seen[e].get(s, 0) < v:
                    seen[e][s] = v
                    queue[e].append(lambda eng, s=s, v=v: eng.wait_ge(sems[s], v))

        def op(e, after, fn):
            wait(e, after)
            queue[e].append(lambda eng: fn(eng).then_inc(sems[e], 1))
            count[e] += 1
            return (e, count[e])

        def dma(sem, after, dst, src, e="sp"):
            wait(e, after)
            queue[e].append(lambda eng: eng.dma_start(dst, src).then_inc(sems[sem], 16))
            count[sem] += 16
            return (sem, count[sem])

        dma_t, split_t, done_t = [], [], []

        def load_chunk(i):
            wd = chunks[i][1]
            free = split_t[i - NRAW] if i >= NRAW else []
            src = w_d[offs[i]:offs[i + 1]].rearrange("(p n) -> p n", p=128)
            dma_t.append(dma(f"raw{i % NRAW}", free, raw[:, i % NRAW, 0:wd], src))

        def split_chunk(i):
            wd = chunks[i][1]
            free = [done_t[i - NHL]] if i >= NHL else []
            r, h, l = raw[:, i % NRAW, 0:wd], wH[:, i % NHL, 0:wd], wL[:, i % NHL, 0:wd]
            th = op("act", free + [dma_t[i]], lambda e: e.activation(h, r, ACT.Copy))
            tl = op("dve", free + [dma_t[i], th],
                    lambda e: e.tensor_tensor(l, r, h.bitcast(F32), ALU.subtract))
            split_t.append([th, tl])

        def pump():
            while len(split_t) < len(chunks) and len(split_t) - NHL < len(done_t):
                while len(dma_t) < min(len(chunks), len(split_t) + NRAW):
                    load_chunk(len(dma_t))
                split_chunk(len(split_t))
            while len(dma_t) < min(len(chunks), len(split_t) + NRAW):
                load_chunk(len(dma_t))

        def take(key):
            i = len(done_t)
            assert chunks[i][0] == key, (chunks[i][0], key)
            pump()
            return wH[:, i % NHL, :], wL[:, i % NHL, :], split_t[i]

        def mm3(eng, out, lhs, rhs, start, stop):
            eng.matmul(out, lhs[0], rhs[1], start=start, stop=False)
            eng.matmul(out, lhs[1], rhs[0], start=False, stop=False)
            return eng.matmul(out, lhs[0], rhs[0], start=False, stop=stop)

        bank_t = [[] for _ in range(8)]

        def a_mm(name, col, width, kt, group, lhs, banks, after):
            t = None
            for k in range(0, kt, group):
                n = min(group, kt - k)
                h, l, ready = take(("a", name, col, width, k, n))

                def go(eng, k=k, n=n, h=h, l=l):
                    for tok in range(2):
                        for j in range(n):
                            s = slice(128 * tok, 128 * tok + 128)
                            w = slice(j * width, (j + 1) * width)
                            last = mm3(eng, ps[:, banks[tok], 0:width], (lhs[0][:, k + j, s], lhs[1][:, k + j, s]),
                                       (h[:, w], l[:, w]), k + j == 0, k + j == kt - 1)
                    return last
                t = op("pe", after + ready + bank_t[banks[0]] + bank_t[banks[1]], go)
                done_t.append(t)
            return t

        def s_mm(pairs, rhs, outs, after):
            h, l, ready = take(("s", tuple(pairs), 8))

            def go(eng):
                for i, out in enumerate(outs):
                    for k in range(8):
                        w = slice((8 * i + k) * 128, (8 * i + k + 1) * 128)
                        last = mm3(eng, out, (h[:, w], l[:, w]), (rhs[0][:, k, :], rhs[1][:, k, :]),
                                   k == 0, k == 7)
                return last
            t = op("pe", after + ready, go)
            done_t.append(t)
            return t

        def bcast(off, width, after):
            return dma("bc", after, bc[:, 0:width],
                       rows_d[off:off + width].partition_broadcast(128))

        stat = [0]

        def stats(n):
            stat[0] += n
            assert stat[0] <= 256
            return st[:, stat[0] - n:stat[0]]

        def power(ss, n, inv, after):
            out = stats(n)
            t = op("pool", after, lambda e: e.tensor_scalar(out, ss, inv, EPS, ALU.mult, ALU.add))
            t = op("pool", [t], lambda e: e.tensor_tensor(out, out, consts[:, 0:1].to_broadcast([128, n])
                                                          if n > 1 else consts[:, 0:1], ALU.pow))
            return out, t

        def transposes(src, kt, banks, dst, after, free, width=128):
            out = []
            g = 0
            for tok in range(2):
                for k0 in range(0, kt, 4):
                    n = min(4, kt - k0)
                    b = banks[g % len(banks)]
                    g += 1

                    def go(eng, tok=tok, k0=k0, n=n, b=b):
                        for j in range(n):
                            last = eng.transpose(ps[0:width, b, 128 * j:128 * j + 128], src(tok, k0 + j), ident[:, :])
                        return last
                    t = op("pe", after[tok] + bank_t[b], go)
                    pv = ps[0:width, b, 0:128 * n].rearrange("p (k t) -> p k t", t=128)
                    s = slice(128 * tok, 128 * tok + 128)
                    if len(dst) == 2:
                        h, l = dst[0][:, k0:k0 + n, s], dst[1][:, k0:k0 + n, s]
                        th = op("act", [t] + free, lambda e, h=h, pv=pv: e.activation(h, pv, ACT.Copy))
                        tl = op("dve", [th] + free, lambda e, h=h, l=l, pv=pv:
                                e.tensor_tensor(l, pv, h.bitcast(F32), ALU.subtract))
                        bank_t[b] = [th, tl]
                        out += [th, tl]
                    else:
                        d = dst[0][:, k0:k0 + n, s]
                        th = op("act", [t] + free, lambda e, d=d, pv=pv: e.activation(d, pv, ACT.Copy))
                        bank_t[b] = [th]
                        out.append(th)
            return out

        def norm_parts(src, width, scratch, gain, gain_t, dst, after, banks=(4, 5, 6, 7), free=()):
            ready = []
            for tok in range(2):
                ss = stats(1)
                t = op("act", after[tok], lambda e, tok=tok, ss=ss:
                       e.activation(scratch(tok), src(tok), ACT.Square, accum_out=ss))
                rs, tp = power(ss, 1, 1.0 / width, [t])
                t = op("dve", [tp, gain_t, t], lambda e, tok=tok, rs=rs:
                       e.scalar_tensor_tensor(scratch(tok), src(tok), rs, gain, ALU.mult, ALU.mult))
                ready.append([t])
            return transposes(lambda tok, k: scratch(tok)[:, 128 * k:128 * k + 128], width // 128, banks, dst,
                              ready, list(free)), ready

        def post_norm(gain_t, after):
            out = []
            for tok in range(2):
                ss = stats(1)
                y = ps[:, 2 * tok:2 * tok + 2, :]
                d = xn[:, tok, :].rearrange("p (b n) -> p b n", b=2)
                g = bc[:, :].rearrange("p (b n) -> p b n", b=2)
                t1 = op("act", after, lambda e, y=y, d=d, ss=ss: e.activation(d, y, ACT.Square, accum_out=ss))
                rs, tp = power(ss, 1, 1.0 / 1024, [t1])
                t = op("dve", [tp, t1, gain_t], lambda e, y=y, d=d, g=g, rs=rs:
                       e.scalar_tensor_tensor(d, y, rs, g, ALU.mult, ALU.mult))
                bank_t[2 * tok] = bank_t[2 * tok + 1] = [t]
                out.append(op("dve", [t], lambda e, tok=tok:
                              e.tensor_tensor(xr[:, tok, :], xr[:, tok, :], xn[:, tok, :], ALU.add)))
            return out

        def add_mix(after):
            out = []
            for tok in range(2):
                v = xr[:, tok, :].rearrange("p (b n) -> p b n", b=2)
                t = op("dve", after, lambda e, tok=tok, v=v:
                       e.tensor_tensor(v, ps[:, 2 * tok:2 * tok + 2, :], v, ALU.add))
                bank_t[2 * tok] = bank_t[2 * tok + 1] = [t]
                out.append(t)
            return out

        def project(name, kt, lhs, after):
            for n in range(2):
                t = a_mm(name, 512 * n, 512, kt, 4, lhs, (n, 2 + n), after)
            return t

        c_sync = [
            dma("in", [], xr[:, :, :], x_d.rearrange("(t p) n -> p t n", p=128)),
        ]
        c_sync.append(dma("in", [], ident[:, :], const_d[:, 0:128]))
        c_sync.append(dma("in", [], amask[:, :], const_d[:, 128:512]))
        posi = FF[:, 0:2].bitcast(I32)
        c_sync.append(dma("in", [], posi, pos_d))
        invf = FF[:, 16:40]
        c_sync.append(dma("in", [], invf, const_d[:, 512:536]))
        c_sync.append(dma("in", [], cols[:, :], cols_d))
        mtmp0 = FF[:, 3072:4096]
        c_sync.append(dma("in", [], mtmp0, const_d[:, 536:1560]))
        t_in = c_sync[-1]
        t_bc = bcast(R_PRE_MIX, 1024, [])
        bgate = FF[:, 12800:14848]
        t_bg = dma("bg", [], bgate, rows_d[R_BGATE:R_BGATE + 2048].partition_broadcast(128))
        t_c = op("dve", [], lambda e: e.memset(consts[:, 0:1], -0.5))
        t_c = op("dve", [], lambda e: e.memset(consts[:, 1:2], float(np.pi / 2)))
        t_hm = op("dve", [t_in], lambda e: e.tensor_copy(hmask[:, :, :].rearrange("p l t -> p (l t)"), mtmp0))
        pump()

        t_h, t_xn = norm_parts(lambda tok: xr[:, tok, :], 1024, lambda tok: xn[:, tok, :], bc[:, :], t_bc,
                               (aH, aL), [[t_in, t_c], [t_in, t_c]])
        act = (aH, aL)

        posf, ang, nn, rr, ab = (FF[:, 48:50], FF[:, 64:112], FF[:, 128:176], FF[:, 192:240], FF[:, 256:304])
        rope = FF[:, 8256:8352]
        sn, cs = rope[:, 0:48], rope[:, 48:96]
        t = op("dve", [t_in], lambda e: e.tensor_copy(posf, posi))
        for tok in range(2):
            ta = op("dve", [t], lambda e, tok=tok:
                    e.tensor_scalar(ang[:, 24 * tok:24 * tok + 24], invf, posf[:, tok:tok + 1], None, ALU.mult))
        t = op("dve", [ta], lambda e: e.tensor_scalar(nn, ang, 1.0 / TWO_PI, MAGIC, ALU.mult, ALU.add))
        t = op("dve", [t], lambda e: e.tensor_scalar(nn, nn, MAGIC, None, ALU.subtract))
        src = ang
        for part in (PI_1, PI_2, PI_3):
            t = op("dve", [t], lambda e, part=part, src=src:
                   e.scalar_tensor_tensor(rr, nn, -part, src, ALU.mult, ALU.add))
            src = rr
        t = op("dve", [t], lambda e: e.tensor_scalar(rr, rr, 3.1415925, -3.1415925, ALU.min, ALU.max))
        t = op("dve", [t], lambda e: e.scalar_tensor_tensor(ab, rr, -1.0, rr, ALU.mult, ALU.max))
        op("act", [t], lambda e: e.activation(sn, rr, ACT.Sin))
        t_rope = op("act", [t, t_c], lambda e: e.activation(cs, ab, ACT.Sin, scale=-1.0, bias=consts[:, 1:2]))

        def table(x, heads, half, lo):
            v = x.rearrange("p (t f) -> p t f", t=2)[:, :, lo:lo + half]
            return v.unsqueeze(2).to_broadcast([128, 2, heads, half])

        def rotate(v1, v2, heads, half, lo, tmp, after):
            c, s = table(cs, heads, half, lo), table(sn, heads, half, lo)
            n = 2 * heads * half
            a, b = (tmp[:, i * n:(i + 1) * n].rearrange("p (t h f) -> p t h f", t=2, h=heads) for i in range(2))
            t1 = op("dve", after + [t_rope], lambda e: e.tensor_tensor(a, v1, s, ALU.mult))
            t2 = op("dve", [], lambda e: e.tensor_tensor(b, v2, s, ALU.mult))
            t3 = op("dve", [t1, t2], lambda e: e.tensor_tensor(v1, v1, c, ALU.mult))
            t4 = op("dve", [t3], lambda e: e.tensor_tensor(v2, v2, c, ALU.mult))
            t5 = op("dve", [t4], lambda e: e.tensor_tensor(v1, v1, b, ALU.subtract))
            return op("dve", [t5], lambda e: e.tensor_tensor(v2, v2, a, ALU.add))

        va = FF[:, 0:1024].rearrange("p (t n) -> p t n", t=2)
        mqT = FF[:, 1024:2048].rearrange("p (k t) -> p k t", k=4)
        mkT = FF[:, 2048:3072].rearrange("p (k t) -> p k t", k=4)
        vb = FF[:, 3072:4096].rearrange("p (t n) -> p t n", t=2)
        gates = FF[:, 4096:8192].rearrange("p (t n) -> p t n", t=2)
        rtmp = FF[:, 11008:12032]
        cq = FF[:, 8384:9152].rearrange("p (t n) -> p t n", t=2)
        ckr = FF[:, 9152:9728].rearrange("p (t n) -> p t n", t=2)
        kcat = FF[:, 9728:11264].rearrange("p (t h n) -> p t h n", t=2, h=8)
        lqT = FF[0:96, 12800:14848].rearrange("p (h t) -> p h t", h=8)
        lkT = FF[0:96, 10752:12800].rearrange("p (h t) -> p h t", h=8)
        qk = xn

        def evac(dst, banks, width, t, after=(), eng="act"):
            out = []
            for tok in range(2):
                if eng == "act":
                    out.append(op("act", [t, *after], lambda e, tok=tok:
                                  e.activation(dst(tok), ps[:, banks[tok], 0:width], ACT.Copy)))
                else:
                    out.append(op("dve", [t, *after], lambda e, tok=tok:
                                  e.tensor_copy(dst(tok), ps[:, banks[tok], 0:width])))
                bank_t[banks[tok]] = [out[-1]]
            return out

        t = a_mm("w_in", 0, 512, 8, 4, act, (0, 1), t_h)
        t_q = evac(lambda tok: qk[:, tok, 0:512], (0, 1), 512, t, t_h)
        t = a_mm("w_in", 512, 512, 8, 4, act, (2, 3), t_h)
        t_k = evac(lambda tok: qk[:, tok, 512:1024], (2, 3), 512, t, t_h, "dve")
        qk4 = qk[:, :, :].rearrange("p t (h d) -> p t h d", d=64)
        t_rq = rotate(qk4[:, :, :, 0:8], qk4[:, :, :, 8:16], 16, 8, 0, rtmp, t_q + t_k)
        t = a_mm("w_in", 1024, 512, 8, 4, act, (0, 1), t_h)
        t_va = evac(lambda tok: va[:, tok, :], (0, 1), 512, t, [t_rope])
        t = a_mm("w_in", 1536, 384, 8, 4, act, (2, 3), t_h)
        t_cq = evac(lambda tok: cq[:, tok, :], (2, 3), 384, t)
        t = a_mm("w_in", 1920, 288, 8, 4, act, (0, 1), t_h)
        t_ck = evac(lambda tok: ckr[:, tok, :], (0, 1), 288, t)
        t_mq = transposes(lambda tok, k: qk[:, tok, 128 * k:128 * k + 128], 4, (4, 5), (mqT,), [[t_rq], [t_rq]], [])
        t_mk = transposes(lambda tok, k: qk[:, tok, 512 + 128 * k:640 + 128 * k], 4, (6, 7), (mkT,),
                          [[t_rq], [t_rq]], [])
        cqT = tuple(RR[:, i * 768:(i + 1) * 768].rearrange("p (k t) -> p k t", k=3) for i in range(2))
        ckT = tuple(RR[:, 1536 + i * 512:2048 + i * 512].rearrange("p (k t) -> p k t", k=2) for i in range(2))
        t_bc = bcast(R_QN, 640, t_xn[0] + t_xn[1])
        lat = []
        for src, width, g0, dst in ((cq, 384, 0, cqT), (ckr, 256, 384, ckT)):
            ready = []
            for tok in range(2):
                ss = stats(1)
                t = op("act", t_cq + t_ck, lambda e, tok=tok, ss=ss, src=src, width=width:
                       e.activation(gates[:, tok, 0:width], src[:, tok, 0:width], ACT.Square, accum_out=ss))
                rs, tp = power(ss, 1, 1.0 / width, [t])
                t = op("dve", [tp, t_bc], lambda e, tok=tok, rs=rs, src=src, width=width, g0=g0:
                       e.scalar_tensor_tensor(src[:, tok, 0:width], src[:, tok, 0:width], rs, bc[:, g0:g0 + width],
                                              ALU.mult, ALU.mult))
                ready.append([t])
            lat.append(transposes(lambda tok, k, src=src: src[:, tok, 128 * k:128 * k + 128], width // 128,
                                  (4, 5, 6, 7), dst, ready, []))
        t_bc = bcast(R_POST_MIX, 1024, ready[0] + ready[1])
        t_g = []
        for n in range(4):
            banks = (0, 1) if n % 2 else (2, 3)
            t = a_mm("w_in", 2208 + 512 * n, 512, 8, 4, act, banks, t_h)
            for tok in range(2):
                d = gates[:, tok, 512 * n:512 * n + 512]
                td = op("dve", [t, t_bg], lambda e, d=d, n=n, b=banks[tok]:
                        e.tensor_tensor(d, ps[:, b, :], bgate[:, 512 * n:512 * n + 512], ALU.add))
                bank_t[banks[tok]] = [td]
                t_g.append(op("act", [td], lambda e, d=d: e.activation(d, d, ACT.Sigmoid)))
        lq = xn[:, :, 0:768].rearrange("p t (h d) -> p t h d", d=96)
        t_lq = []
        for n in range(2):
            t = a_mm("w_uq", 384 * n, 384, 3, 3, cqT, (4, 5), lat[0])
            t_lq += evac(lambda tok, n=n: xn[:, tok, 384 * n:384 * n + 384], (4, 5), 384, t, t_mq + t_mk)
        t_kv, t_kn = [], []
        for n in range(2):
            t = a_mm("w_ukv", 512 * n, 512, 2, 2, ckT, (6, 7), lat[1])
            for tok in range(2):
                src = ps[:, 6 + tok, :].rearrange("p (h d) -> p h d", d=128)
                t1 = op("act", [t] + t_lq, lambda e, n=n, tok=tok, src=src:
                        e.activation(kcat[:, tok, 4 * n:4 * n + 4, 0:64], src[:, :, 0:64], ACT.Copy))
                t2 = op("act", [], lambda e, n=n, tok=tok, src=src:
                        e.activation(vb[:, tok, 256 * n:256 * n + 256].rearrange("p (h d) -> p h d", d=64),
                                     src[:, :, 64:128], ACT.Copy))
                bank_t[6 + tok] = [t2]
                t_kv += [t2]
                t_kn += [t1]
        t_rl = rotate(lq[:, :, :, 64:80], lq[:, :, :, 80:96], 8, 16, 8, FF[:, 11264:11776], t_lq)
        kr4 = ckr[:, :, 256:288].unsqueeze(2)
        t_rk = rotate(kr4[:, :, :, 0:16], kr4[:, :, :, 16:32], 1, 16, 8, FF[:, 11776:11904], t_ck)
        t_kc = []
        for tok in range(2):
            t_kc.append(op("dve", [t_rk] + t_kn, lambda e, tok=tok:
                           e.tensor_copy(kcat[:, tok, :, 64:96],
                                         ckr[:, tok, 256:288].unsqueeze(1).to_broadcast([128, 8, 32]))))
        t_q2 = transposes(lambda tok, h: lq[:, tok, h, :], 8, (4, 5), (lqT,), [[t_rl], [t_rl]], t_g, 96)
        kt_banks = (0, 1, 2, 3)
        tt = []
        for i, (tok, k0) in enumerate(((0, 0), (0, 4), (1, 0), (1, 4))):
            def go(eng, i=i, tok=tok, k0=k0):
                for j in range(4):
                    last = eng.transpose(ps[0:96, i, 128 * j:128 * j + 128], kcat[:, tok, k0 + j, :], ident[:, :])
                return last
            tt.append(op("pe", t_kc + t_kn + bank_t[i], go))
        t_k2 = []
        for i, (tok, k0) in enumerate(((0, 0), (0, 4), (1, 0), (1, 4))):
            t_k2.append(op("act", tt + t_q2, lambda e, i=i, tok=tok, k0=k0:
                           e.activation(lkT[:, k0:k0 + 4, 128 * tok:128 * tok + 128],
                                        ps[0:96, i, :].rearrange("p (k t) -> p k t", t=128), ACT.Copy)))
            bank_t[i] = [t_k2[-1]]

        oT = [tuple(RR[:, (2 * a + i) * 1024:(2 * a + i + 1) * 1024].rearrange("p (k t) -> p k t", k=4)
                    for i in range(2)) for a in range(2)]
        at = FF[:, 8384:10688]
        sm = [at[:, i * 384:(i + 1) * 384] for i in range(2)]
        pp = [at[:, 768 + i * 384:1152 + i * 384] for i in range(2)]
        pT = [at[:, 1536 + i * 384:1920 + i * 384] for i in range(2)]
        sm_t, pp_t, pT_t = [[], []], [[], []], [[], []]
        head = {}
        t_o = [[], []]

        def scores(i):
            b = 4 + i % 2
            h = i % 8
            if i < 8:
                r = slice(64 * (h % 2), 64 * (h % 2) + 64)
                q, k, scale, dep = mqT[r, h // 2, :], mkT[r, h // 2, :], 0.125, t_mq + t_mk
            else:
                q, k, scale, dep = lqT[:, h, :], lkT[:, h, :], 96 ** -0.5, t_q2 + t_k2

            def go(eng):
                eng.matmul(ps[:, b, 0:128], q[:, 0:128], k[:, 0:128], start=True, stop=True)
                return eng.matmul(ps[:, b, 128:384], q[:, 128:256], k[:, 0:256], start=True, stop=True)
            t = op("pe", dep + bank_t[b], go)
            j = i % 2
            ts = op("dve", [t] + sm_t[j] + t_k2 + t_kc, lambda e:
                    e.scalar_tensor_tensor(sm[j], ps[:, b, 0:384], scale, amask[:, :], ALU.mult, ALU.add))
            bank_t[b] = [ts]
            m = stats(6) if i < 2 else head[i - 2]["m"]
            head[i] = {"m": m}
            op("dve", [ts], lambda e: e.tensor_reduce(m[:, 0:1], sm[j][:, 0:128], AX, ALU.max, negate=True))
            tm = op("dve", [ts], lambda e: e.tensor_reduce(m[:, 1:2], sm[j][:, 128:384], AX, ALU.max, negate=True))
            op("act", [tm] + pp_t[j], lambda e:
               e.activation(pp[j][:, 0:128], sm[j][:, 0:128], ACT.Exp, bias=m[:, 0:1], accum_out=m[:, 2:3]))
            te = op("act", [], lambda e:
                    e.activation(pp[j][:, 128:384], sm[j][:, 128:384], ACT.Exp, bias=m[:, 1:2], accum_out=m[:, 3:4]))
            sm_t[j] = [te]
            tr = op("dve", [te], lambda e: e.reciprocal(m[:, 4:6], m[:, 2:4]))
            op("dve", [tr], lambda e: e.tensor_scalar(pp[j][:, 0:128], pp[j][:, 0:128], m[:, 4:5], None, ALU.mult))
            head[i]["p"] = op("dve", [tr], lambda e:
                              e.tensor_scalar(pp[j][:, 128:384], pp[j][:, 128:384], m[:, 5:6], None, ALU.mult))

        def flip(i):
            j, b = i % 2, 6 + i % 2

            def go(eng):
                for n in range(3):
                    last = eng.transpose(ps[:, b, 128 * n:128 * n + 128], pp[j][:, 128 * n:128 * n + 128], ident[:, :])
                return last
            t = op("pe", [head[i]["p"]] + bank_t[b], go)
            pp_t[j] = [t]
            te = op("act", [t] + pT_t[j], lambda e: e.activation(pT[j], ps[:, b, 0:384], ACT.Copy))
            bank_t[b] = [te]
            head[i]["pT"] = te

        def mix(i):
            j, h = i % 2, i % 8
            b = (i // 2) % 2
            v = (va if i < 8 else vb)[:, :, 64 * h:64 * h + 64]
            r = slice(64 * (h % 2), 64 * (h % 2) + 64)
            dep = t_va if i < 8 else t_kv

            def go(eng):
                eng.matmul(ps[r, b, 0:128], v[:, 0, :], pT[j][:, 0:128], start=True, stop=True)
                eng.matmul(ps[r, b, 128:256], v[:, 0, :], pT[j][:, 128:256], start=True, stop=False)
                return eng.matmul(ps[r, b, 128:256], v[:, 1, :], pT[j][:, 256:384], start=False, stop=True)
            t = op("pe", [head[i]["pT"]] + dep + (bank_t[b] if h % 2 == 0 else []), go)
            pT_t[j] = [t]
            if h % 2:
                hi, lo = (o[:, h // 2, :] for o in oT[i // 8])
                th = op("act", [t] + (lat_done if i < 8 else []), lambda e: e.activation(hi, ps[:, b, 0:256], ACT.Copy))
                tl = op("dve", [th], lambda e: e.tensor_tensor(lo, ps[:, b, 0:256], hi.bitcast(F32), ALU.subtract))
                bank_t[b] = [th, tl]
                t_o[i // 8] += [th, tl]

        lat_done = [("pe", count["pe"])]
        for i in range(18):
            if i < 16:
                scores(i)
            if 1 <= i < 17:
                flip(i - 1)
            if i >= 2:
                mix(i - 2)

        merged = xn
        t_m = [[], []]
        mtmp = FF[:, 0:1024].rearrange("p (t n) -> p t n", t=2)
        for n in range(2):
            t_a = a_mm("w_branch_a", 512 * n, 512, 4, 4, oT[0], (0, 1), t_o[0])
            t_b = a_mm("w_branch_b", 512 * n, 512, 4, 4, oT[1], (2, 3), t_o[1])
            for tok in range(2):
                d = merged[:, tok, 512 * n:512 * n + 512]
                g = gates[:, tok, :]
                t1 = op("dve", [t_a, t_g[-1]], lambda e, d=d, g=g, tok=tok, n=n:
                        e.tensor_tensor(d, ps[:, tok, :], g[:, 512 * n:512 * n + 512], ALU.mult))
                t2 = op("dve", [t_b, t1], lambda e, g=g, tok=tok, n=n:
                        e.tensor_tensor(mtmp[:, tok, :], ps[:, 2 + tok, :], g[:, 1024 + 512 * n:1536 + 512 * n],
                                        ALU.mult))
                bank_t[tok], bank_t[2 + tok] = [t1], [t2]
                t_m[tok] = [op("dve", [t1, t2], lambda e, d=d, tok=tok: e.tensor_tensor(d, d, mtmp[:, tok, :], ALU.add))]
        t_mt = transposes(lambda tok, k: merged[:, tok, 128 * k:128 * k + 128], 8, (4, 5, 6, 7), act, t_m,
                          [done_t[-1]])
        t = project("w_out", 8, act, t_mt)
        t_x = post_norm(t_bc, [t])

        def norm_x(row, t_x):
            t_b = bcast(row, 1024, t_x)
            return norm_parts(lambda tok: xr[:, tok, :], 1024, lambda tok: xn[:, tok, :], bc[:, :], t_b,
                              act, [[t_x[0], done_t[-1]], [t_x[1], done_t[-1]]])

        hid = [tuple(RR[:, (2 * j + i) * 512:(2 * j + i + 1) * 512].rearrange("p (f t) -> p f t", f=2)
                     for i in range(2)) for j in range(2)]
        htmp = [FF[:, j * 1024:j * 1024 + 1024].rearrange("p (a f t) -> p a f t", a=2, f=2) for j in range(2)]
        hid_t = [[], []]

        def down(name, j, n, ready):
            h, l, wt = take(("d", name, j))
            lhs = hid[j % 2]

            def go(eng):
                for f in range(2):
                    for tok in range(2):
                        for c in range(2):
                            s = slice(128 * tok, 128 * tok + 128)
                            w = slice(1024 * f + 512 * c, 1024 * f + 512 * c + 512)
                            last = mm3(eng, ps[:, 2 * tok + c, :], (lhs[0][:, f, s], lhs[1][:, f, s]),
                                       (h[:, w], l[:, w]), j == 0 and f == 0, j == n - 1 and f == 1)
                return last
            t = op("pe", wt + ready + (bank_t[0] + bank_t[2] if j == 0 else []), go)
            done_t.append(t)
            hid_t[j % 2] = [t]
            return t

        t_n, t_xs = norm_x(R_PRE_MLP, t_x)
        t_bc = bcast(R_POST_MLP, 1024, t_xs[0] + t_xs[1])
        ready = {}
        for j in range(17):
            if j < 16:
                b = 4 + j % 4
                tu = s_mm([("w_up", 2 * j), ("w_up", 2 * j + 1)], act,
                          [ps[:, b, 0:256], ps[:, b, 256:512]], t_n + bank_t[b])
                r, q = htmp[j % 2][:, 0], htmp[j % 2][:, 1]
                hi, lo = hid[j % 2]
                pv = ps[:, b, :].rearrange("p (f t) -> p f t", f=2)
                dep = ready[j - 2] if j >= 2 else []
                t1 = op("act", [tu] + dep, lambda e, r=r, pv=pv: e.activation(r, pv, ACT.Relu))
                bank_t[b] = [t1]
                t2 = op("act", [t1] + hid_t[j % 2] + t_mt, lambda e, r=r, hi=hi: e.activation(hi, r, ACT.Square))
                t3 = op("dve", [t1], lambda e, r=r, q=q: e.tensor_tensor(q, r, r, ALU.mult))
                t4 = op("dve", [t2, t3] + hid_t[j % 2], lambda e, q=q, hi=hi, lo=lo:
                        e.tensor_tensor(lo, q, hi.bitcast(F32), ALU.subtract))
                ready[j] = [t2, t4]
            if j:
                t = down("w_down", j - 1, 16, ready[j - 1])
        t_x = post_norm(t_bc, [t])

        t_n, t_xs = norm_x(R_MIX0, t_x)
        t_bc = bcast(R_HNORM, 1024, t_xs[0] + t_xs[1])
        lbt = stats(40)
        mx, e0, e1, lb, om = (lbt[:, 8 * i:8 * i + 8] for i in range(5))
        l0, l1 = cols[:, C_LB0:C_LB0 + 8], cols[:, C_LB1:C_LB1 + 8]
        t1 = op("dve", [t_in], lambda e: e.tensor_tensor(mx, l0, l1, ALU.max))
        t2 = op("dve", [t1], lambda e: e.tensor_tensor(e0, l0, mx, ALU.subtract))
        t3 = op("dve", [t1], lambda e: e.tensor_tensor(e1, l1, mx, ALU.subtract))
        e01 = lbt[:, 8:24]
        t4 = op("act", [t2, t3], lambda e: e.activation(e01, e01, ACT.Exp))
        t5 = op("dve", [t4], lambda e: e.tensor_tensor(mx, e0, e1, ALU.add))
        t6 = op("dve", [t5], lambda e: e.reciprocal(mx, mx))
        t7 = op("dve", [t6], lambda e: e.tensor_tensor(lb, e0, mx, ALU.mult))
        t_lb = op("dve", [t7], lambda e: e.tensor_tensor(om, e1, mx, ALU.mult))

        Q = FF[:, 0:2048].rearrange("p (h t) -> p h t", h=8)
        K = FF[:, 2048:4096].rearrange("p (h t) -> p h t", h=8)
        E0 = FF[:, 4096:6144]
        E1 = FF[:, 6144:7168]
        V = FF[:, 7168:9216].rearrange("p (t n) -> p t n", t=2)
        G = FF[:, 9216:11264].rearrange("p (t n) -> p t n", t=2)
        AC = FF[:, 11264:13312].rearrange("p (h t) -> p h t", h=8)
        XC = FF[:, 13312:14336].rearrange("p (h t) -> p h t", h=8)
        sg = [FF[:, 14336 + 256 * i:14592 + 256 * i] for i in range(2)]
        E = E0.rearrange("p (h t) -> p h t", h=8)
        t_z = op("pool", t_x, lambda e: e.memset(AC, 0.0))
        sg_t = [[], []]
        t_hd = []
        for h in range(8):
            b = 4 + h % 4
            tu = s_mm([("hgrn_w_in", h), ("hgrn_w_in", 8 + h)], act,
                      [ps[:, b, 0:256], ps[:, b, 256:512]], t_n + bank_t[b])
            qv, fv = ps[:, b, 0:256], ps[:, b, 256:512]
            s = sg[h % 2]
            c = slice(h, h + 1)
            t1 = op("act", [tu] + sg_t[h % 2], lambda e, s=s, qv=qv: e.activation(s, qv, ACT.Sigmoid))
            t2 = op("act", [], lambda e, h=h, fv=fv: e.activation(E[:, h, :], fv, ACT.Sigmoid))
            t3 = op("act", [], lambda e, h=h, fv=fv: e.activation(K[:, h, :], fv, ACT.Sigmoid, scale=-1.0))
            t4 = op("dve", [t3], lambda e, h=h, s=s, qv=qv: e.tensor_tensor(Q[:, h, :], qv, s, ALU.mult))
            bank_t[b] = [t3, t4]
            sg_t[h % 2] = [t4]
            t5 = op("dve", [t2, t_lb], lambda e, h=h, c=c:
                    e.tensor_scalar(E[:, h, :], E[:, h, :], om[:, c], lb[:, c], ALU.mult, ALU.add))
            t6 = op("dve", [t3, t_lb], lambda e, h=h, c=c:
                    e.tensor_scalar(K[:, h, :], K[:, h, :], om[:, c], None, ALU.mult))
            t_hd.append([t4, t5, t6])
        t_v, t_gg = [], []
        for n in range(4):
            banks = (0, 1) if n % 2 else (2, 3)
            t = a_mm("hgrn_w_in", 2048 + 512 * n, 512, 8, 4, act, banks, t_n)
            if n < 2:
                t_v += evac(lambda tok, n=n: V[:, tok, 512 * n:512 * n + 512], banks, 512, t, t_x)
                continue
            for tok in range(2):
                d = G[:, tok, 512 * n - 1024:512 * n - 512]
                b = banks[tok]
                t1 = op("act", [t], lambda e, d=d, b=b: e.activation(d, ps[:, b, :], ACT.Sigmoid))
                t2 = op("dve", [t1], lambda e, d=d, b=b: e.tensor_tensor(d, ps[:, b, :], d, ALU.mult))
                bank_t[b] = [t2]
                t_gg.append(op("dve", [t2, t_bc], lambda e, d=d, n=n:
                               e.tensor_tensor(d, d, bc[:, 512 * n - 1024:512 * n - 512], ALU.mult)))

        rd_t = [[], []]
        up_t = [t_hd[0] + t_hd[1] + t_hd[2] + t_hd[3], t_hd[4] + t_hd[5] + t_hd[6] + t_hd[7]]
        ac_t = [[t_z], [t_z]]

        def level(g, lev):
            b0 = 4 if g else 0

            def go(eng):
                for h in range(4):
                    for blk in range(2):
                        s = slice(128 * blk, 128 * blk + 128)
                        c = 256 * (h % 2) + 128 * blk
                        last = eng.matmul(ps[:, b0 + h // 2, c:c + 128], K[:, 4 * g + h, s], Q[:, 4 * g + h, s],
                                          start=True, stop=True)
                return last
            t = op("pe", up_t[g] + bank_t[b0] + bank_t[b0 + 1], go)
            rd_t[g] = [t]
            d = AC[:, 4 * g:4 * g + 4, :].rearrange("p h (b t) -> p (h b) t", t=128)
            m = hmask[:, lev, :].unsqueeze(1).to_broadcast([128, 8, 128])
            src = ps[:, b0:b0 + 2, :].rearrange("p b (c t) -> p (b c) t", t=128)
            tc = op("dve", [t] + ac_t[g], lambda e: e.copy_predicated(d, m, src))
            bank_t[b0] = bank_t[b0 + 1] = [tc]
            ac_t[g] = [tc]

        for g in range(2):
            level(g, 0)
        ev = [E0[:, 1024 * g:1024 * g + 1024] for g in range(2)]
        od = [E1[:, 512 * g:512 * g + 512] for g in range(2)]
        for g in range(2):
            qg = Q[:, 4 * g:4 * g + 4, :]
            eg = E[:, 4 * g:4 * g + 4, :]
            t = op("dve", rd_t[g] + up_t[g], lambda e, qg=qg, eg=eg: e.tensor_tensor(qg, qg, eg, ALU.mult))
            up_t[g] = up_t[g] + [t]
            level(g, 1)
        hs, lev = 1, 2
        cur = [ev, od]
        e_t = [[], []]
        while hs < 128:
            for g in range(2):
                n = 1024 // (2 * hs)
                e2 = cur[0][g][:, 0:2 * n].rearrange("p (n w) -> p n w", w=2)
                q2 = FF[:, 1024 * g:1024 * g + 1024].rearrange("p (n w s) -> p n w s", w=2, s=hs)[:, :, 1, :]
                k2 = FF[:, 2048 + 1024 * g:3072 + 1024 * g].rearrange("p (n w s) -> p n w s", w=2, s=hs)[:, :, 0, :]
                f0 = e2[:, :, 0:1].to_broadcast([128, n, hs])
                f1 = e2[:, :, 1:2].to_broadcast([128, n, hs])
                nx = cur[1][g][:, 0:n]
                t1 = op("dve", rd_t[g] + up_t[g] + e_t[g], lambda e, q2=q2, f0=f0: e.tensor_tensor(q2, q2, f0, ALU.mult))
                t2 = op("pool", rd_t[g] + up_t[g] + e_t[g], lambda e, k2=k2, f1=f1:
                        e.tensor_tensor(k2, k2, f1, ALU.mult))
                if hs < 64:
                    t3 = op("pool", up_t[g] + e_t[g], lambda e, nx=nx, e2=e2:
                            e.tensor_tensor(nx, e2[:, :, 0], e2[:, :, 1], ALU.mult))
                    e_t[g] = [t3]
                up_t[g] = [t1, t2]
                if hs < 64:
                    level(g, lev)
            hs *= 2
            lev += 1
            cur.reverse()
        t_xc = []
        for g in range(2):
            b0 = 4 if g else 0

            def go(eng, g=g, b0=b0):
                for h in range(4):
                    last = eng.matmul(ps[:, b0, 128 * h:128 * h + 128], K[:, 4 * g + h, 0:128], Q[:, 4 * g + h, 128:256],
                                      start=True, stop=True)
                return last
            t = op("pe", up_t[g] + bank_t[b0], go)
            d = XC[:, 4 * g:4 * g + 4, :].rearrange("p h t -> p (h t)")
            te = op("act", [t], lambda e, d=d, b0=b0: e.activation(d, ps[:, b0, :], ACT.Copy))
            bank_t[b0] = [te]
            t_xc.append(te)
        t_oh = []
        for tok in range(2):
            for g in range(2):
                def go(eng, tok=tok, g=g):
                    for h in range(4 * g, 4 * g + 4):
                        o = ps[:, 2 * tok + g, 128 * (h % 4):128 * (h % 4) + 128]
                        c = slice(128 * h, 128 * h + 128)
                        if tok:
                            eng.matmul(o, XC[:, h, :], V[:, 0, c], start=True, stop=False)
                        last = eng.matmul(o, AC[:, h, 128 * tok:128 * tok + 128], V[:, tok, c],
                                          start=not tok, stop=True)
                    return last
                t_oh.append(op("pe", t_xc + ac_t[g] + t_v + bank_t[2 * tok + g], go))
        t_m = [[], []]
        for tok in range(2):
            y = ps[:, 2 * tok:2 * tok + 2, :]
            d = xn[:, tok, :].rearrange("p (b n) -> p b n", b=2)
            t1 = op("act", [t_oh[2 * tok + 1]], lambda e, y=y, d=d: e.activation(d, y, ACT.Square))
            ss = stats(8)
            t2 = op("dve", [t1], lambda e, tok=tok, ss=ss:
                    e.tensor_reduce(ss, xn[:, tok, :].rearrange("p (h n) -> p h n", h=8), AX, ALU.add))
            rs, tp = power(ss, 8, 1.0 / 128, [t2])
            t3 = op("dve", t_gg + [t2], lambda e, y=y, d=d, tok=tok:
                    e.tensor_tensor(d, y, G[:, tok, :].rearrange("p (b n) -> p b n", b=2), ALU.mult))
            bank_t[2 * tok] = bank_t[2 * tok + 1] = [t3]
            v = xn[:, tok, :].rearrange("p (h n) -> p h n", h=8)
            t_m[tok] = [op("dve", [t3, tp], lambda e, v=v, rs=rs:
                           e.tensor_tensor(v, v, rs.unsqueeze(2).to_broadcast([128, 8, 128]), ALU.mult))]
        t_mt = transposes(lambda tok, k: xn[:, tok, 128 * k:128 * k + 128], 8, (4, 5, 6, 7), act, t_m, [done_t[-1]])
        t = project("hgrn_w_out", 8, act, t_mt)
        t_x = add_mix([t])

        def swiglu(layer, row, t_x):
            t_n, _ = norm_x(row, t_x)
            ready = {}
            for j in range(12):
                if j < 11:
                    b = 4 + 2 * (j % 2)
                    for i in range(2):
                        f = 2 * j + i
                        tu = s_mm([(f"ffn_in{layer}", f), (f"ffn_in{layer}", 22 + f)], act,
                                  [ps[:, b + i, 0:256], ps[:, b + i, 256:512]], t_n + bank_t[b + i])
                    gv, uv = ps[:, b:b + 2, 0:256], ps[:, b:b + 2, 256:512]
                    s, q = htmp[j % 2][:, 0], htmp[j % 2][:, 1]
                    hi, lo = hid[j % 2]
                    t1 = op("act", [tu] + (ready[j - 2] if j >= 2 else []), lambda e, s=s, gv=gv:
                            e.activation(s, gv, ACT.Sigmoid))
                    t2 = op("dve", [t1], lambda e, s=s, gv=gv: e.tensor_tensor(s, gv, s, ALU.mult))
                    t3 = op("dve", [t2], lambda e, s=s, q=q, uv=uv: e.tensor_tensor(q, uv, s, ALU.mult))
                    bank_t[b] = bank_t[b + 1] = [t3]
                    t4 = op("act", [t3] + hid_t[j % 2], lambda e, q=q, hi=hi: e.activation(hi, q, ACT.Copy))
                    t5 = op("dve", [t4], lambda e, q=q, hi=hi, lo=lo:
                            e.tensor_tensor(lo, q, hi.bitcast(F32), ALU.subtract))
                    ready[j] = [t4, t5]
                if j:
                    t = down(f"ffn_out{layer}", j - 1, 11, ready[j - 1])
            return add_mix([t])

        t_x = swiglu(0, R_FFN0, t_x)

        t_n, t_xs = norm_x(R_MIX1, t_x)
        ct = stats(40)
        nl, z, w1, lw, c4 = (ct[:, 8 * i:8 * i + 8] for i in range(5))
        lam = cols[:, C_LAM:C_LAM + 8]
        t = op("dve", [t_in], lambda e: e.scalar_tensor_tensor(nl, lam, -1.0, lam, ALU.mult, ALU.min))
        t = op("act", [t], lambda e: e.activation(z, nl, ACT.Exp))
        t = op("dve", [t], lambda e: e.tensor_scalar(w1, z, 1.0, None, ALU.add))
        t = op("act", [t], lambda e: e.activation(lw, w1, ACT.Ln))
        t = op("dve", [t], lambda e: e.tensor_scalar(w1, w1, 1.0, 1e-30, ALU.subtract, ALU.max))
        t = op("dve", [t], lambda e: e.tensor_scalar(nl, lam, -1.0, 0.0, ALU.mult, ALU.max))
        t = op("dve", [t], lambda e: e.reciprocal(c4, w1))
        t = op("dve", [t], lambda e: e.tensor_tensor(c4, c4, z, ALU.mult))
        t = op("dve", [t], lambda e: e.tensor_tensor(c4, c4, lw, ALU.mult))
        t = op("dve", [t], lambda e: e.tensor_scalar(w1, w1, 1e-30, None, ALU.is_le))
        t = op("dve", [t], lambda e: e.tensor_tensor(w1, w1, z, ALU.mult))
        t = op("dve", [t], lambda e: e.tensor_tensor(c4, c4, w1, ALU.add))
        t = op("dve", [t], lambda e: e.tensor_tensor(c4, c4, nl, ALU.add))
        t_c4 = op("dve", [t], lambda e: e.tensor_scalar(c4, c4, 4.0, None, ALU.mult))

        Y = FF[:, 0:2048].rearrange("p (h t) -> p h t", h=8)
        U = FF[:, 2048:4120].rearrange("p (h t) -> p h t", h=8)
        UC = FF[:, 4128:6176].rearrange("p (h t) -> p h t", h=8)
        RG = FF[:, 6176:8224].rearrange("p (h t) -> p h t", h=8)
        IG = FF[:, 8224:10272].rearrange("p (h t) -> p h t", h=8)
        WW = FF[:, 10272:12320].rearrange("p (h t) -> p h t", h=8)
        uH = RR[:, 0:2048].rearrange("p (h t) -> p h t", h=8)
        uL = RR[:, 2048:4096].rearrange("p (h t) -> p h t", h=8)
        t_p = op("pool", t_x, lambda e: e.memset(U[:, :, 0:3], 0.0))
        t_u, t_y = [], []
        for f in range(8):
            b = 4 + f % 4
            tu = s_mm([("lru_w_in", f), ("lru_w_in", 8 + f)], act,
                      [ps[:, b, 0:256], ps[:, b, 256:512]], t_n + bank_t[b])
            t1 = op("act", [tu], lambda e, f=f, b=b: e.activation(Y[:, f, :], ps[:, b, 0:256], ACT.Gelu_apprx_tanh))
            t2 = op("act", [], lambda e, f=f, b=b: e.activation(U[:, f, 3:259], ps[:, b, 256:512], ACT.Copy))
            bank_t[b] = [t2]
            t_y.append(t1)
            t3 = op("dve", [t2, t_p, t_in], lambda e, f=f:
                    e.tensor_scalar(UC[:, f, :], U[:, f, 0:256], cols[:, C_CONVW + f:C_CONVW + f + 1],
                                    cols[:, C_CONVB + f:C_CONVB + f + 1], ALU.mult, ALU.add))
            for tap in range(1, 4):
                c = C_CONVW + 8 * tap + f
                t3 = op("dve", [t3], lambda e, f=f, tap=tap, c=c:
                        e.scalar_tensor_tensor(UC[:, f, :], U[:, f, tap:tap + 256], cols[:, c:c + 1], UC[:, f, :],
                                               ALU.mult, ALU.add))
            th = op("act", [t3], lambda e, f=f: e.activation(uH[:, f, :], UC[:, f, :], ACT.Copy))
            tl = op("dve", [th], lambda e, f=f:
                    e.tensor_tensor(uL[:, f, :], UC[:, f, :], uH[:, f, :].bitcast(F32), ALU.subtract))
            t_u.append([th, tl])
        t_ri = []
        for n in range(4):
            if n % 2 == 0:
                h, l, wt = take(("g", n))
            b = (0, 2, 4, 6)[n]

            def go(eng, n=n, b=b, h=h, l=l):
                for m in range(2):
                    for fo in range(2):
                        for k in range(2):
                            w0 = (((n % 2) * 2 + m) * 2 + k) * 256 + 128 * fo
                            w = slice(w0, w0 + 128)
                            last = mm3(eng, ps[:, b + m, 256 * fo:256 * fo + 256], (h[:, w], l[:, w]),
                                       (uH[:, 2 * n + k, :], uL[:, 2 * n + k, :]), k == 0, k == 1)
                return last
            t = op("pe", wt + t_u[2 * n] + t_u[2 * n + 1] + bank_t[b] + bank_t[b + 1], go)
            if n % 2:
                done_t.append(t)
            for m, (dst, col) in enumerate(((RG, C_BA), (IG, C_BX))):
                for fo in range(2):
                    f = 2 * n + fo
                    te = op("act", [t], lambda e, dst=dst, col=col, f=f, fo=fo, bb=b + m:
                            e.activation(dst[:, f, :], ps[:, bb, 256 * fo:256 * fo + 256], ACT.Sigmoid,
                                         bias=cols[:, col + f:col + f + 1]))
                bank_t[b + m] = [te]
            t_ri.append(te)
        for f in range(8):
            tv = op("act", [t_ri[f // 2], t_c4], lambda e, f=f:
                    e.activation(RG[:, f, :], RG[:, f, :], ACT.Tanh, scale=c4[:, f:f + 1]))
        hsT = [[], []]
        for g in range(2):
            r = slice(4 * g, 4 * g + 4)
            v = RG[:, r, :]
            t1 = op("dve", [tv], lambda e, r=r, v=v: e.tensor_scalar(WW[:, r, :], v, 1.0, None, ALU.add))
            t1 = op("dve", [t1], lambda e, r=r: e.reciprocal(WW[:, r, :], WW[:, r, :]))
            ts = op("act", t_u[7] + [tv], lambda e, r=r, v=v: e.activation(U[:, r, 0:256], v, ACT.Sqrt))
            t2 = op("pool", [t_ri[-1]], lambda e, r=r: e.tensor_tensor(IG[:, r, :], IG[:, r, :], UC[:, r, :], ALU.mult))
            t3 = op("dve", [ts], lambda e, r=r, v=v: e.tensor_scalar(v, v, -1.0, 1.0, ALU.mult, ALU.add))
            t3 = op("dve", [t3, t1], lambda e, r=r, v=v: e.tensor_tensor(v, v, WW[:, r, :], ALU.mult))
            t4 = op("dve", [ts, t1], lambda e, r=r:
                    e.tensor_tensor(WW[:, r, :], WW[:, r, :], U[:, r, 0:256], ALU.mult))
            t5 = op("dve", [t4, t2], lambda e, r=r: e.scalar_tensor_tensor(
                WW[:, r, :].rearrange("p h t -> p (h t)"), WW[:, r, :].rearrange("p h t -> p (h t)"), 2.0,
                IG[:, r, :].rearrange("p h t -> p (h t)"), ALU.mult, ALU.mult))
            for f in range(4 * g, 4 * g + 4):
                t6 = op("dve", [t5, t3], lambda e, f=f:
                        e.tensor_tensor_scan(WW[:, f, :], RG[:, f, :], WW[:, f, :], 0.0, ALU.mult, ALU.add))
            t7 = op("dve", [t6] + t_y, lambda e, r=r: e.tensor_tensor(WW[:, r, :], WW[:, r, :], Y[:, r, :], ALU.mult))
            t8 = op("act", [t7, done_t[-1]], lambda e, r=r: e.activation(aH[:, r, :], WW[:, r, :], ACT.Copy))
            t9 = op("dve", [t8], lambda e, r=r:
                    e.tensor_tensor(aL[:, r, :], WW[:, r, :], aH[:, r, :].bitcast(F32), ALU.subtract))
            hsT += [t8, t9]
            t_hs = [t8, t9]
        t = project("lru_w_out", 8, act, t_hs)
        t_x = add_mix([t])
        t_x = swiglu(1, R_FFN1, t_x)

        t_b = bcast(R_FINAL, 1024, t_x)
        for tok in range(2):
            ss = stats(1)
            t = op("act", [t_x[tok]], lambda e, tok=tok, ss=ss:
                   e.activation(xn[:, tok, :], xr[:, tok, :], ACT.Square, accum_out=ss))
            rs, tp = power(ss, 1, 1.0 / 1024, [t])
            t = op("dve", [tp, t_b, t], lambda e, tok=tok, rs=rs:
                   e.scalar_tensor_tensor(xn[:, tok, :], xr[:, tok, :], rs, bc[:, :], ALU.mult, ALU.mult))
            t_out = dma("out", [t], out_d[128 * tok:128 * tok + 128, :], xn[:, tok, :])
        wait("sp", [t_out])
        assert len(done_t) == len(chunks)

        block = ctx.enter_context(nc.Block())

        @block.sync
        def _(eng):
            for f in queue["sp"]:
                f(eng)

        @block.gpsimd
        def _(eng):
            for f in queue["pool"]:
                f(eng)

        @block.scalar
        def _(eng):
            for f in queue["act"]:
                f(eng)

        @block.vector
        def _(eng):
            for f in queue["dve"]:
                f(eng)

        @block.tensor
        def _(eng):
            for f in queue["pe"]:
                f(eng)


def kernel(**inputs):
    import concourse.bacc as bacc
    from concourse.bass_utils import run_bass_kernel_spmd

    a = {k: np.asarray(v) for k, v in inputs.items()}
    w = {
        "w_in": a["w_in"][0], "w_uq": a["w_uq"][0], "w_ukv": a["w_ukv"][0],
        "w_branch_a": a["w_branch_a"][0], "w_branch_b": a["w_branch_b"][0], "w_out": a["w_out"][0],
        "w_up": a["w_up"][0], "w_down": a["w_down"][0],
        "hgrn_w_in": a["hgrn_w_in_2"][0], "hgrn_w_out": a["hgrn_w_out_2"][0],
        "lru_w_in": a["lru_w_in_2"][0], "lru_w_out": a["lru_w_out_2"][0],
        "lru_wa": a["lru_wa_2"][0], "lru_wx": a["lru_wx_2"][0],
        "ffn_in0": a["ffn_w_in_2"][0], "ffn_in1": a["ffn_w_in_2"][1],
        "ffn_out0": a["ffn_w_out_2"][0], "ffn_out1": a["ffn_w_out_2"][1],
    }
    stream = np.concatenate([np.ascontiguousarray(lay_chunk(w, key)).reshape(-1) for key, _ in chunk_list()])

    def col(v):
        return v.reshape(-1, 128).T

    cols = np.ascontiguousarray(np.concatenate(
        [col(a["hgrn_lb_2"][0]), col(a["hgrn_lb_2"][1]), col(a["lru_conv_b_2"][0]), col(a["lru_ba_2"][0]),
         col(a["lru_bx_2"][0]), col(a["lru_lambda_2"][0])] + [col(a["lru_conv_w_2"][0][t]) for t in range(4)], axis=1))
    rows = np.concatenate([
        a["g_pre_mix"][0], a["g_post_mix"][0], a["g_pre_mlp"][0], a["g_post_mlp"][0],
        a["norm_mix_2"][0], a["norm_mix_2"][1], a["norm_ffn_2"][0], a["norm_ffn_2"][1], a["norm_final_2"],
        a["b_gate"][0], np.tile(a["hgrn_norm_2"][0], 8), a["g_q_norm"][0], a["g_kv_norm"][0]])

    def inv_freq(r):
        return np.power(np.float32(500000.0), -np.arange(r // 2, dtype=np.float32) * np.float32(2.0 / r))

    const = np.zeros((128, 1560), np.float32)
    const[:, 0:128] = np.eye(128)
    tri = np.where(np.arange(128)[None, :] <= np.arange(128)[:, None], 0.0, -1e38)
    const[:, 128:256] = tri
    const[:, 384:512] = tri
    const[:, 512:520] = inv_freq(16)
    const[:, 520:536] = inv_freq(32)
    s, t = np.arange(128)[:, None], np.arange(128)[None, :]
    mask = np.zeros((128, 8, 128), np.float32)
    mask[:, 0] = s == t
    for n in range(7):
        h = 1 << n
        mask[:, n + 1] = ((t // h) % 2 == 1) & (s // h == t // h - 1)

    const[:, 536:] = mask.reshape(128, 1024)

    arrays = {
        "x_in": np.ascontiguousarray(a["x"][0]),
        "pos_in": np.ascontiguousarray(a["positions"].reshape(2, 128).T.astype(np.int32)),
        "w_stream": stream, "cols_in": cols, "rows_in": rows, "const_in": const,
    }
    nc = bacc.Bacc("TRN2", target_bir_lowering=False, num_devices=1)
    args = [nc.dram_tensor(k, v.shape, mybir.dt.from_np(v.dtype), kind="ExternalInput").ap()
            for k, v in arrays.items()]
    args.append(nc.dram_tensor("out_0", (256, 1024), F32, kind="ExternalOutput").ap())
    program(nc, *args)
    r = run_bass_kernel_spmd(nc, [arrays], core_ids=[0])
    return r.results[0]["out_0"].reshape(1, 256, 1024)
```

```python
import numpy as np
import concourse.bass as bass
from concourse import mybir
from contextlib import ExitStack

F32 = mybir.dt.float32
F32R = mybir.dt.float32r
I32 = mybir.dt.int32
U8 = mybir.dt.uint8
ALU = mybir.AluOpType
ACT = mybir.ActivationFunctionType
AX = mybir.AxisListType.X

EPS = 1e-6
TWO_PI = 2.0 * np.pi
PI_1 = 6.28125
PI_2 = 0.00193500518798828125
PI_3 = float(TWO_PI - PI_1 - PI_2)
MAGIC = 12582912.0

C_LB0, C_LB1, C_CONVB, C_BA, C_BX, C_LAM, C_CONVW, C_N = 0, 8, 16, 24, 32, 40, 48, 80
R_PRE_MIX, R_POST_MIX, R_PRE_MLP, R_POST_MLP = 0, 1024, 2048, 3072
R_MIX0, R_MIX1, R_FFN0, R_FFN1, R_FINAL = 4096, 5120, 6144, 7168, 8192
R_BGATE, R_HNORM, R_QN, R_KVN, R_N = 9216, 11264, 12288, 12672, 12928


def chunk_list():
    out = []

    def a_type(name, col, width, kt, group):
        for k in range(0, kt, group):
            out.append((("a", name, col, width, k, min(group, kt - k)), width * min(group, kt - k)))

    def s_type(pairs, kt):
        out.append((("s", tuple(pairs), kt), 128 * kt * len(pairs)))

    def rows(name, n):
        for j in range(n):
            out.append((("d", name, j), 2048))

    for col, width in ((1536, 384), (1920, 288), (0, 512), (512, 512)):
        a_type("w_in", col, width, 8, 4)
    s_type([("w_ukv", h) for h in range(8)], 2)
    a_type("w_ukv_v", 0, 512, 2, 2)
    a_type("w_uq", 0, 384, 3, 3)
    a_type("w_uq", 384, 384, 3, 3)
    a_type("w_in", 1024, 512, 8, 4)
    for n in range(4):
        a_type("w_in", 2208 + 512 * n, 512, 8, 4)
    for n in range(2):
        a_type("w_branch_a", 512 * n, 512, 4, 4)
        a_type("w_branch_b", 512 * n, 512, 4, 4)
    rows("w_out", 4)

    def mlp(up, down, units, first, whole):
        a_type(first, 0, 512, 8, 4)
        lead = 2 if whole == 2 else 0
        for j in range(units + 1):
            if whole <= j + lead < units:
                for u in up(j + lead):
                    s_type(u, 8)
            if 0 < j < units:
                out.append((("d", down, j - 1), 2048))
        out.append((("d", down, units - 1), 2048))

    mlp(lambda j: [[("w_up", 2 * j), ("w_up", 2 * j + 1)]], "w_down", 16, "w_up", 2)
    a_type("hgrn_w_in", 2048, 512, 8, 4)
    for h in range(8):
        s_type([("hgrn_w_in", h), ("hgrn_w_in", 8 + h)], 8)
    for n in range(1, 4):
        a_type("hgrn_w_in", 2048 + 512 * n, 512, 8, 4)
    rows("hgrn_w_out", 4)
    mlp(lambda j: [[("ffn_in0", f), ("ffn_in0", 22 + f)] for f in (2 * j, 2 * j + 1)], "ffn_out0", 11, "ffn_first0", 1)
    a_type("lru_first", 0, 512, 8, 4)
    for step in range(7):
        n = step
        if 0 < n < 4:
            for f in (2 * n, 2 * n + 1):
                s_type([("lru_w_in", f), ("lru_w_in", 8 + f)], 8)
        if 0 <= n - 1 < 4:
            out.append((("g", n - 1), 1024))
        if 0 <= n - 3 < 4:
            out.append((("d", "lru_w_out", n - 3), 2048))
    mlp(lambda j: [[("ffn_in1", f), ("ffn_in1", 22 + f)] for f in (2 * j, 2 * j + 1)], "ffn_out1", 11, "ffn_first1", 1)
    return out


def lay_chunk(w, key):
    if key[0] == "a":
        _, name, col, width, k, n = key
        return w[name][128 * k:128 * (k + n), col:col + width].reshape(n, 128, width).transpose(1, 0, 2)
    if key[0] == "s":
        _, pairs, kt = key
        return np.concatenate([w[name][:, 128 * f:128 * f + 128].reshape(kt, 128, 128).transpose(1, 0, 2)
                               for name, f in pairs], axis=1)
    if key[0] == "d":
        _, name, j = key
        return w[name][256 * j:256 * j + 256].reshape(2, 128, 1024).transpose(1, 0, 2)
    return np.concatenate([w[name][key[1]].reshape(2, 128, 256).transpose(1, 0, 2)
                           for name in ("lru_wa", "lru_wx")], axis=1)


def program(nc, x_d, pos_d, w_d, cols_d, rows_d, const_d, out_d):
    NRAW, NHL = 3, 4
    ENG = ("pe", "act", "dve", "pool", "sp")
    chunks = chunk_list()
    offs = np.concatenate([[0], np.cumsum([128 * wd for _, wd in chunks])]).tolist()

    ctx = ExitStack()
    with ctx:
        def sb(name, shape, dt=F32):
            return ctx.enter_context(nc.sbuf_tensor(name, shape, dt))

        raw = sb("raw", [128, NRAW, 2048])
        wH = sb("wH", [128, NHL, 2048], F32R)
        wL = sb("wL", [128, NHL, 2048], F32R)
        xr = sb("xr", [128, 2, 1024])
        xn = sb("xn", [128, 2, 1024])
        aH = sb("aH", [128, 8, 256], F32R)
        aL = sb("aL", [128, 8, 256], F32R)
        RR = sb("RR", [128, 4608], F32R)
        bc = sb("bc", [128, 1024])
        ident = sb("ident", [128, 128])
        amask = sb("amask", [128, 384])
        hmask = sb("hmask", [128, 8, 128], U8)
        cols = sb("cols", [128, C_N])
        st = sb("st", [128, 256])
        consts = sb("consts", [128, 32])
        FF = sb("FF", [128, 14848])
        ps = ctx.enter_context(nc.psum_tensor("ps", [128, 8, 512], F32))

        sems = {e: ctx.enter_context(nc.semaphore(f"s_{e}")) for e in ENG}
        for n in range(NRAW):
            sems[f"raw{n}"] = ctx.enter_context(nc.semaphore(f"s_raw{n}"))
        for n in ("x0", "x1", "id", "in", "bc", "bg", "out"):
            sems[n] = ctx.enter_context(nc.semaphore(f"s_{n}"))
        queue = {e: [] for e in ENG}
        count = {s: 0 for s in sems}
        seen = {e: {} for e in ENG}

        def wait(e, after):
            for t in after:
                if t is None:
                    continue
                s, v = t
                if seen[e].get(s, 0) < v:
                    seen[e][s] = v
                    queue[e].append(lambda eng, s=s, v=v: eng.wait_ge(sems[s], v))

        def op(e, after, fn):
            wait(e, after)
            queue[e].append(lambda eng: fn(eng).then_inc(sems[e], 1))
            count[e] += 1
            return (e, count[e])

        def dma(sem, after, dst, src, e="sp"):
            wait(e, after)
            queue[e].append(lambda eng: eng.dma_start(dst, src).then_inc(sems[sem], 16))
            count[sem] += 16
            return (sem, count[sem])

        dma_t, split_t, done_t = [], [], []

        def load_chunk(i):
            wd = chunks[i][1]
            free = split_t[i - NRAW] if i >= NRAW else []
            src = w_d[offs[i]:offs[i + 1]].rearrange("(p n) -> p n", p=128)
            dma_t.append(dma(f"raw{i % NRAW}", free, raw[:, i % NRAW, 0:wd], src))

        def split_chunk(i):
            wd = chunks[i][1]
            free = [done_t[i - NHL]] if i >= NHL else []
            r, h, l = raw[:, i % NRAW, 0:wd], wH[:, i % NHL, 0:wd], wL[:, i % NHL, 0:wd]
            th = op("act", free + [dma_t[i]], lambda e: e.activation(h, r, ACT.Copy))
            tl = op("dve", free + [dma_t[i], th],
                    lambda e: e.tensor_tensor(l, r, h.bitcast(F32), ALU.subtract))
            split_t.append([th, tl])

        taken = [0]

        def pump():
            while len(split_t) < len(chunks) and len(split_t) - NHL < len(done_t):
                while len(dma_t) < min(len(chunks), len(split_t) + NRAW):
                    load_chunk(len(dma_t))
                split_chunk(len(split_t))
            while len(dma_t) < min(len(chunks), len(split_t) + NRAW):
                load_chunk(len(dma_t))

        def take(key, ahead=True):
            i = taken[0]
            taken[0] += 1
            assert chunks[i][0] == key, (chunks[i][0], key)
            if ahead or i >= len(split_t):
                pump()
            return wH[:, i % NHL, :], wL[:, i % NHL, :], split_t[i]

        def mm3(eng, out, lhs, rhs, start, stop):
            eng.matmul(out, lhs[0], rhs[1], start=start, stop=False)
            eng.matmul(out, lhs[1], rhs[0], start=False, stop=False)
            return eng.matmul(out, lhs[0], rhs[0], start=False, stop=stop)

        bank_t = [[] for _ in range(8)]
        TOK = (slice(0, 128), slice(128, 256))

        def a_pieces(name, col, width, kt, group, lhs, banks, after, end, ahead=True, by_chunk=False):
            parts = {}
            out = []
            steps = [(tok, k) for tok in range(2) for k in range(0, kt, group)]
            if by_chunk:
                steps.sort(key=lambda s: s[1])
            for tok, k in steps:
                    def piece(tok=tok, k=k, n=min(group, kt - k)):
                        if tok == 0:
                            parts[k] = take(("a", name, col, width, k, n), ahead)
                        h, l, ready = parts[k]

                        def go(eng):
                            for j in range(n):
                                w = slice(j * width, (j + 1) * width)
                                last = mm3(eng, ps[:, banks[tok], 0:width],
                                           (lhs[0][:, k + j, TOK[tok]], lhs[1][:, k + j, TOK[tok]]),
                                           (h[:, w], l[:, w]), k + j == 0, k + j == kt - 1)
                            return last
                        t = op("pe", after[tok] + ready + bank_t[banks[tok]], go)
                        if tok == 1:
                            done_t.append(t)
                        if k + n == kt:
                            end(tok, t)
                    out.append(piece)
            return out

        def a_mm(*args):
            for piece in a_pieces(*args):
                piece()

        def s_mm(pairs, rhs, outs, after, kt=8):
            h, l, ready = take(("s", tuple(pairs), kt))

            def go(eng):
                for i, out in enumerate(outs):
                    for k in range(kt):
                        w = slice((kt * i + k) * 128, (kt * i + k + 1) * 128)
                        last = mm3(eng, out, (h[:, w], l[:, w]), (rhs[0][:, k, :], rhs[1][:, k, :]),
                                   k == 0, k == kt - 1)
                return last
            t = op("pe", after + ready, go)
            done_t.append(t)
            return t

        def d_part(part, tok, lhs, f0, first, last, after):
            h, l, ready = part

            def go(eng):
                for f in range(2):
                    for c in range(2):
                        w = slice(1024 * f + 512 * c, 1024 * f + 512 * c + 512)
                        end = mm3(eng, ps[:, 2 * tok + c, :],
                                  (lhs[0][:, f0 + f, TOK[tok]], lhs[1][:, f0 + f, TOK[tok]]),
                                  (h[:, w], l[:, w]), first and f == 0, last and f == 1)
                return end
            return op("pe", ready + after + (bank_t[2 * tok] + bank_t[2 * tok + 1] if first else []), go)

        def d_pair(name, j, lhs, f0, first, last, after):
            parts = [take(("d", name, j)), None]
            out = []
            for tok in range(2):
                for c in range(2):
                    if tok == 0 and c == 1:
                        parts[1] = take(("d", name, j + 1))
                    t = d_part(parts[c], tok, lhs[c], f0[c], first and c == 0, last and c == 1, after[c][tok])
                    if tok == 1:
                        done_t.append(t)
                out.append(t)
            return out

        def project(name, after):
            d_pair(name, 0, (act, act), (0, 2), True, False, (after, after))
            return d_pair(name, 2, (act, act), (4, 6), False, True, (after, after))

        def bcast(off, width, after):
            return dma("bc", after, bc[:, 0:width], rows_d[off:off + width].partition_broadcast(128))

        stat = [0]

        def stats(n):
            stat[0] += n
            assert stat[0] <= 256
            return st[:, stat[0] - n:stat[0]]

        def power(ss, n, inv, after):
            out = stats(n)
            t = op("pool", after, lambda e: e.tensor_scalar(out, ss, inv, EPS, ALU.mult, ALU.add))
            t = op("pool", [t], lambda e: e.tensor_tensor(out, out, consts[:, 0:1].to_broadcast([128, n])
                                                          if n > 1 else consts[:, 0:1], ALU.pow))
            return out, t

        def flip_tok(src, kt, banks, dst, tok, after, free, width=128):
            out = []
            for g, k0 in enumerate(range(0, kt, 4)):
                n = min(4, kt - k0)
                b = banks[g % len(banks)]

                def go(eng, k0=k0, n=n, b=b):
                    for j in range(n):
                        last = eng.transpose(ps[0:width, b, 128 * j:128 * j + 128], src(k0 + j), ident[:, :])
                    return last
                t = op("pe", after[g] + bank_t[b], go)
                pv = ps[0:width, b, 0:128 * n].rearrange("p (k t) -> p k t", t=128)
                h = dst[0][:, k0:k0 + n, TOK[tok]]
                th = op("act", [t] + free, lambda e, h=h, pv=pv: e.activation(h, pv, ACT.Copy))
                bank_t[b] = [th]
                out.append(th)
                if len(dst) == 2:
                    l = dst[1][:, k0:k0 + n, TOK[tok]]
                    tl = op("dve", [th] + free, lambda e, h=h, l=l, pv=pv:
                            e.tensor_tensor(l, pv, h.bitcast(F32), ALU.subtract))
                    bank_t[b] = [th, tl]
                    out.append(tl)
            return out

        def norm_tok(tok, src, width, dst_sb, gain, gain_t, after):
            ss = stats(1)
            t = op("act", after, lambda e: e.activation(dst_sb, src, ACT.Square, accum_out=ss))
            rs, tp = power(ss, 1, 1.0 / width, [t])
            out = []
            half = 512 if width == 1024 else width
            for c in range(0, width, half):
                out.append([op("dve", [tp, gain_t, t], lambda e, c=c: e.scalar_tensor_tensor(
                    dst_sb[:, c:c + half], src[:, c:c + half], rs, gain[:, c:c + half], ALU.mult, ALU.mult))])
            return out

        def copier(out, dst, banks, width, after, engines=("act", "act")):
            def end(tok, t):
                if engines[tok] == "act":
                    t = op("act", [t] + after, lambda e: e.activation(dst(tok), ps[:, banks[tok], 0:width], ACT.Copy))
                else:
                    t = op("dve", [t] + after, lambda e: e.tensor_copy(dst(tok), ps[:, banks[tok], 0:width]))
                bank_t[banks[tok]] = [t]
                out.append(t)
            return end

        xv = x_d.rearrange("(t p) n -> t p n", p=128)
        t_x0 = [dma("x0", [], xr[:, 0, :], xv[0]), dma("x1", [], xr[:, 1, :], xv[1])]
        t_bc = bcast(R_PRE_MIX, 1024, [])
        t_id = dma("id", [], ident[:, :], const_d[:, 0:128], "act")
        posi = FF[:, 0:2].bitcast(I32)
        invf = FF[:, 16:40]
        mtmp0 = FF[:, 3072:4096]
        dma("in", [], posi, pos_d, "act")
        dma("in", [], invf, const_d[:, 512:536], "act")
        dma("in", [], amask[:, :], const_d[:, 128:512], "act")
        dma("in", [], cols[:, :], cols_d, "act")
        t_in = dma("in", [], mtmp0, const_d[:, 536:1560], "act")
        op("dve", [], lambda e: e.memset(consts[:, 0:1], -0.5))
        t_c = op("dve", [], lambda e: e.memset(consts[:, 1:2], float(np.pi / 2)))
        wait("pool", [t_c])
        op("act", [t_c], lambda e: e.activation(consts[:, 2:3], consts[:, 1:2], ACT.Square))
        for n in range(NRAW):
            load_chunk(n)
        act = (aH, aL)

        cq = FF[:, 8384:9152].rearrange("p (t n) -> p t n", t=2)
        t_h, t_xn, t_cq = [], [], []
        first = a_pieces("w_in", 1536, 384, 8, 4, act, (0, 1), t_h,
                         copier(t_cq, lambda tok: cq[:, tok, :], (0, 1), 384, []))
        wait("pe", [t_id])
        halves = [None, None]

        def first_norm(tok):
            halves[tok] = norm_tok(tok, xr[:, tok, :], 1024, xn[:, tok, :], bc[:, :], t_bc, [t_x0[tok]])
            t_xn.extend(halves[tok][0] + halves[tok][1])

        def first_flip(tok):
            t_h.append(flip_tok(lambda k: xn[:, tok, 128 * k:128 * k + 128], 8, (4 + 2 * tok, 5 + 2 * tok),
                                act, tok, halves[tok], []))
        first_norm(0)
        first_flip(0)
        first_norm(1)
        split_chunk(0)
        split_chunk(1)
        first[0]()
        first[1]()
        first_flip(1)
        first[2]()
        first[3]()
        t_hh = t_h[0] + t_h[1]
        t_bc = bcast(R_QN, 640, t_xn)
        t_hm = op("dve", [t_in], lambda e: e.tensor_copy(hmask[:, :, :].rearrange("p l t -> p (l t)"), mtmp0))

        posf, ang, nn, rr, ab = (FF[:, 48:50], FF[:, 64:112], FF[:, 128:176], FF[:, 192:240], FF[:, 256:304])
        rope = FF[:, 8256:8352]
        sn, cs = rope[:, 0:48], rope[:, 48:96]
        t = op("dve", [t_in], lambda e: e.tensor_copy(posf, posi))
        for tok in range(2):
            ta = op("dve", [t], lambda e, tok=tok:
                    e.tensor_scalar(ang[:, 24 * tok:24 * tok + 24], invf, posf[:, tok:tok + 1], None, ALU.mult))
        t = op("dve", [ta], lambda e: e.tensor_scalar(nn, ang, 1.0 / TWO_PI, MAGIC, ALU.mult, ALU.add))
        t = op("dve", [t], lambda e: e.tensor_scalar(nn, nn, MAGIC, None, ALU.subtract))
        src = ang
        for part in (PI_1, PI_2, PI_3):
            t = op("dve", [t], lambda e, part=part, src=src:
                   e.scalar_tensor_tensor(rr, nn, -part, src, ALU.mult, ALU.add))
            src = rr
        t = op("dve", [t], lambda e: e.tensor_scalar(rr, rr, 3.1415925, -3.1415925, ALU.min, ALU.max))
        t = op("dve", [t], lambda e: e.scalar_tensor_tensor(ab, rr, -1.0, rr, ALU.mult, ALU.max))
        op("act", [t], lambda e: e.activation(sn, rr, ACT.Sin))
        t_rope = op("act", [t, t_c], lambda e: e.activation(cs, ab, ACT.Sin, scale=-1.0, bias=consts[:, 1:2]))

        def table(x, heads, half, lo):
            v = x.rearrange("p (t f) -> p t f", t=2)[:, :, lo:lo + half]
            return v.unsqueeze(2).to_broadcast([128, 2, heads, half])

        def rotate(v1, v2, heads, half, lo, tmp, after):
            c, s = table(cs, heads, half, lo), table(sn, heads, half, lo)
            n = 2 * heads * half
            a, b = (tmp[:, i * n:(i + 1) * n].rearrange("p (t h f) -> p t h f", t=2, h=heads) for i in range(2))
            t1 = op("dve", after + [t_rope], lambda e: e.tensor_tensor(a, v1, s, ALU.mult))
            t2 = op("dve", [], lambda e: e.tensor_tensor(b, v2, s, ALU.mult))
            t3 = op("dve", [t1, t2], lambda e: e.tensor_tensor(v1, v1, c, ALU.mult))
            t4 = op("dve", [t3], lambda e: e.tensor_tensor(v2, v2, c, ALU.mult))
            t5 = op("dve", [t4], lambda e: e.tensor_tensor(v1, v1, b, ALU.subtract))
            return op("dve", [t5], lambda e: e.tensor_tensor(v2, v2, a, ALU.add))

        va = FF[:, 0:1024].rearrange("p (t n) -> p t n", t=2)
        mqT = FF[:, 1024:2048].rearrange("p (k t) -> p k t", k=4)
        mkT = FF[:, 2048:3072].rearrange("p (k t) -> p k t", k=4)
        vb = FF[:, 3072:4096].rearrange("p (t n) -> p t n", t=2)
        gates = FF[:, 4096:8192].rearrange("p (t n) -> p t n", t=2)
        ckr = FF[:, 9152:9728].rearrange("p (t n) -> p t n", t=2)
        rtmp = FF[:, 9728:10752]
        lkT = FF[0:96, 10752:12800].rearrange("p (h t) -> p h t", h=8)
        lqT = FF[0:96, 12800:14848].rearrange("p (h t) -> p h t", h=8)
        qk = xn

        t_ck, t_q, t_k, t_va, t_lq, t_vb = [], [], [], [], [], []
        a_mm("w_in", 1920, 288, 8, 4, act, (2, 3), t_h, copier(t_ck, lambda tok: ckr[:, tok, :], (2, 3), 288, []))
        cqT = tuple(RR[:, i * 768:(i + 1) * 768].rearrange("p (k t) -> p k t", k=3) for i in range(2))
        ckT = tuple(RR[:, 1536 + i * 512:2048 + i * 512].rearrange("p (k t) -> p k t", k=2) for i in range(2))
        lat_n = []
        for src, width, g0, t_s in ((cq, 384, 0, t_cq), (ckr, 256, 384, t_ck)):
            for tok in range(2):
                ss = stats(1)
                t = op("act", [t_s[tok]], lambda e, tok=tok, ss=ss, src=src, width=width, g0=g0:
                       e.activation(gates[:, tok, g0:g0 + width], src[:, tok, 0:width], ACT.Square, accum_out=ss))
                rs, tp = power(ss, 1, 1.0 / width, [t])
                lat_n.append(op("dve", [tp, t_bc, t], lambda e, tok=tok, rs=rs, src=src, width=width, g0=g0:
                                e.scalar_tensor_tensor(src[:, tok, 0:width], src[:, tok, 0:width], rs,
                                                       bc[:, g0:g0 + width], ALU.mult, ALU.mult)))
        t_bc = bcast(R_POST_MIX, 1024, lat_n)
        a_mm("w_in", 0, 512, 8, 4, act, (0, 1), t_h,
             copier(t_q, lambda tok: qk[:, tok, 0:512], (0, 1), 512, t_hh))
        a_mm("w_in", 512, 512, 8, 4, act, (2, 3), t_h,
             copier(t_k, lambda tok: qk[:, tok, 512:1024], (2, 3), 512, t_hh, ("dve", "dve")))
        qk4 = qk[:, :, :].rearrange("p t (h d) -> p t h d", d=64)
        t_rq = rotate(qk4[:, :, :, 0:8], qk4[:, :, :, 8:16], 16, 8, 0, rtmp, t_q + t_k)
        lat = [[[], []], [[], []]]
        for tok in range(2):
            lat[0][tok] = flip_tok(lambda k, tok=tok: cq[:, tok, 128 * k:128 * k + 128], 3, (4 + tok,), cqT, tok,
                                   [[lat_n[tok]]], [])
            lat[1][tok] = flip_tok(lambda k, tok=tok: ckr[:, tok, 128 * k:128 * k + 128], 2, (6 + tok,), ckT, tok,
                                   [[lat_n[2 + tok]]], [])
        t_kn = s_mm([("w_ukv", h) for h in range(8)], ckT,
                    [ps[:, 4 + h // 2, 256 * (h % 2):256 * (h % 2) + 256] for h in range(8)],
                    lat[1][0] + lat[1][1] + bank_t[4] + bank_t[5] + bank_t[6] + bank_t[7], kt=2)
        t_k2 = []
        for g in range(2):
            t_k2.append(op("act", [t_kn, t_rq], lambda e, g=g: e.activation(
                lkT[0:64, 4 * g:4 * g + 4, :].rearrange("p (b h) t -> p b (h t)", b=2),
                ps[0:64, 4 + 2 * g:6 + 2 * g, :], ACT.Copy)))
            bank_t[4 + 2 * g] = bank_t[5 + 2 * g] = [t_k2[-1]]
        a_mm("w_ukv_v", 0, 512, 2, 2, ckT, (2, 3), lat[1],
             copier(t_vb, lambda tok: vb[:, tok, :], (2, 3), 512, [t_hm]))
        t_mqk = []
        for tok in range(2):
            t_mqk += flip_tok(lambda k, tok=tok: qk[:, tok, 128 * k:128 * k + 128], 4, (4 + tok,), (mqT,), tok,
                              [[t_rq]], [])
            t_mqk += flip_tok(lambda k, tok=tok: qk[:, tok, 512 + 128 * k:640 + 128 * k], 4, (6 + tok,), (mkT,), tok,
                              [[t_rq]], [])
        lq = xn[:, :, 0:768].rearrange("p t (h d) -> p t h d", d=96)
        for n in range(2):
            banks = (2, 3) if n else (0, 1)
            a_mm("w_uq", 384 * n, 384, 3, 3, cqT, banks, lat[0],
                 copier(t_lq, lambda tok, n=n: xn[:, tok, 384 * n:384 * n + 384], banks, 384, t_mqk))
        lat_done = done_t[-1]
        a_mm("w_in", 1024, 512, 8, 4, act, (0, 1), t_h,
             copier(t_va, lambda tok: va[:, tok, :], (0, 1), 512, [t_rope]))
        kr4 = ckr[:, :, 256:288].unsqueeze(2)
        t_rk = rotate(kr4[:, :, :, 0:16], kr4[:, :, :, 16:32], 1, 16, 8, FF[:, 10240:10368], [t_ck[1], t_rq])
        t_rl = rotate(lq[:, :, :, 64:80], lq[:, :, :, 80:96], 8, 16, 8, FF[:, 9728:10752], t_lq + [t_rk])

        def go(eng):
            for tok in range(2):
                last = eng.transpose(ps[0:32, 2, TOK[tok]], ckr[:, tok, 256:288], ident[:, :])
            return last
        t = op("pe", [t_rk] + bank_t[2], go)
        t_k2.append(op("act", [t], lambda e: e.activation(
            lkT[64:96, :, :], ps[0:32, 2, 0:256].unsqueeze(1).to_broadcast([32, 8, 256]), ACT.Copy)))
        bank_t[2] = [t_k2[-1]]
        t_q2 = []
        for tok in range(2):
            t_q2 += flip_tok(lambda h, tok=tok: lq[:, tok, h, :], 8, (4 + 2 * tok, 5 + 2 * tok), (lqT,), tok,
                             [[t_rl], [t_rl]], [], 96)
        bgate = xn[:, :, :].rearrange("p t n -> p (t n)")
        t_bg = dma("bg", t_q2, bgate, rows_d[R_BGATE:R_BGATE + 2048].partition_broadcast(128))

        oT = [tuple(RR[:, (2 * a + i) * 1024:(2 * a + i + 1) * 1024].rearrange("p (k t) -> p k t", k=4)
                    for i in range(2)) for a in range(2)]
        at = FF[:, 8384:10688]
        sm = [at[:, i * 384:(i + 1) * 384] for i in range(3)]
        pT = [at[:, 1152 + i * 384:1536 + i * 384] for i in range(2)]
        sm_t, pT_t = [[], [], []], [[], []]
        at_free = t_q2 + t_k2 + [t_rl]
        head = {}
        t_o = [[], []]
        t_g = [[], []]

        def scores(i):
            b = 4 + i % 2
            h = i % 8
            if i < 8:
                r = slice(64 * (h % 2), 64 * (h % 2) + 64)
                q, k, scale, dep = mqT[r, h // 2, :], mkT[r, h // 2, :], 0.125, t_mqk
            else:
                q, k, scale, dep = lqT[:, h, :], lkT[:, h, :], 96 ** -0.5, t_q2 + t_k2

            def go(eng):
                eng.matmul(ps[:, b, 0:128], q[:, 0:128], k[:, 0:128], start=True, stop=True)
                return eng.matmul(ps[:, b, 128:384], q[:, 128:256], k[:, 0:256], start=True, stop=True)
            t = op("pe", dep + bank_t[b], go)
            j = i % 3
            ts = op("dve", [t] + sm_t[j] + at_free, lambda e:
                    e.scalar_tensor_tensor(sm[j], ps[:, b, 0:384], scale, amask[:, :], ALU.mult, ALU.add))
            bank_t[b] = [ts]
            m = stats(6) if i < 3 else head[i - 3]["m"]
            head[i] = {"m": m}
            op("dve", [ts], lambda e: e.tensor_reduce(m[:, 0:1], sm[j][:, 0:128], AX, ALU.max, negate=True))
            tm = op("dve", [ts], lambda e: e.tensor_reduce(m[:, 1:2], sm[j][:, 128:384], AX, ALU.max, negate=True))
            op("act", [tm], lambda e:
               e.activation(sm[j][:, 0:128], sm[j][:, 0:128], ACT.Exp, bias=m[:, 0:1], accum_out=m[:, 2:3]))
            te = op("act", [], lambda e:
                    e.activation(sm[j][:, 128:384], sm[j][:, 128:384], ACT.Exp, bias=m[:, 1:2], accum_out=m[:, 3:4]))
            head[i]["e"] = te

        def scale_p(i):
            j, m, te = i % 3, head[i]["m"], head[i]["e"]
            tr = op("dve", [te], lambda e: e.reciprocal(m[:, 4:6], m[:, 2:4]))
            op("dve", [tr], lambda e: e.tensor_scalar(sm[j][:, 0:128], sm[j][:, 0:128], m[:, 4:5], None, ALU.mult))
            head[i]["p"] = op("dve", [tr], lambda e:
                              e.tensor_scalar(sm[j][:, 128:384], sm[j][:, 128:384], m[:, 5:6], None, ALU.mult))

        def flip(i):
            j, c, b = i % 3, i % 2, 6 + i % 2

            def go(eng):
                for n in range(3):
                    last = eng.transpose(ps[:, b, 128 * n:128 * n + 128], sm[j][:, 128 * n:128 * n + 128], ident[:, :])
                return last
            t = op("pe", [head[i]["p"]] + bank_t[b], go)
            sm_t[j] = [t]
            te = op("act", [t] + pT_t[c], lambda e: e.activation(pT[c], ps[:, b, 0:384], ACT.Copy))
            bank_t[b] = [te]
            head[i]["pT"] = te

        def mix(i):
            j, h = i % 2, i % 8
            b = (i // 2) % 2
            v = (va if i < 8 else vb)[:, :, 64 * h:64 * h + 64]
            r = slice(64 * (h % 2), 64 * (h % 2) + 64)
            dep = t_va if i < 8 else t_vb

            def go(eng):
                eng.matmul(ps[r, b, 0:128], v[:, 0, :], pT[j][:, 0:128], start=True, stop=True)
                eng.matmul(ps[r, b, 128:256], v[:, 0, :], pT[j][:, 128:256], start=True, stop=False)
                return eng.matmul(ps[r, b, 128:256], v[:, 1, :], pT[j][:, 256:384], start=False, stop=True)
            t = op("pe", [head[i]["pT"]] + dep + (bank_t[b] if h % 2 == 0 else []), go)
            pT_t[j] = [t]
            if h % 2:
                hi, lo = (o[:, h // 2, :] for o in oT[i // 8])
                th = op("act", [t, lat_done], lambda e: e.activation(hi, ps[:, b, 0:256], ACT.Copy))
                tl = op("dve", [th], lambda e: e.tensor_tensor(lo, ps[:, b, 0:256], hi.bitcast(F32), ALU.subtract))
                bank_t[b] = [th, tl]
                t_o[i // 8] += [th, tl]

        fill = []
        for n in range(4):
            def gate(tok, t, n=n):
                d = gates[:, tok, 512 * n:512 * n + 512]
                td = op("dve", [t, t_bg] + lat_n, lambda e: e.tensor_tensor(
                    d, ps[:, 2 + tok, :], bgate[:, 512 * n:512 * n + 512], ALU.add))
                bank_t[2 + tok] = [td]
                t_g[tok].append(td)
            fill += a_pieces("w_in", 2208 + 512 * n, 512, 8, 4, act, (2, 3), t_h, gate, by_chunk=True)
        for i in range(19):
            if i < 16:
                scores(i)
            if 1 <= i < 17:
                scale_p(i - 1)
            if i < 14 or 15 <= i < 17:
                fill.pop(0)()
            if 2 <= i < 18:
                flip(i - 2)
            if i >= 3:
                mix(i - 3)
        for tok in range(2):
            t_g[tok] = [op("act", t_g[tok], lambda e, tok=tok:
                           e.activation(gates[:, tok, :], gates[:, tok, :], ACT.Sigmoid))]

        merged = xn
        t_m = [[], []]
        mtmp = FF[:, 0:1024].rearrange("p (t n) -> p t n", t=2)
        for n in range(2):
            t_a, t_b = [None, None], [None, None]

            def end_a(tok, t):
                t_a[tok] = t

            def end_b(tok, t, n=n):
                d = merged[:, tok, 512 * n:512 * n + 512]
                g = gates[:, tok, :]
                t1 = op("dve", [t_a[tok]] + t_g[0] + t_g[1], lambda e:
                        e.tensor_tensor(d, ps[:, 4 * n + tok, :], g[:, 512 * n:512 * n + 512], ALU.mult))
                t2 = op("dve", [t, t1], lambda e:
                        e.tensor_tensor(mtmp[:, tok, :], ps[:, 4 * n + 2 + tok, :], g[:, 1024 + 512 * n:1536 + 512 * n],
                                        ALU.mult))
                bank_t[4 * n + tok], bank_t[4 * n + 2 + tok] = [t1], [t2]
                t_m[tok].append([op("dve", [t1, t2], lambda e: e.tensor_tensor(d, d, mtmp[:, tok, :], ALU.add))])
            pa = a_pieces("w_branch_a", 512 * n, 512, 4, 4, oT[0], (4 * n, 4 * n + 1), [t_o[0], t_o[0]], end_a)
            pb = a_pieces("w_branch_b", 512 * n, 512, 4, 4, oT[1], (4 * n + 2, 4 * n + 3), [t_o[1], t_o[1]], end_b)
            pa[0]()
            pb[0]()
            pa[1]()
            if n == 0:
                pb[1]()
        t_mt = []
        for tok in range(2):
            t_mt.append(flip_tok(lambda k, tok=tok: merged[:, tok, 128 * k:128 * k + 128], 8,
                                 (2 * tok, 2 * tok + 1), act, tok, t_m[tok], []))
            if tok == 0:
                pb[1]()
        t_y = project("w_out", t_mt)

        def residual(tok, t, post_t):
            y = ps[:, 2 * tok:2 * tok + 2, :]
            v = xr[:, tok, :].rearrange("p (b n) -> p b n", b=2)
            if post_t is None:
                t = op("dve", [t], lambda e: e.tensor_tensor(v, y, v, ALU.add))
                bank_t[2 * tok] = bank_t[2 * tok + 1] = [t]
                return t
            ss = stats(1)
            d = xn[:, tok, :].rearrange("p (b n) -> p b n", b=2)
            g = bc[:, :].rearrange("p (b n) -> p b n", b=2)
            t1 = op("act", [t], lambda e: e.activation(d, y, ACT.Square, accum_out=ss))
            rs, tp = power(ss, 1, 1.0 / 1024, [t1])
            t = op("dve", [tp, t1, post_t], lambda e: e.scalar_tensor_tensor(d, y, rs, g, ALU.mult, ALU.mult))
            bank_t[2 * tok] = bank_t[2 * tok + 1] = [t]
            post_done.append(t)
            return op("dve", [t], lambda e: e.tensor_tensor(xr[:, tok, :], xr[:, tok, :], xn[:, tok, :], ALU.add))

        post_done = []

        def between(t_y, post_t, row, post_row, name, col, end):
            t_a, halves_t = [], []
            pieces = a_pieces(name, col, 512, 8, 4, act, (6, 7), t_a, end, ahead=False)
            t_gain = dma("bg", bc2_t[0], bc2, rows_d[row:row + 1024].partition_broadcast(128))
            halves = []

            def norm(tok):
                t = residual(tok, t_y[tok], post_t)
                halves.append(norm_tok(tok, xr[:, tok, :], 1024, xn[:, tok, :], bc2, t_gain, [t]))
                halves_t.extend(halves[tok][0] + halves[tok][1])

            def flip(tok):
                t_a.append(flip_tok(lambda k: xn[:, tok, 128 * k:128 * k + 128], 8,
                                    (4, 5), act, tok, halves[tok], [t_y[tok]]))
            norm(0)
            flip(0)
            norm(1)
            pieces[0]()
            pieces[1]()
            flip(1)
            pump()
            pieces[2]()
            pieces[3]()
            bc2_t[0] = halves_t
            if post_row is not None:
                post_t = bcast(post_row, 1024, halves_t + post_done)
            return t_a, post_t

        def turned(outs, banks, t_a):
            def end(tok, t):
                d = xn[:, tok, 0:512]
                tc = op("act", [t], lambda e: e.activation(d, ps[:, 6 + tok, :], ACT.Copy))
                bank_t[6 + tok] = [tc]

                def turn():
                    def go(eng):
                        for i, out in enumerate(outs):
                            last = eng.transpose(out[:, TOK[tok]], xn[:, tok, 128 * i:128 * i + 128], ident[:, :])
                        return last
                    return op("pe", [tc] + bank_t[banks[0]] + bank_t[banks[1]], go)
                t_a.append(turn)
            return end

        bc2 = FF[:, 13824:14848]
        bc2_t = [t_o[1]]

        hid = [tuple(RR[:, (2 * j + i) * 512:(2 * j + i + 1) * 512].rearrange("p (f t) -> p f t", f=2)
                     for i in range(2)) for j in range(2)]
        htmp = [FF[:, j * 1024:j * 1024 + 1024].rearrange("p (a f t) -> p a f t", a=2, f=2) for j in range(2)]

        def mlp(down, n, up, post, beside=lambda: None):
            ready = {}
            free = [[], []]
            for j in range(n):
                ready[j] = post(j, up(j), free[j % 2], ready.get(j - 2, []))
                if j == 3:
                    beside()
                if 0 < j < n - 1:
                    part = take(("d", down, j - 1))
                    for tok in range(2):
                        t = d_part(part, tok, hid[(j - 1) % 2], 0, j == 1, False, ready[j - 1])
                    done_t.append(t)
                    free[(j - 1) % 2] = [t]
            a, b = n - 2, n - 1
            return d_pair(down, a, (hid[a % 2], hid[b % 2]), (0, 0), False, True,
                          ((ready[a], ready[a]), (ready[b], ready[b])))

        lbt, ct = stats(40), stats(48)
        mx, e0, e1, lb, om = (lbt[:, 8 * i:8 * i + 8] for i in range(5))
        nl, z, w1, lw, c4, c8 = (ct[:, 8 * i:8 * i + 8] for i in range(6))
        t_bound = []

        def lower_bounds():
            l0, l1 = cols[:, C_LB0:C_LB0 + 8], cols[:, C_LB1:C_LB1 + 8]
            t1 = op("dve", [t_in], lambda e: e.tensor_tensor(mx, l0, l1, ALU.max))
            t2 = op("dve", [t1], lambda e: e.tensor_tensor(e0, l0, mx, ALU.subtract))
            t3 = op("dve", [t1], lambda e: e.tensor_tensor(e1, l1, mx, ALU.subtract))
            e01 = lbt[:, 8:24]
            t4 = op("act", [t2, t3], lambda e: e.activation(e01, e01, ACT.Exp))
            t5 = op("dve", [t4], lambda e: e.tensor_tensor(mx, e0, e1, ALU.add))
            t6 = op("dve", [t5], lambda e: e.reciprocal(mx, mx))
            t7 = op("dve", [t6], lambda e: e.tensor_tensor(lb, e0, mx, ALU.mult))
            t_bound.append(op("dve", [t7], lambda e: e.tensor_tensor(om, e1, mx, ALU.mult)))
            lam = cols[:, C_LAM:C_LAM + 8]
            t = op("dve", [t_in], lambda e: e.scalar_tensor_tensor(nl, lam, -1.0, lam, ALU.mult, ALU.min))
            t = op("act", [t], lambda e: e.activation(z, nl, ACT.Exp))
            t = op("dve", [t], lambda e: e.tensor_scalar(w1, z, 1.0, None, ALU.add))
            t = op("act", [t], lambda e: e.activation(lw, w1, ACT.Ln))
            t = op("dve", [t], lambda e: e.tensor_scalar(w1, w1, 1.0, 1e-30, ALU.subtract, ALU.max))
            t = op("dve", [t], lambda e: e.tensor_scalar(nl, lam, -1.0, 0.0, ALU.mult, ALU.max))
            t = op("dve", [t], lambda e: e.reciprocal(c4, w1))
            t = op("dve", [t], lambda e: e.tensor_tensor(c4, c4, z, ALU.mult))
            t = op("dve", [t], lambda e: e.tensor_tensor(c4, c4, lw, ALU.mult))
            t = op("dve", [t], lambda e: e.tensor_scalar(w1, w1, 1e-30, None, ALU.is_le))
            t = op("dve", [t], lambda e: e.tensor_tensor(w1, w1, z, ALU.mult))
            t = op("dve", [t], lambda e: e.tensor_tensor(c4, c4, w1, ALU.add))
            t = op("dve", [t], lambda e: e.tensor_tensor(c4, c4, nl, ALU.add))
            t = op("dve", [t], lambda e: e.tensor_scalar(c4, c4, 4.0, None, ALU.mult))
            t_bound.append(op("dve", [t], lambda e: e.tensor_scalar(c8, c4, -2.0, None, ALU.mult)))

        def relu_stage(t_y, post_t):
            UB = (4, 5, 6, 7)
            outs = lambda j: [ps[:, UB[j % 4], 0:256], ps[:, UB[j % 4], 256:512]]
            pair = lambda j: [("w_up", 2 * j), ("w_up", 2 * j + 1)]
            turns = []
            t_a, post_t = between(t_y, post_t, R_PRE_MLP, R_POST_MLP, "w_up", 0,
                                  turned(outs(0) + outs(1), (4, 5), turns))
            t_a = t_a[0] + t_a[1]
            tk = []

            def up(j):
                n = j + 2
                if n < 16:
                    t = s_mm(pair(n), act, outs(n), t_a + bank_t[UB[n % 4]])
                if j == 0:
                    tk.extend([[turn() for turn in turns][1]] * 2)
                if n < 16:
                    tk.append(t)
                return tk[j]

            def post(j, tu, free, before):
                b = UB[j % 4]
                r, q = htmp[j % 2][:, 0], htmp[j % 2][:, 1]
                hi, lo = hid[j % 2]
                pv = ps[:, b, :].rearrange("p (f t) -> p f t", f=2)
                t1 = op("act", [tu] + before, lambda e: e.activation(r, pv, ACT.Relu))
                bank_t[b] = [t1]
                t2 = op("act", [t1] + free, lambda e: e.activation(hi, r, ACT.Square))
                t3 = op("dve", [t1], lambda e: e.tensor_tensor(q, r, r, ALU.mult))
                t4 = op("dve", [t2, t3] + free, lambda e: e.tensor_tensor(lo, q, hi.bitcast(F32), ALU.subtract))
                return [t2, t4]
            return mlp("w_down", 16, up, post, lower_bounds), post_t

        t_y, t_post = relu_stage(t_y, t_bc)
        t_lb, t_c4 = t_bound

        Q = FF[:, 0:2048].rearrange("p (h t) -> p h t", h=8)
        K = FF[:, 2048:4096].rearrange("p (h t) -> p h t", h=8)
        E0 = FF[:, 4096:6144]
        E1 = FF[:, 6144:7168]
        V = FF[:, 7168:9216].rearrange("p (t n) -> p t n", t=2)
        G = FF[:, 9216:11264].rearrange("p (t n) -> p t n", t=2)
        AC = FF[:, 11264:13312].rearrange("p (h t) -> p h t", h=8)
        XC = FF[:, 13312:14336].rearrange("p (h t) -> p h t", h=8)
        sg = [FF[:, 14336 + 256 * i:14592 + 256 * i] for i in range(2)]
        E = E0.rearrange("p (h t) -> p h t", h=8)
        h_pair = lambda h: [("hgrn_w_in", h), ("hgrn_w_in", 8 + h)]
        h_bank = lambda h: 4 + h % 4
        h_outs = lambda h: [ps[:, h_bank(h), 0:256], ps[:, h_bank(h), 256:512]]
        t_v = []
        t_a2, t_bc = between(t_y, t_post, R_MIX0, R_HNORM, "hgrn_w_in", 2048,
                             copier(t_v, lambda tok: V[:, tok, 0:512], (6, 7), 512, t_y))
        t_a = t_a2[0] + t_a2[1]
        t_z = op("pool", t_y, lambda e: e.memset(AC, 0.0))
        sg_t = [[], []]
        t_hd = []
        for h in range(8):
            b = h_bank(h)
            tu = s_mm(h_pair(h), act, h_outs(h), t_a + bank_t[b])
            qv, fv = ps[:, b, 0:256], ps[:, b, 256:512]
            s = sg[h % 2]
            c = slice(h, h + 1)
            t1 = op("act", [tu] + sg_t[h % 2], lambda e, s=s, qv=qv: e.activation(s, qv, ACT.Sigmoid))
            t2 = op("act", [], lambda e, h=h, fv=fv: e.activation(E[:, h, :], fv, ACT.Sigmoid))
            t3 = op("act", [], lambda e, h=h, fv=fv: e.activation(K[:, h, :], fv, ACT.Sigmoid, scale=-1.0))
            t4 = op("dve", [t3], lambda e, h=h, s=s, qv=qv: e.tensor_tensor(Q[:, h, :], qv, s, ALU.mult))
            bank_t[b] = [t3, t4]
            sg_t[h % 2] = [t4]
            t5 = op("dve", [t2, t_lb], lambda e, h=h, c=c:
                    e.tensor_scalar(E[:, h, :], E[:, h, :], om[:, c], lb[:, c], ALU.mult, ALU.add))
            t6 = op("dve", [t3, t_lb], lambda e, h=h, c=c:
                    e.tensor_scalar(K[:, h, :], K[:, h, :], om[:, c], None, ALU.mult))
            t_hd.append([t4, t5, t6])

        t_gg = []
        fill = []
        for n in range(1, 4):
            banks = (0, 1) if n % 2 else (2, 3)
            if n < 2:
                end = copier(t_v, lambda tok, n=n: V[:, tok, 512 * n:512 * n + 512], banks, 512, t_y)
            else:
                def end(tok, t, n=n, banks=banks):
                    d = G[:, tok, 512 * n - 1024:512 * n - 512]
                    b = banks[tok]
                    t1 = op("act", [t], lambda e: e.activation(d, ps[:, b, :], ACT.Sigmoid))
                    t2 = op("dve", [t1], lambda e: e.tensor_tensor(d, ps[:, b, :], d, ALU.mult))
                    bank_t[b] = [t2]
                    t_gg.append(op("dve", [t2, t_bc], lambda e:
                                   e.tensor_tensor(d, d, bc[:, 512 * n - 1024:512 * n - 512], ALU.mult)))
            fill += a_pieces("hgrn_w_in", 2048 + 512 * n, 512, 8, 4, act, banks, t_a2, end, by_chunk=True)

        rd_t = [[], []]
        up_t = [t_hd[0] + t_hd[1] + t_hd[2] + t_hd[3], t_hd[4] + t_hd[5] + t_hd[6] + t_hd[7]]
        ac_t = [[t_z], [t_z]]
        e_t = [[], []]
        cur = [[E0[:, 1024 * g:1024 * g + 1024] for g in range(2)], [E1[:, 512 * g:512 * g + 512] for g in range(2)]]

        def level(g):
            b0 = 4 + 2 * g

            def go(eng):
                for h in range(4):
                    for blk in range(2):
                        s = TOK[blk]
                        c = 256 * (h % 2) + 128 * blk
                        last = eng.matmul(ps[:, b0 + h // 2, c:c + 128], K[:, 4 * g + h, s], Q[:, 4 * g + h, s],
                                          start=True, stop=True)
                return last
            t = op("pe", up_t[g] + bank_t[b0] + bank_t[b0 + 1], go)
            rd_t[g] = [t]

        def gather(g, lev):
            b0 = 4 + 2 * g
            d = AC[:, 4 * g:4 * g + 4, :].rearrange("p h (b t) -> p (h b) t", t=128)
            m = hmask[:, lev, :].unsqueeze(1).to_broadcast([128, 8, 128])
            src = ps[:, b0:b0 + 2, :].rearrange("p b (c t) -> p (b c) t", t=128)
            tc = op("dve", rd_t[g] + ac_t[g], lambda e: e.copy_predicated(d, m, src))
            bank_t[b0] = bank_t[b0 + 1] = [tc]
            ac_t[g] = [tc]

        def grow(g, hs):
            if hs == 0:
                qg, eg = Q[:, 4 * g:4 * g + 4, :], E[:, 4 * g:4 * g + 4, :]
                t = op("dve", rd_t[g] + up_t[g], lambda e: e.tensor_tensor(qg, qg, eg, ALU.mult))
                up_t[g] = up_t[g] + [t]
                return
            n = 1024 // (2 * hs)
            e2 = cur[0][g][:, 0:2 * n].rearrange("p (n w) -> p n w", w=2)
            q2 = FF[:, 1024 * g:1024 * g + 1024].rearrange("p (n w s) -> p n w s", w=2, s=hs)[:, :, 1, :]
            k2 = FF[:, 2048 + 1024 * g:3072 + 1024 * g].rearrange("p (n w s) -> p n w s", w=2, s=hs)[:, :, 0, :]
            f0 = e2[:, :, 0:1].to_broadcast([128, n, hs])
            f1 = e2[:, :, 1:2].to_broadcast([128, n, hs])
            nx = cur[1][g][:, 0:n]
            t1 = op("dve", rd_t[g] + up_t[g] + e_t[g], lambda e: e.tensor_tensor(q2, q2, f0, ALU.mult))
            t2 = op("pool", rd_t[g] + up_t[g] + e_t[g], lambda e: e.tensor_tensor(k2, k2, f1, ALU.mult))
            if hs < 64:
                e_t[g] = [op("pool", up_t[g] + e_t[g], lambda e:
                             e.tensor_tensor(nx, e2[:, :, 0], e2[:, :, 1], ALU.mult))]
            up_t[g] = [t1, t2]

        hs = 0
        for lev in range(8):
            for g in range(2):
                level(g)
                if fill:
                    fill.pop(0)()
                grow(g, hs)
                gather(g, lev)
            if hs:
                cur.reverse()
            hs = max(1, 2 * hs)
        t_xc = []
        for g in range(2):
            b0 = 4 + 2 * g

            def go(eng, g=g, b0=b0):
                for h in range(4):
                    last = eng.matmul(ps[:, b0, 128 * h:128 * h + 128], K[:, 4 * g + h, 0:128], Q[:, 4 * g + h, 128:256],
                                      start=True, stop=True)
                return last
            t = op("pe", up_t[g] + bank_t[b0], go)
            d = XC[:, 4 * g:4 * g + 4, :].rearrange("p h t -> p (h t)")
            te = op("act", [t], lambda e, d=d, b0=b0: e.activation(d, ps[:, b0, :], ACT.Copy))
            bank_t[b0] = [te]
            t_xc.append(te)
        t_oh = []
        for tok in range(2):
            for g in range(2):
                def go(eng, tok=tok, g=g):
                    for h in range(4 * g, 4 * g + 4):
                        o = ps[:, 2 * tok + g, 128 * (h % 4):128 * (h % 4) + 128]
                        c = slice(128 * h, 128 * h + 128)
                        if tok:
                            eng.matmul(o, XC[:, h, :], V[:, 0, c], start=True, stop=False)
                        last = eng.matmul(o, AC[:, h, TOK[tok]], V[:, tok, c], start=not tok, stop=True)
                    return last
                t_oh.append(op("pe", (t_xc if tok else []) + ac_t[g] + t_v + bank_t[2 * tok + g], go))
        t_mt = []
        for tok in range(2):
            y = ps[:, 2 * tok:2 * tok + 2, :]
            d = xn[:, tok, :].rearrange("p (b n) -> p b n", b=2)
            t1 = op("act", [t_oh[2 * tok + 1]], lambda e, y=y, d=d: e.activation(d, y, ACT.Square))
            ss = stats(8)
            t2 = op("dve", [t1], lambda e, tok=tok, ss=ss:
                    e.tensor_reduce(ss, xn[:, tok, :].rearrange("p (h n) -> p h n", h=8), AX, ALU.add))
            rs, tp = power(ss, 8, 1.0 / 128, [t2])
            t3 = op("dve", t_gg + [t2], lambda e, y=y, d=d, tok=tok:
                    e.tensor_tensor(d, y, G[:, tok, :].rearrange("p (b n) -> p b n", b=2), ALU.mult))
            bank_t[2 * tok] = bank_t[2 * tok + 1] = [t3]
            v = xn[:, tok, :].rearrange("p (h n) -> p h n", h=8)
            halves = [[op("dve", [t3, tp], lambda e, v=v, rs=rs, c=c:
                          e.tensor_tensor(v[:, c:c + 4, :], v[:, c:c + 4, :],
                                          rs[:, c:c + 4].unsqueeze(2).to_broadcast([128, 4, 128]), ALU.mult))]
                      for c in (0, 4)]
            t_mt.append(flip_tok(lambda k, tok=tok: xn[:, tok, 128 * k:128 * k + 128], 8,
                                 (4 + 2 * tok, 5 + 2 * tok), act, tok, halves, []))
        bc2_t[0] = bc2_t[0] + t_mt[1]
        t_y = project("hgrn_w_out", t_mt)

        def swiglu(layer, row, t_y, post_row=None):
            def pair(f):
                return [(f"ffn_in{layer}", f), (f"ffn_in{layer}", 22 + f)]

            def outs(f):
                b = 4 + f % 4
                return [ps[:, b, 0:256], ps[:, b, 256:512]]
            turns = []
            o = outs(0) + outs(1)
            t_a, post_t = between(t_y, None, row, post_row, f"ffn_first{layer}", 0,
                                  turned([o[0], o[2], o[1], o[3]], (4, 5), turns))
            t_a = t_a[0] + t_a[1]

            def up(j):
                if j == 0:
                    s_mm(pair(2), act, outs(2), t_a + bank_t[6])
                    return [turn() for turn in turns][1]
                for f in (2 * j, 2 * j + 1):
                    if f > 2:
                        t = s_mm(pair(f), act, outs(f), t_a + bank_t[4 + f % 4])
                return t

            def post(j, tu, free, before):
                b = 4 + 2 * (j % 2)
                gv, uv = ps[:, b:b + 2, 0:256], ps[:, b:b + 2, 256:512]
                s, q = htmp[j % 2][:, 0], htmp[j % 2][:, 1]
                hi, lo = hid[j % 2]
                t1 = op("act", [tu] + before, lambda e: e.activation(s, gv, ACT.Sigmoid))
                t2 = op("dve", [t1], lambda e: e.tensor_tensor(s, gv, s, ALU.mult))
                t3 = op("dve", [t2], lambda e: e.tensor_tensor(q, uv, s, ALU.mult))
                bank_t[b] = bank_t[b + 1] = [t3]
                t4 = op("act", [t3] + free, lambda e: e.activation(hi, q, ACT.Copy))
                t5 = op("dve", [t4], lambda e: e.tensor_tensor(lo, q, hi.bitcast(F32), ALU.subtract))
                return [t4, t5]
            return mlp(f"ffn_out{layer}", 11, up, post), post_t

        t_y, _ = swiglu(0, R_FFN0, t_y)

        l_pair = lambda f: [("lru_w_in", f), ("lru_w_in", 8 + f)]
        l_bank = lambda f: (0 if f // 2 == 1 else 4) + f % 2
        l_outs = lambda f: [ps[:, l_bank(f), 0:256], ps[:, l_bank(f), 256:512]]
        turns = []
        o = l_outs(0) + l_outs(1)
        t_a, _ = between(t_y, None, R_MIX1, None, "lru_first", 0, turned([o[0], o[2], o[1], o[3]], (4, 5), turns))
        t_a = t_a[0] + t_a[1]

        def buf(off, width, parts=2):
            return [FF[:, off + parts * width * i:off + parts * width * (i + 1)].rearrange("p (f t) -> p f t", f=2)
                    for i in range(2)]
        Y, U, UC = buf(0, 256), buf(1024, 260), buf(2064, 256)
        RG, IG, VV, SQ, AA = buf(3088, 256), buf(4112, 256), buf(5136, 256), buf(6160, 256), buf(7184, 256)
        WW = buf(8208, 256)
        uP = [tuple(RR[:, (2 * j + i) * 512:(2 * j + i + 1) * 512].rearrange("p (f t) -> p f t", f=2)
                    for i in range(2)) for j in range(2)]
        hP = [tuple(RR[:, 2048 + (2 * j + i) * 512:2048 + (2 * j + i + 1) * 512].rearrange("p (f t) -> p f t", f=2)
                    for i in range(2)) for j in range(2)]
        t_p = [op("pool", t_y, lambda e, i=i: e.memset(U[i][:, :, 0:3], 0.0)) for i in range(2)]
        unit = {}

        def lru_in(n):
            if n:
                for f in (2 * n, 2 * n + 1):
                    if f > 2:
                        t = s_mm(l_pair(f), act, l_outs(f), t_a + bank_t[l_bank(f)])
            else:
                s_mm(l_pair(2), act, l_outs(2), t_a + bank_t[l_bank(2)])
                t = [turn() for turn in turns][1]
            i, b = n % 2, l_bank(2 * n)
            old = unit[n - 2] if n >= 2 else {"end": [], "gate": []}
            t1 = op("act", [t] + t_y + old["end"], lambda e:
                    e.activation(Y[i], ps[:, b:b + 2, 0:256], ACT.Gelu_apprx_tanh))
            t2 = op("act", [t] + old["end"], lambda e: e.activation(U[i][:, :, 3:259], ps[:, b:b + 2, 256:512], ACT.Copy))
            bank_t[b] = bank_t[b + 1] = [t2]
            ends = []
            for c in range(2):
                f = 2 * n + c
                t3 = op("dve", [t2, t_p[i], t_in], lambda e, c=c, f=f:
                        e.tensor_scalar(UC[i][:, c, :], U[i][:, c, 0:256], cols[:, C_CONVW + f:C_CONVW + f + 1],
                                        cols[:, C_CONVB + f:C_CONVB + f + 1], ALU.mult, ALU.add))
                for tap in range(1, 4):
                    w = C_CONVW + 8 * tap + f
                    t3 = op("dve", [t3], lambda e, c=c, tap=tap, w=w:
                            e.scalar_tensor_tensor(UC[i][:, c, :], U[i][:, c, tap:tap + 256], cols[:, w:w + 1],
                                                   UC[i][:, c, :], ALU.mult, ALU.add))
                ends.append(t3)
            hi, lo = uP[i]
            th = op("act", ends + old["gate"], lambda e: e.activation(hi, UC[i], ACT.Copy))
            tl = op("dve", [th], lambda e: e.tensor_tensor(lo, UC[i], hi.bitcast(F32), ALU.subtract))
            unit[n] = {"y": t1, "u": [th, tl]}

        def lru_gate(n):
            i = n % 2
            h, l, wt = take(("g", n))
            hi, lo = uP[i]

            def go(eng):
                for m in range(2):
                    for fo in range(2):
                        for k in range(2):
                            w0 = (2 * m + k) * 256 + 128 * fo
                            w = slice(w0, w0 + 128)
                            last = mm3(eng, ps[:, 6 + m, 256 * fo:256 * fo + 256], (h[:, w], l[:, w]),
                                       (hi[:, k, :], lo[:, k, :]), k == 0, k == 1)
                return last
            t = op("pe", wt + unit[n]["u"] + bank_t[6] + bank_t[7], go)
            done_t.append(t)
            unit[n]["gate"] = [t]
            for m, (dst, col) in enumerate(((RG, C_BA), (IG, C_BX))):
                for fo in range(2):
                    f = 2 * n + fo
                    te = op("act", [t], lambda e, dst=dst, col=col, f=f, fo=fo, bb=6 + m:
                            e.activation(dst[i][:, fo, :], ps[:, bb, 256 * fo:256 * fo + 256], ACT.Sigmoid,
                                         bias=cols[:, col + f:col + f + 1]))
                bank_t[6 + m] = [te]
            for fo in range(2):
                tv = op("act", [te, t_c4], lambda e, fo=fo, f=2 * n + fo:
                        e.activation(VV[i][:, fo, :], RG[i][:, fo, :], ACT.Tanh, scale=c4[:, f:f + 1]))
            for fo in range(2):
                ta = op("act", [te], lambda e, fo=fo, f=2 * n + fo:
                        e.activation(AA[i][:, fo, :], RG[i][:, fo, :], ACT.Exp, scale=c8[:, f:f + 1]))
            ts = op("act", [tv], lambda e: e.activation(SQ[i], VV[i], ACT.Sqrt))
            flat = lambda x: x.rearrange("p f t -> p (f t)")
            t1 = op("dve", [te], lambda e: e.tensor_tensor(IG[i], IG[i], UC[i], ALU.mult))
            t2 = op("dve", [ta, tv], lambda e: e.scalar_tensor_tensor(
                flat(RG[i]), flat(AA[i]), 1.0, flat(VV[i]), ALU.add, ALU.mult))
            t3 = op("dve", [t2], lambda e: e.tensor_scalar(RG[i], RG[i], -1.0, 1.0, ALU.mult, ALU.add))
            t4 = op("dve", [ts], lambda e: e.scalar_tensor_tensor(
                flat(SQ[i]), flat(AA[i]), 1.0, flat(SQ[i]), ALU.add, ALU.mult))
            t5 = op("dve", [t4, t1], lambda e: e.tensor_tensor(SQ[i], SQ[i], IG[i], ALU.mult))
            for fo in range(2):
                t6 = op("dve", [t5, t3], lambda e, fo=fo: e.tensor_tensor_scan(
                    WW[i][:, fo, :], RG[i][:, fo, :], SQ[i][:, fo, :], 0.0, ALU.mult, ALU.add))
            t7 = op("dve", [t6, unit[n]["y"]], lambda e: e.tensor_tensor(WW[i], WW[i], Y[i], ALU.mult))
            unit[n]["w"] = t7
            unit[n]["end"] = [t7]

        def lru_hidden(n):
            i, t7 = n % 2, unit[n]["w"]
            ho, lw_ = hP[i]
            free = unit[n - 2]["down"] if n >= 2 else []
            t8 = op("act", [t7] + free, lambda e: e.activation(ho, WW[i], ACT.Copy))
            t9 = op("dve", [t8], lambda e: e.tensor_tensor(lw_, WW[i], ho.bitcast(F32), ALU.subtract))
            unit[n]["end"] = [t8, t9]

        def lru_down(n):
            part = take(("d", "lru_w_out", n))
            out = [d_part(part, tok, hP[n % 2], 0, n == 0, n == 3, unit[n]["end"]) for tok in range(2)]
            done_t.append(out[1])
            unit[n]["down"] = [out[1]]
            return out

        for step in range(5):
            if step < 4:
                lru_in(step)
            if step >= 2:
                lru_hidden(step - 2)
            if step >= 1:
                lru_gate(step - 1)
            if step >= 3:
                t_y = lru_down(step - 3)
        lru_hidden(3)
        for n in (2, 3):
            t_y = lru_down(n)
        t_y, t_b = swiglu(1, R_FFN1, t_y, R_FINAL)

        for tok in range(2):
            t = residual(tok, t_y[tok], None)
            halves = norm_tok(tok, xr[:, tok, :], 1024, xn[:, tok, :], bc[:, :], t_b, [t])
            for c in range(2):
                t_out = dma("out", halves[c], out_d[128 * tok:128 * tok + 128, 512 * c:512 * c + 512],
                            xn[:, tok, 512 * c:512 * c + 512])
        wait("sp", [t_out])
        assert len(done_t) == len(chunks)

        block = ctx.enter_context(nc.Block())

        @block.sync
        def _(eng):
            for f in queue["sp"]:
                f(eng)

        @block.gpsimd
        def _(eng):
            for f in queue["pool"]:
                f(eng)

        @block.scalar
        def _(eng):
            for f in queue["act"]:
                f(eng)

        @block.vector
        def _(eng):
            for f in queue["dve"]:
                f(eng)

        @block.tensor
        def _(eng):
            for f in queue["pe"]:
                f(eng)


def kernel(**inputs):
    import concourse.bacc as bacc
    from concourse.bass_utils import run_bass_kernel_spmd

    a = {k: np.asarray(v) for k, v in inputs.items()}
    w = {
        "w_in": a["w_in"][0], "w_uq": a["w_uq"][0], "w_ukv": a["w_ukv"][0],
        "w_branch_a": a["w_branch_a"][0], "w_branch_b": a["w_branch_b"][0], "w_out": a["w_out"][0],
        "w_up": a["w_up"][0], "w_down": a["w_down"][0],
        "hgrn_w_in": a["hgrn_w_in_2"][0], "hgrn_w_out": a["hgrn_w_out_2"][0],
        "lru_w_in": a["lru_w_in_2"][0], "lru_w_out": a["lru_w_out_2"][0],
        "w_ukv_v": a["w_ukv"][0].reshape(256, 8, 128)[:, :, 64:].reshape(256, 512),
        "ffn_first0": np.concatenate([a["ffn_w_in_2"][0][:, c:c + 256] for c in (0, 2816)], axis=1),
        "ffn_first1": np.concatenate([a["ffn_w_in_2"][1][:, c:c + 256] for c in (0, 2816)], axis=1),
        "lru_first": np.concatenate([a["lru_w_in_2"][0][:, c:c + 256] for c in (0, 1024)], axis=1),
        "lru_wa": a["lru_wa_2"][0], "lru_wx": a["lru_wx_2"][0],
        "ffn_in0": a["ffn_w_in_2"][0], "ffn_in1": a["ffn_w_in_2"][1],
        "ffn_out0": a["ffn_w_out_2"][0], "ffn_out1": a["ffn_w_out_2"][1],
    }
    stream = np.concatenate([np.ascontiguousarray(lay_chunk(w, key)).reshape(-1) for key, _ in chunk_list()])

    def col(v):
        return v.reshape(-1, 128).T

    cols = np.ascontiguousarray(np.concatenate(
        [col(a["hgrn_lb_2"][0]), col(a["hgrn_lb_2"][1]), col(a["lru_conv_b_2"][0]), col(a["lru_ba_2"][0]),
         col(a["lru_bx_2"][0]), col(a["lru_lambda_2"][0])] + [col(a["lru_conv_w_2"][0][t]) for t in range(4)], axis=1))
    rows = np.concatenate([
        a["g_pre_mix"][0], a["g_post_mix"][0], a["g_pre_mlp"][0], a["g_post_mlp"][0],
        a["norm_mix_2"][0], a["norm_mix_2"][1], a["norm_ffn_2"][0], a["norm_ffn_2"][1], a["norm_final_2"],
        a["b_gate"][0], np.tile(a["hgrn_norm_2"][0], 8), a["g_q_norm"][0], a["g_kv_norm"][0]])

    def inv_freq(r):
        return np.power(np.float32(500000.0), -np.arange(r // 2, dtype=np.float32) * np.float32(2.0 / r))

    const = np.zeros((128, 1560), np.float32)
    const[:, 0:128] = np.eye(128)
    tri = np.where(np.arange(128)[None, :] <= np.arange(128)[:, None], 0.0, -1e38)
    const[:, 128:256] = tri
    const[:, 384:512] = tri
    const[:, 512:520] = inv_freq(16)
    const[:, 520:536] = inv_freq(32)
    s, t = np.arange(128)[:, None], np.arange(128)[None, :]
    mask = np.zeros((128, 8, 128), np.float32)
    mask[:, 0] = s == t
    for n in range(7):
        h = 1 << n
        mask[:, n + 1] = ((t // h) % 2 == 1) & (s // h == t // h - 1)

    const[:, 536:] = mask.reshape(128, 1024)

    arrays = {
        "x_in": np.ascontiguousarray(a["x"][0]),
        "pos_in": np.ascontiguousarray(a["positions"].reshape(2, 128).T.astype(np.int32)),
        "w_stream": stream, "cols_in": cols, "rows_in": rows, "const_in": const,
    }
    nc = bacc.Bacc("TRN2", target_bir_lowering=False, num_devices=1)
    args = [nc.dram_tensor(k, v.shape, mybir.dt.from_np(v.dtype), kind="ExternalInput").ap()
            for k, v in arrays.items()]
    args.append(nc.dram_tensor("out_0", (256, 1024), F32, kind="ExternalOutput").ap())
    program(nc, *args)
    r = run_bass_kernel_spmd(nc, [arrays], core_ids=[0])
    return r.results[0]["out_0"].reshape(1, 256, 1024)
```

```python
import numpy as np
import concourse.bass as bass
from concourse import mybir
from contextlib import ExitStack

F32 = mybir.dt.float32
F32R = mybir.dt.float32r
I32 = mybir.dt.int32
U8 = mybir.dt.uint8
ALU = mybir.AluOpType
ACT = mybir.ActivationFunctionType
AX = mybir.AxisListType.X

EPS = 1e-6
TWO_PI = 2.0 * np.pi
PI_1 = 6.28125
PI_2 = 0.00193500518798828125
PI_3 = float(TWO_PI - PI_1 - PI_2)
MAGIC = 12582912.0

C_LB0, C_LB1, C_CONVB, C_BA, C_BX, C_LAM, C_CONVW, C_N = 0, 8, 16, 24, 32, 40, 48, 80
R_PRE_MIX, R_POST_MIX, R_PRE_MLP, R_POST_MLP = 0, 1024, 2048, 3072
R_MIX0, R_MIX1, R_FFN0, R_FFN1, R_FINAL = 4096, 5120, 6144, 7168, 8192
R_BGATE, R_HNORM, R_QN, R_KVN, R_N = 9216, 11264, 12288, 12672, 12928


def chunk_list():
    out = []

    def a_type(name, col, width, kt, group):
        for k in range(0, kt, group):
            out.append((("a", name, col, width, k, min(group, kt - k)), width * min(group, kt - k)))

    def s_type(pairs, kt):
        out.append((("s", tuple(pairs), kt), 128 * kt * len(pairs)))

    def rows(name, n):
        for j in range(n):
            out.append((("d", name, j), 2048))

    for col, width in ((1536, 384), (1920, 288), (0, 512), (512, 512)):
        a_type("w_in", col, width, 8, 4)
    s_type([("w_ukv", h) for h in range(8)], 2)
    a_type("w_ukv_v", 0, 512, 2, 2)
    a_type("w_uq", 0, 384, 3, 3)
    a_type("w_uq", 384, 384, 3, 3)
    a_type("w_in", 1024, 512, 8, 4)
    for n in range(4):
        a_type("w_in", 2208 + 512 * n, 512, 8, 4)
    for n in range(2):
        a_type("w_branch_a", 512 * n, 512, 4, 4)
        a_type("w_branch_b", 512 * n, 512, 4, 4)
    rows("w_out", 4)

    def mlp(up, down, units, first, whole):
        a_type(first, 0, 512, 8, 4)
        lead = 2 if whole == 2 else 0
        for j in range(units + 1):
            if whole <= j + lead < units:
                for u in up(j + lead):
                    s_type(u, 8)
            if 0 < j < units - 3:
                out.append((("d", down, j - 1), 2048))
        for j in range(units - 4, units):
            out.append((("d", down, j), 2048))

    mlp(lambda j: [[("w_up", 2 * j), ("w_up", 2 * j + 1)]], "w_down", 16, "w_up", 2)
    a_type("hgrn_w_in", 2048, 512, 8, 4)
    for h in range(8):
        s_type([("hgrn_w_in", h), ("hgrn_w_in", 8 + h)], 8)
    for n in range(1, 4):
        a_type("hgrn_w_in", 2048 + 512 * n, 512, 8, 4)
    rows("hgrn_w_out", 4)
    mlp(lambda j: [[("ffn_in0", f), ("ffn_in0", 22 + f)] for f in (2 * j, 2 * j + 1)], "ffn_out0", 11, "ffn_first0", 1)
    a_type("lru_first", 0, 512, 8, 4)
    for kind, n in (("s", 2), ("s", 3), ("s", 4), ("g", 0), ("s", 5), ("g", 1), ("s", 6), ("s", 7), ("g", 2),
                    ("d", 0), ("g", 3), ("d", 1), ("d", 2), ("d", 3)):
        if kind == "s":
            s_type([("lru_w_in", n), ("lru_w_in", 8 + n)], 8)
        elif kind == "g":
            out.append((("g", n), 1024))
        else:
            out.append((("d", "lru_w_out", n), 2048))
    mlp(lambda j: [[("ffn_in1", f), ("ffn_in1", 22 + f)] for f in (2 * j, 2 * j + 1)], "ffn_out1", 11, "ffn_first1", 1)
    return out


def lay_chunk(w, key):
    if key[0] == "a":
        _, name, col, width, k, n = key
        return w[name][128 * k:128 * (k + n), col:col + width].reshape(n, 128, width).transpose(1, 0, 2)
    if key[0] == "s":
        _, pairs, kt = key
        return np.concatenate([w[name][:, 128 * f:128 * f + 128].reshape(kt, 128, 128).transpose(1, 0, 2)
                               for name, f in pairs], axis=1)
    if key[0] == "d":
        _, name, j = key
        return w[name][256 * j:256 * j + 256].reshape(2, 128, 1024).transpose(1, 0, 2)
    return np.concatenate([w[name][key[1]].reshape(2, 128, 256).transpose(1, 0, 2)
                           for name in ("lru_wa", "lru_wx")], axis=1)


def program(nc, x_d, pos_d, w_d, cols_d, rows_d, const_d, out_d):
    NRAW, NHL = 3, 4
    ENG = ("pe", "act", "dve", "pool", "sp")
    chunks = chunk_list()
    offs = np.concatenate([[0], np.cumsum([128 * wd for _, wd in chunks])]).tolist()

    ctx = ExitStack()
    with ctx:
        def sb(name, shape, dt=F32):
            return ctx.enter_context(nc.sbuf_tensor(name, shape, dt))

        raw = sb("raw", [128, NRAW, 2048])
        wH = sb("wH", [128, NHL, 2048], F32R)
        wL = sb("wL", [128, NHL, 2048], F32R)
        xr = sb("xr", [128, 2, 1024])
        xn = sb("xn", [128, 2, 1024])
        aH = sb("aH", [128, 8, 256], F32R)
        aL = sb("aL", [128, 8, 256], F32R)
        RR = sb("RR", [128, 4608], F32R)
        bc = sb("bc", [128, 1024])
        ident = sb("ident", [128, 128])
        amask = sb("amask", [128, 384])
        hmask = sb("hmask", [128, 8, 128], U8)
        cols = sb("cols", [128, C_N])
        st = sb("st", [128, 256])
        consts = sb("consts", [128, 32])
        FF = sb("FF", [128, 14848])
        ps = ctx.enter_context(nc.psum_tensor("ps", [128, 8, 512], F32))

        sems = {e: ctx.enter_context(nc.semaphore(f"s_{e}")) for e in ENG}
        for n in range(NRAW):
            sems[f"raw{n}"] = ctx.enter_context(nc.semaphore(f"s_raw{n}"))
        for n in ("x0", "x1", "id", "in", "bc", "bg", "out"):
            sems[n] = ctx.enter_context(nc.semaphore(f"s_{n}"))
        queue = {e: [] for e in ENG}
        count = {s: 0 for s in sems}
        seen = {e: {} for e in ENG}

        def wait(e, after):
            for t in after:
                if t is None:
                    continue
                s, v = t
                if seen[e].get(s, 0) < v:
                    seen[e][s] = v
                    queue[e].append(lambda eng, s=s, v=v: eng.wait_ge(sems[s], v))

        def op(e, after, fn):
            wait(e, after)
            queue[e].append(lambda eng: fn(eng).then_inc(sems[e], 1))
            count[e] += 1
            return (e, count[e])

        def dma(sem, after, dst, src, e="sp"):
            wait(e, after)
            queue[e].append(lambda eng: eng.dma_start(dst, src).then_inc(sems[sem], 16))
            count[sem] += 16
            return (sem, count[sem])

        dma_t, split_t, done_t = [], [], []

        def load_chunk(i):
            wd = chunks[i][1]
            free = split_t[i - NRAW] if i >= NRAW else []
            src = w_d[offs[i]:offs[i + 1]].rearrange("(p n) -> p n", p=128)
            dma_t.append(dma(f"raw{i % NRAW}", free, raw[:, i % NRAW, 0:wd], src))

        def split_chunk(i):
            wd = chunks[i][1]
            free = [done_t[i - NHL]] if i >= NHL else []
            r, h, l = raw[:, i % NRAW, 0:wd], wH[:, i % NHL, 0:wd], wL[:, i % NHL, 0:wd]
            th = op("act", free + [dma_t[i]], lambda e: e.activation(h, r, ACT.Copy))
            tl = op("dve", free + [dma_t[i], th],
                    lambda e: e.tensor_tensor(l, r, h.bitcast(F32), ALU.subtract))
            split_t.append([th, tl])

        taken = [0]

        def pump(upto=len(chunks)):
            while len(split_t) < upto and len(split_t) - NHL < len(done_t):
                while len(dma_t) < min(len(chunks), len(split_t) + NRAW):
                    load_chunk(len(dma_t))
                split_chunk(len(split_t))
            while len(dma_t) < min(len(chunks), len(split_t) + NRAW):
                load_chunk(len(dma_t))

        def take(key, ahead=True, upto=len(chunks)):
            i = taken[0]
            taken[0] += 1
            assert chunks[i][0] == key, (chunks[i][0], key)
            if ahead or i >= len(split_t):
                pump(upto)
            return wH[:, i % NHL, :], wL[:, i % NHL, :], split_t[i]

        def mm3(eng, out, lhs, rhs, start, stop):
            eng.matmul(out, lhs[0], rhs[1], start=start, stop=False)
            eng.matmul(out, lhs[1], rhs[0], start=False, stop=False)
            return eng.matmul(out, lhs[0], rhs[0], start=False, stop=stop)

        bank_t = [[] for _ in range(8)]
        TOK = (slice(0, 128), slice(128, 256))

        def a_pieces(name, col, width, kt, group, lhs, banks, after, end, ahead=True, by_chunk=False,
                     cut=False):
            parts = {}
            out = []
            steps = [(tok, k, 0, min(group, kt - k)) for tok in range(2) for k in range(0, kt, group)]
            if by_chunk:
                steps.sort(key=lambda s: s[1])
            if cut:
                steps[1:2] = [(0, 4, 0, 2), (0, 4, 2, 4)]
            for tok, k, j0, j1 in steps:
                    def piece(tok=tok, k=k, j0=j0, j1=j1, n=min(group, kt - k)):
                        if tok == 0 and j0 == 0:
                            parts[k] = take(("a", name, col, width, k, n), ahead)
                        h, l, ready = parts[k]

                        def go(eng):
                            for j in range(j0, j1):
                                w = slice(j * width, (j + 1) * width)
                                last = mm3(eng, ps[:, banks[tok], 0:width],
                                           (lhs[0][:, k + j, TOK[tok]], lhs[1][:, k + j, TOK[tok]]),
                                           (h[:, w], l[:, w]), k + j == 0, k + j == kt - 1)
                            return last
                        t = op("pe", after[tok] + ready + bank_t[banks[tok]], go)
                        if tok == 1:
                            done_t.append(t)
                        if k + j1 == kt:
                            end(tok, t)
                    out.append(piece)
            return out

        def a_mm(*args):
            for piece in a_pieces(*args):
                piece()

        def s_mm(pairs, rhs, outs, after, kt=8):
            h, l, ready = take(("s", tuple(pairs), kt))

            def go(eng):
                for i, out in enumerate(outs):
                    for k in range(kt):
                        w = slice((kt * i + k) * 128, (kt * i + k + 1) * 128)
                        last = mm3(eng, out, (h[:, w], l[:, w]), (rhs[0][:, k, :], rhs[1][:, k, :]),
                                   k == 0, k == kt - 1)
                return last
            t = op("pe", after + ready, go)
            done_t.append(t)
            return t

        def d_part(part, tok, lhs, f0, first, last, after):
            h, l, ready = part

            def go(eng):
                for f in range(2):
                    for c in range(2):
                        w = slice(1024 * f + 512 * c, 1024 * f + 512 * c + 512)
                        end = mm3(eng, ps[:, 2 * tok + c, :],
                                  (lhs[0][:, f0 + f, TOK[tok]], lhs[1][:, f0 + f, TOK[tok]]),
                                  (h[:, w], l[:, w]), first and f == 0, last and f == 1)
                return end
            return op("pe", ready + after + (bank_t[2 * tok] + bank_t[2 * tok + 1] if first else []), go)

        def d_group(name, js, lhs, f0, first, after, upto=len(chunks), amid=lambda: None):
            parts, t_y = [], []
            n = len(js)
            for c in range(n):
                if c == n - 1:
                    amid()
                parts.append(take(("d", name, js[c]), upto=upto))
                t = d_part(parts[c], 0, lhs[c], f0[c], first and c == 0, c == n - 1, after[c][0])
            t_y.append(t)

            def rest(beside):
                for c in range(n):
                    if c and c == n - 1:
                        beside()
                    t = d_part(parts[c], 1, lhs[c], f0[c], first and c == 0, c == n - 1, after[c][1])
                    done_t.append(t)
                    if c < min(2, n - 1):
                        pump()
                if n == 1:
                    beside()
                t_y.append(t)
            return t_y, rest

        def project(name, after, amid):
            return d_group(name, (0, 1, 2, 3), (act,) * 4, (0, 2, 4, 6), True, (after,) * 4, amid=amid)

        def bcast(off, width, after):
            return dma("bc", after, bc[:, 0:width], rows_d[off:off + width].partition_broadcast(128))

        stat = [0]

        def stats(n):
            stat[0] += n
            assert stat[0] <= 256
            return st[:, stat[0] - n:stat[0]]

        def power(ss, n, inv, after):
            out = stats(n)
            t = op("pool", after, lambda e: e.tensor_scalar(out, ss, inv, EPS, ALU.mult, ALU.add))
            t = op("pool", [t], lambda e: e.tensor_tensor(out, out, consts[:, 0:1].to_broadcast([128, n])
                                                          if n > 1 else consts[:, 0:1], ALU.pow))
            return out, t

        def flip_tok(src, kt, banks, dst, tok, after, free, width=128):
            out = []
            for g, k0 in enumerate(range(0, kt, 4)):
                n = min(4, kt - k0)
                b = banks[g % len(banks)]

                def go(eng, k0=k0, n=n, b=b):
                    for j in range(n):
                        last = eng.transpose(ps[0:width, b, 128 * j:128 * j + 128], src(k0 + j), ident[:, :])
                    return last
                t = op("pe", after[g] + bank_t[b], go)
                pv = ps[0:width, b, 0:128 * n].rearrange("p (k t) -> p k t", t=128)
                h = dst[0][:, k0:k0 + n, TOK[tok]]
                th = op("act", [t] + free, lambda e, h=h, pv=pv: e.activation(h, pv, ACT.Copy))
                bank_t[b] = [th]
                out.append(th)
                if len(dst) == 2:
                    l = dst[1][:, k0:k0 + n, TOK[tok]]
                    tl = op("dve", [th] + free, lambda e, h=h, l=l, pv=pv:
                            e.tensor_tensor(l, pv, h.bitcast(F32), ALU.subtract))
                    bank_t[b] = [th, tl]
                    out.append(tl)
            return out

        def norm_tok(tok, src, width, dst_sb, gain, gain_t, after):
            ss = stats(1)
            t = op("act", after, lambda e: e.activation(dst_sb, src, ACT.Square, accum_out=ss))
            rs, tp = power(ss, 1, 1.0 / width, [t])
            out = []
            half = 512 if width == 1024 else width
            for c in range(0, width, half):
                out.append([op("dve", [tp, gain_t, t], lambda e, c=c: e.scalar_tensor_tensor(
                    dst_sb[:, c:c + half], src[:, c:c + half], rs, gain[:, c:c + half], ALU.mult, ALU.mult))])
            return out

        def copier(out, dst, banks, width, after, engines=("act", "act")):
            def end(tok, t):
                if engines[tok] == "act":
                    t = op("act", [t] + after, lambda e: e.activation(dst(tok), ps[:, banks[tok], 0:width], ACT.Copy))
                else:
                    t = op("dve", [t] + after, lambda e: e.tensor_copy(dst(tok), ps[:, banks[tok], 0:width]))
                bank_t[banks[tok]] = [t]
                out.append(t)
            return end

        xv = x_d.rearrange("(t p) n -> t p n", p=128)
        t_x0 = [dma("x0", [], xr[:, 0, :], xv[0])]
        t_bc = bcast(R_PRE_MIX, 1024, [])
        t_id = dma("id", [], ident[:, :], const_d[:, 0:128])
        load_chunk(0)
        t_x0.append(dma("x1", [], xr[:, 1, :], xv[1]))
        load_chunk(1)
        posi = FF[:, 0:2].bitcast(I32)
        invf = FF[:, 16:40]
        mtmp0 = FF[:, 3072:4096]
        dma("in", [], posi, pos_d)
        dma("in", [], invf, const_d[:, 512:536])
        t_in = dma("in", [], mtmp0, const_d[:, 536:1560])
        load_chunk(2)
        dma("in", [], amask[:, :], const_d[:, 128:512])
        t_in = dma("in", [], cols[:, :], cols_d)
        op("dve", [], lambda e: e.memset(consts[:, 0:1], -0.5))
        t_c = op("dve", [], lambda e: e.memset(consts[:, 1:2], float(np.pi / 2)))
        wait("pool", [t_c])
        op("act", [t_c], lambda e: e.activation(consts[:, 2:3], consts[:, 1:2], ACT.Square))
        act = (aH, aL)

        cq = FF[:, 8384:9152].rearrange("p (t n) -> p t n", t=2)
        t_h, t_xn, t_cq = [], [], []
        first = a_pieces("w_in", 1536, 384, 8, 4, act, (0, 1), t_h,
                         copier(t_cq, lambda tok: cq[:, tok, :], (0, 1), 384, []), cut=True)
        wait("pe", [t_id])
        halves = [None, None]

        def first_norm(tok):
            halves[tok] = norm_tok(tok, xr[:, tok, :], 1024, xn[:, tok, :], bc[:, :], t_bc, [t_x0[tok]])
            t_xn.extend(halves[tok][0] + halves[tok][1])

        def first_flip(tok):
            t_h.append(flip_tok(lambda k: xn[:, tok, 128 * k:128 * k + 128], 8, (4 + 2 * tok, 5 + 2 * tok),
                                act, tok, halves[tok], []))
        first_norm(0)
        first_flip(0)
        split_chunk(0)
        first_norm(1)
        split_chunk(1)
        first[0]()
        first[1]()
        first_flip(1)
        for piece in first[2:]:
            piece()
        t_hh = t_h[0] + t_h[1]
        t_bc = bcast(R_QN, 640, t_xn)
        t_hm = op("dve", [t_in], lambda e: e.tensor_copy(hmask[:, :, :].rearrange("p l t -> p (l t)"), mtmp0))

        posf, ang, nn, rr, ab = (FF[:, 48:50], FF[:, 64:112], FF[:, 128:176], FF[:, 192:240], FF[:, 256:304])
        rope = FF[:, 8256:8352]
        sn, cs = rope[:, 0:48], rope[:, 48:96]
        t = op("dve", [t_in], lambda e: e.tensor_copy(posf, posi))
        for tok in range(2):
            ta = op("dve", [t], lambda e, tok=tok:
                    e.tensor_scalar(ang[:, 24 * tok:24 * tok + 24], invf, posf[:, tok:tok + 1], None, ALU.mult))
        t = op("dve", [ta], lambda e: e.tensor_scalar(nn, ang, 1.0 / TWO_PI, MAGIC, ALU.mult, ALU.add))
        t = op("dve", [t], lambda e: e.tensor_scalar(nn, nn, MAGIC, None, ALU.subtract))
        src = ang
        for part in (PI_1, PI_2, PI_3):
            t = op("dve", [t], lambda e, part=part, src=src:
                   e.scalar_tensor_tensor(rr, nn, -part, src, ALU.mult, ALU.add))
            src = rr
        t = op("dve", [t], lambda e: e.tensor_scalar(rr, rr, 3.1415925, -3.1415925, ALU.min, ALU.max))
        t = op("dve", [t], lambda e: e.scalar_tensor_tensor(ab, rr, -1.0, rr, ALU.mult, ALU.max))
        op("act", [t], lambda e: e.activation(sn, rr, ACT.Sin))
        t_rope = op("act", [t, t_c], lambda e: e.activation(cs, ab, ACT.Sin, scale=-1.0, bias=consts[:, 1:2]))

        def table(x, heads, half, lo):
            v = x.rearrange("p (t f) -> p t f", t=2)[:, :, lo:lo + half]
            return v.unsqueeze(2).to_broadcast([128, 2, heads, half])

        def rotate(v1, v2, heads, half, lo, tmp, after):
            c, s = table(cs, heads, half, lo), table(sn, heads, half, lo)
            n = 2 * heads * half
            a, b = (tmp[:, i * n:(i + 1) * n].rearrange("p (t h f) -> p t h f", t=2, h=heads) for i in range(2))
            t1 = op("dve", after + [t_rope], lambda e: e.tensor_tensor(a, v1, s, ALU.mult))
            t2 = op("dve", [], lambda e: e.tensor_tensor(b, v2, s, ALU.mult))
            t3 = op("dve", [t1, t2], lambda e: e.tensor_tensor(v1, v1, c, ALU.mult))
            t4 = op("dve", [t3], lambda e: e.tensor_tensor(v2, v2, c, ALU.mult))
            t5 = op("dve", [t4], lambda e: e.tensor_tensor(v1, v1, b, ALU.subtract))
            return op("dve", [t5], lambda e: e.tensor_tensor(v2, v2, a, ALU.add))

        va = FF[:, 0:1024].rearrange("p (t n) -> p t n", t=2)
        mqT = FF[:, 1024:2048].rearrange("p (k t) -> p k t", k=4)
        mkT = FF[:, 2048:3072].rearrange("p (k t) -> p k t", k=4)
        vb = FF[:, 3072:4096].rearrange("p (t n) -> p t n", t=2)
        gates = FF[:, 4096:8192].rearrange("p (t n) -> p t n", t=2)
        ckr = FF[:, 9152:9728].rearrange("p (t n) -> p t n", t=2)
        rtmp = FF[:, 9728:10752]
        lkT = FF[0:96, 10752:12800].rearrange("p (h t) -> p h t", h=8)
        lqT = FF[0:96, 12800:14848].rearrange("p (h t) -> p h t", h=8)
        qk = xn

        t_ck, t_q, t_k, t_va, t_lq, t_vb = [], [], [], [], [], []
        a_mm("w_in", 1920, 288, 8, 4, act, (2, 3), t_h, copier(t_ck, lambda tok: ckr[:, tok, :], (2, 3), 288, []))
        cqT = tuple(RR[:, i * 768:(i + 1) * 768].rearrange("p (k t) -> p k t", k=3) for i in range(2))
        ckT = tuple(RR[:, 1536 + i * 512:2048 + i * 512].rearrange("p (k t) -> p k t", k=2) for i in range(2))
        lat_n = []
        for src, width, g0, t_s in ((cq, 384, 0, t_cq), (ckr, 256, 384, t_ck)):
            for tok in range(2):
                ss = stats(1)
                t = op("act", [t_s[tok]], lambda e, tok=tok, ss=ss, src=src, width=width, g0=g0:
                       e.activation(gates[:, tok, g0:g0 + width], src[:, tok, 0:width], ACT.Square, accum_out=ss))
                rs, tp = power(ss, 1, 1.0 / width, [t])
                lat_n.append(op("dve", [tp, t_bc, t], lambda e, tok=tok, rs=rs, src=src, width=width, g0=g0:
                                e.scalar_tensor_tensor(src[:, tok, 0:width], src[:, tok, 0:width], rs,
                                                       bc[:, g0:g0 + width], ALU.mult, ALU.mult)))
        t_bc = bcast(R_POST_MIX, 1024, lat_n)
        a_mm("w_in", 0, 512, 8, 4, act, (0, 1), t_h,
             copier(t_q, lambda tok: qk[:, tok, 0:512], (0, 1), 512, t_hh))
        a_mm("w_in", 512, 512, 8, 4, act, (2, 3), t_h,
             copier(t_k, lambda tok: qk[:, tok, 512:1024], (2, 3), 512, t_hh, ("dve", "dve")))
        qk4 = qk[:, :, :].rearrange("p t (h d) -> p t h d", d=64)
        lat = [[[], []], [[], []]]
        for tok in range(2):
            lat[0][tok] = flip_tok(lambda k, tok=tok: cq[:, tok, 128 * k:128 * k + 128], 3, (4 + tok,), cqT, tok,
                                   [[lat_n[tok]]], [])
            lat[1][tok] = flip_tok(lambda k, tok=tok: ckr[:, tok, 128 * k:128 * k + 128], 2, (6 + tok,), ckT, tok,
                                   [[lat_n[2 + tok]]], [])
        t_rq = rotate(qk4[:, :, :, 0:8], qk4[:, :, :, 8:16], 16, 8, 0, rtmp, t_q + t_k)
        t_kn = s_mm([("w_ukv", h) for h in range(8)], ckT,
                    [ps[:, 4 + h // 2, 256 * (h % 2):256 * (h % 2) + 256] for h in range(8)],
                    lat[1][0] + lat[1][1] + bank_t[4] + bank_t[5] + bank_t[6] + bank_t[7], kt=2)
        t_k2 = []
        for g in range(2):
            t_k2.append(op("act", [t_kn, t_rq], lambda e, g=g: e.activation(
                lkT[0:64, 4 * g:4 * g + 4, :].rearrange("p (b h) t -> p b (h t)", b=2),
                ps[0:64, 4 + 2 * g:6 + 2 * g, :], ACT.Copy)))
            bank_t[4 + 2 * g] = bank_t[5 + 2 * g] = [t_k2[-1]]
        a_mm("w_ukv_v", 0, 512, 2, 2, ckT, (2, 3), lat[1],
             copier(t_vb, lambda tok: vb[:, tok, :], (2, 3), 512, [t_hm]))
        t_mqk = []
        for tok in range(2):
            t_mqk += flip_tok(lambda k, tok=tok: qk[:, tok, 128 * k:128 * k + 128], 4, (4 + tok,), (mqT,), tok,
                              [[t_rq]], [])
            t_mqk += flip_tok(lambda k, tok=tok: qk[:, tok, 512 + 128 * k:640 + 128 * k], 4, (6 + tok,), (mkT,), tok,
                              [[t_rq]], [])
        lq = xn[:, :, 0:768].rearrange("p t (h d) -> p t h d", d=96)
        for n in range(2):
            banks = (2, 3) if n else (0, 1)
            a_mm("w_uq", 384 * n, 384, 3, 3, cqT, banks, lat[0],
                 copier(t_lq, lambda tok, n=n: xn[:, tok, 384 * n:384 * n + 384], banks, 384, t_mqk))
        lat_done = done_t[-1]
        a_mm("w_in", 1024, 512, 8, 4, act, (0, 1), t_h,
             copier(t_va, lambda tok: va[:, tok, :], (0, 1), 512, [t_rope]))
        kr4 = ckr[:, :, 256:288].unsqueeze(2)
        t_rk = rotate(kr4[:, :, :, 0:16], kr4[:, :, :, 16:32], 1, 16, 8, FF[:, 10240:10368], [t_ck[1], t_rq])
        t_rl = rotate(lq[:, :, :, 64:80], lq[:, :, :, 80:96], 8, 16, 8, FF[:, 9728:10752], t_lq + [t_rk])

        def go(eng):
            for tok in range(2):
                last = eng.transpose(ps[0:32, 2, TOK[tok]], ckr[:, tok, 256:288], ident[:, :])
            return last
        t = op("pe", [t_rk] + bank_t[2], go)
        t_k2.append(op("act", [t], lambda e: e.activation(
            lkT[64:96, :, :], ps[0:32, 2, 0:256].unsqueeze(1).to_broadcast([32, 8, 256]), ACT.Copy)))
        bank_t[2] = [t_k2[-1]]
        t_q2 = []
        for tok in range(2):
            t_q2 += flip_tok(lambda h, tok=tok: lq[:, tok, h, :], 8, (4 + 2 * tok, 5 + 2 * tok), (lqT,), tok,
                             [[t_rl], [t_rl]], [], 96)
        bgate = xn[:, :, :].rearrange("p t n -> p (t n)")
        t_bg = dma("bg", t_q2, bgate, rows_d[R_BGATE:R_BGATE + 2048].partition_broadcast(128))

        oT = [tuple(RR[:, (2 * a + i) * 1024:(2 * a + i + 1) * 1024].rearrange("p (k t) -> p k t", k=4)
                    for i in range(2)) for a in range(2)]
        at = FF[:, 8384:10688]
        sm = [at[:, i * 384:(i + 1) * 384] for i in range(3)]
        pT = [at[:, 1152 + i * 384:1536 + i * 384] for i in range(2)]
        sm_t, pT_t = [[], [], []], [[], []]
        at_free = t_q2 + t_k2 + [t_rl]
        head = {}
        t_o = [[], []]
        t_g = [[], []]

        def scores(i):
            b = 4 + i % 2
            h = i % 8
            if i < 8:
                r = slice(64 * (h % 2), 64 * (h % 2) + 64)
                q, k, scale, dep = mqT[r, h // 2, :], mkT[r, h // 2, :], 0.125, t_mqk
            else:
                q, k, scale, dep = lqT[:, h, :], lkT[:, h, :], 96 ** -0.5, t_q2 + t_k2

            def go(eng):
                eng.matmul(ps[:, b, 0:128], q[:, 0:128], k[:, 0:128], start=True, stop=True)
                return eng.matmul(ps[:, b, 128:384], q[:, 128:256], k[:, 0:256], start=True, stop=True)
            t = op("pe", dep + bank_t[b], go)
            j = i % 3
            ts = op("dve", [t] + sm_t[j] + at_free, lambda e:
                    e.scalar_tensor_tensor(sm[j], ps[:, b, 0:384], scale, amask[:, :], ALU.mult, ALU.add))
            bank_t[b] = [ts]
            m = stats(6) if i < 3 else head[i - 3]["m"]
            head[i] = {"m": m}
            op("dve", [ts], lambda e: e.tensor_reduce(m[:, 0:1], sm[j][:, 0:128], AX, ALU.max, negate=True))
            tm = op("dve", [ts], lambda e: e.tensor_reduce(m[:, 1:2], sm[j][:, 128:384], AX, ALU.max, negate=True))
            op("act", [tm], lambda e:
               e.activation(sm[j][:, 0:128], sm[j][:, 0:128], ACT.Exp, bias=m[:, 0:1], accum_out=m[:, 2:3]))
            te = op("act", [], lambda e:
                    e.activation(sm[j][:, 128:384], sm[j][:, 128:384], ACT.Exp, bias=m[:, 1:2], accum_out=m[:, 3:4]))
            head[i]["e"] = te

        def scale_p(i):
            j, m, te = i % 3, head[i]["m"], head[i]["e"]
            tr = op("dve", [te], lambda e: e.reciprocal(m[:, 4:6], m[:, 2:4]))
            op("dve", [tr], lambda e: e.tensor_scalar(sm[j][:, 0:128], sm[j][:, 0:128], m[:, 4:5], None, ALU.mult))
            head[i]["p"] = op("dve", [tr], lambda e:
                              e.tensor_scalar(sm[j][:, 128:384], sm[j][:, 128:384], m[:, 5:6], None, ALU.mult))

        def flip(i):
            j, c, b = i % 3, i % 2, 6 + i % 2

            def go(eng):
                for n in range(3):
                    last = eng.transpose(ps[:, b, 128 * n:128 * n + 128], sm[j][:, 128 * n:128 * n + 128], ident[:, :])
                return last
            t = op("pe", [head[i]["p"]] + bank_t[b], go)
            sm_t[j] = [t]
            te = op("act", [t] + pT_t[c], lambda e: e.activation(pT[c], ps[:, b, 0:384], ACT.Copy))
            bank_t[b] = [te]
            head[i]["pT"] = te

        def mix(i):
            j, h = i % 2, i % 8
            b = (i // 2) % 2
            v = (va if i < 8 else vb)[:, :, 64 * h:64 * h + 64]
            r = slice(64 * (h % 2), 64 * (h % 2) + 64)
            dep = t_va if i < 8 else t_vb

            def go(eng):
                eng.matmul(ps[r, b, 0:128], v[:, 0, :], pT[j][:, 0:128], start=True, stop=True)
                eng.matmul(ps[r, b, 128:256], v[:, 0, :], pT[j][:, 128:256], start=True, stop=False)
                return eng.matmul(ps[r, b, 128:256], v[:, 1, :], pT[j][:, 256:384], start=False, stop=True)
            t = op("pe", [head[i]["pT"]] + dep + (bank_t[b] if h % 2 == 0 else []), go)
            pT_t[j] = [t]
            if h % 2:
                hi, lo = (o[:, h // 2, :] for o in oT[i // 8])
                th = op("act", [t, lat_done], lambda e: e.activation(hi, ps[:, b, 0:256], ACT.Copy))
                tl = op("dve", [th], lambda e: e.tensor_tensor(lo, ps[:, b, 0:256], hi.bitcast(F32), ALU.subtract))
                bank_t[b] = [th, tl]
                t_o[i // 8] += [th, tl]

        fill = []
        for n in range(4):
            def gate(tok, t, n=n):
                d = gates[:, tok, 512 * n:512 * n + 512]
                td = op("dve", [t, t_bg] + lat_n, lambda e: e.tensor_tensor(
                    d, ps[:, 2 + tok, :], bgate[:, 512 * n:512 * n + 512], ALU.add))
                bank_t[2 + tok] = [td]
                t_g[tok].append(td)
            fill += a_pieces("w_in", 2208 + 512 * n, 512, 8, 4, act, (2, 3), t_h, gate, by_chunk=True)
        for i in range(19):
            if i < 16:
                scores(i)
            if 1 <= i < 17:
                scale_p(i - 1)
            if i < 14 or 15 <= i < 17:
                fill.pop(0)()
            if 2 <= i < 18:
                flip(i - 2)
            if i >= 3:
                mix(i - 3)
        for tok in range(2):
            t_g[tok] = [op("act", t_g[tok], lambda e, tok=tok:
                           e.activation(gates[:, tok, :], gates[:, tok, :], ACT.Sigmoid))]

        bc2 = FF[:, 13824:14848]
        gain = [None]

        def load_gain(row, after):
            gain[0] = dma("bg", after, bc2, rows_d[row:row + 1024].partition_broadcast(128))
        load_gain(R_PRE_MLP, t_o[1])

        merged = xn
        t_m = [[], []]
        mtmp = FF[:, 0:1024].rearrange("p (t n) -> p t n", t=2)
        for n in range(2):
            t_a, t_b = [None, None], [None, None]

            def end_a(tok, t):
                t_a[tok] = t

            def end_b(tok, t, n=n):
                d = merged[:, tok, 512 * n:512 * n + 512]
                g = gates[:, tok, :]
                t1 = op("dve", [t_a[tok]] + t_g[0] + t_g[1], lambda e:
                        e.tensor_tensor(d, ps[:, 4 * n + tok, :], g[:, 512 * n:512 * n + 512], ALU.mult))
                t2 = op("dve", [t, t1], lambda e:
                        e.tensor_tensor(mtmp[:, tok, :], ps[:, 4 * n + 2 + tok, :], g[:, 1024 + 512 * n:1536 + 512 * n],
                                        ALU.mult))
                bank_t[4 * n + tok], bank_t[4 * n + 2 + tok] = [t1], [t2]
                t_m[tok].append([op("dve", [t1, t2], lambda e: e.tensor_tensor(d, d, mtmp[:, tok, :], ALU.add))])
            pa = a_pieces("w_branch_a", 512 * n, 512, 4, 4, oT[0], (4 * n, 4 * n + 1), [t_o[0], t_o[0]], end_a)
            pb = a_pieces("w_branch_b", 512 * n, 512, 4, 4, oT[1], (4 * n + 2, 4 * n + 3), [t_o[1], t_o[1]], end_b)
            pa[0]()
            pb[0]()
            pa[1]()
            if n == 0:
                pb[1]()
        t_mt = [[], []]

        def flip_merged(tok):
            t_mt[tok] += flip_tok(lambda k: merged[:, tok, 128 * k:128 * k + 128], 8,
                                  (2 * tok, 2 * tok + 1), act, tok, t_m[tok], [])
        flip_merged(0)
        pb[1]()
        y = project("w_out", t_mt, lambda: flip_merged(1))

        def residual(tok, t, post_t):
            y = ps[:, 2 * tok:2 * tok + 2, :]
            v = xr[:, tok, :].rearrange("p (b n) -> p b n", b=2)
            if post_t is None:
                t = op("dve", [t], lambda e: e.tensor_tensor(v, y, v, ALU.add))
                bank_t[2 * tok] = bank_t[2 * tok + 1] = [t]
                return t
            ss = stats(1)
            d = xn[:, tok, :].rearrange("p (b n) -> p b n", b=2)
            g = bc[:, :].rearrange("p (b n) -> p b n", b=2)
            t1 = op("act", [t], lambda e: e.activation(d, y, ACT.Square, accum_out=ss))
            rs, tp = power(ss, 1, 1.0 / 1024, [t1])
            t = op("dve", [tp, t1, post_t], lambda e: e.scalar_tensor_tensor(d, y, rs, g, ALU.mult, ALU.mult))
            bank_t[2 * tok] = bank_t[2 * tok + 1] = [t]
            post_done.append(t)
            return op("dve", [t], lambda e: e.tensor_tensor(xr[:, tok, :], xr[:, tok, :], xn[:, tok, :], ALU.add))

        post_done = []

        NEXT_GAIN = {R_PRE_MLP: R_MIX0, R_MIX0: R_FFN0, R_FFN0: R_MIX1, R_MIX1: R_FFN1}

        def between(y, post_t, row, post_row, name, col, end):
            t_y, rest = y
            t_a, halves_t = [], []
            pieces = a_pieces(name, col, 512, 8, 4, act, (6, 7), t_a, end, ahead=False, cut=True)
            t_gain = gain[0]
            halves = []

            def norm(tok):
                t = residual(tok, t_y[tok], post_t)
                halves.append(norm_tok(tok, xr[:, tok, :], 1024, xn[:, tok, :], bc2, t_gain, [t]))
                halves_t.extend(halves[tok][0] + halves[tok][1])

            def flip(tok):
                t_a.append(flip_tok(lambda k: xn[:, tok, 128 * k:128 * k + 128], 8,
                                    (4, 5), act, tok, halves[tok], [t_y[tok]]))
            norm(0)
            rest(lambda: flip(0))
            norm(1)
            pieces[0]()
            pieces[1]()
            flip(1)
            pieces[2]()
            pump()
            pieces[3]()
            pieces[4]()
            if row in NEXT_GAIN:
                load_gain(NEXT_GAIN[row], halves_t)
            if post_row is not None:
                post_t = bcast(post_row, 1024, halves_t + post_done)
            return t_a, post_t

        def turned(outs, banks, t_a):
            def end(tok, t):
                d = xn[:, tok, 0:512]
                tc = op("act", [t], lambda e: e.activation(d, ps[:, 6 + tok, :], ACT.Copy))
                bank_t[6 + tok] = [tc]

                def turn():
                    def go(eng):
                        for i, out in enumerate(outs):
                            last = eng.transpose(out[:, TOK[tok]], xn[:, tok, 128 * i:128 * i + 128], ident[:, :])
                        return last
                    return op("pe", [tc] + bank_t[banks[0]] + bank_t[banks[1]], go)
                t_a.append(turn)
            return end


        hid = [tuple(RR[:, (2 * j + i) * 512:(2 * j + i + 1) * 512].rearrange("p (f t) -> p f t", f=2)
                     for i in range(2)) for j in range(4)]
        htmp = [FF[:, j * 1024:j * 1024 + 1024].rearrange("p (a f t) -> p a f t", a=2, f=2) for j in range(2)]

        def mlp(down, n, up, post, beside=lambda: None):
            ready = {}
            free = [[], [], [], []]
            for j in range(n):
                ready[j] = post(j, up(j), free[j % 4], ready.get(j - 2, []))
                if j == 3:
                    beside()
                if 0 < j < n - 3:
                    part = take(("d", down, j - 1))
                    for tok in range(2):
                        t = d_part(part, tok, hid[(j - 1) % 4], 0, j == 1, False, ready[j - 1])
                    done_t.append(t)
                    free[(j - 1) % 4] = [t]
            js = range(n - 4, n)
            return d_group(down, js, [hid[j % 4] for j in js], (0,) * 4, False, [(ready[j], ready[j]) for j in js])

        lbt, ct = stats(40), stats(48)
        mx, e0, e1, lb, om = (lbt[:, 8 * i:8 * i + 8] for i in range(5))
        nl, z, w1, lw, c4, c8 = (ct[:, 8 * i:8 * i + 8] for i in range(6))
        t_bound = []

        def lower_bounds():
            l0, l1 = cols[:, C_LB0:C_LB0 + 8], cols[:, C_LB1:C_LB1 + 8]
            t1 = op("dve", [t_in], lambda e: e.tensor_tensor(mx, l0, l1, ALU.max))
            t2 = op("dve", [t1], lambda e: e.tensor_tensor(e0, l0, mx, ALU.subtract))
            t3 = op("dve", [t1], lambda e: e.tensor_tensor(e1, l1, mx, ALU.subtract))
            e01 = lbt[:, 8:24]
            t4 = op("act", [t2, t3], lambda e: e.activation(e01, e01, ACT.Exp))
            t5 = op("dve", [t4], lambda e: e.tensor_tensor(mx, e0, e1, ALU.add))
            t6 = op("dve", [t5], lambda e: e.reciprocal(mx, mx))
            t7 = op("dve", [t6], lambda e: e.tensor_tensor(lb, e0, mx, ALU.mult))
            t_bound.append(op("dve", [t7], lambda e: e.tensor_tensor(om, e1, mx, ALU.mult)))
            lam = cols[:, C_LAM:C_LAM + 8]
            t = op("dve", [t_in], lambda e: e.scalar_tensor_tensor(nl, lam, -1.0, lam, ALU.mult, ALU.min))
            t = op("act", [t], lambda e: e.activation(z, nl, ACT.Exp))
            t = op("dve", [t], lambda e: e.tensor_scalar(w1, z, 1.0, None, ALU.add))
            t = op("act", [t], lambda e: e.activation(lw, w1, ACT.Ln))
            t = op("dve", [t], lambda e: e.tensor_scalar(w1, w1, 1.0, 1e-30, ALU.subtract, ALU.max))
            t = op("dve", [t], lambda e: e.tensor_scalar(nl, lam, -1.0, 0.0, ALU.mult, ALU.max))
            t = op("dve", [t], lambda e: e.reciprocal(c4, w1))
            t = op("dve", [t], lambda e: e.tensor_tensor(c4, c4, z, ALU.mult))
            t = op("dve", [t], lambda e: e.tensor_tensor(c4, c4, lw, ALU.mult))
            t = op("dve", [t], lambda e: e.tensor_scalar(w1, w1, 1e-30, None, ALU.is_le))
            t = op("dve", [t], lambda e: e.tensor_tensor(w1, w1, z, ALU.mult))
            t = op("dve", [t], lambda e: e.tensor_tensor(c4, c4, w1, ALU.add))
            t = op("dve", [t], lambda e: e.tensor_tensor(c4, c4, nl, ALU.add))
            t = op("dve", [t], lambda e: e.tensor_scalar(c4, c4, 4.0, None, ALU.mult))
            t_bound.append(op("dve", [t], lambda e: e.tensor_scalar(c8, c4, -2.0, None, ALU.mult)))

        def relu_stage(y, post_t):
            UB = (4, 5, 6, 7)
            outs = lambda j: [ps[:, UB[j % 4], 0:256], ps[:, UB[j % 4], 256:512]]
            pair = lambda j: [("w_up", 2 * j), ("w_up", 2 * j + 1)]
            turns = []
            t_a, post_t = between(y, post_t, R_PRE_MLP, R_POST_MLP, "w_up", 0,
                                  turned(outs(0) + outs(1), (4, 5), turns))
            t_a = t_a[0] + t_a[1]
            tk = []

            def up(j):
                n = j + 2
                if n < 16:
                    t = s_mm(pair(n), act, outs(n), t_a + bank_t[UB[n % 4]])
                if j == 0:
                    tk.extend([[turn() for turn in turns][1]] * 2)
                if n < 16:
                    tk.append(t)
                return tk[j]

            def post(j, tu, free, before):
                b = UB[j % 4]
                r, q = htmp[j % 2][:, 0], htmp[j % 2][:, 1]
                hi, lo = hid[j % 4]
                pv = ps[:, b, :].rearrange("p (f t) -> p f t", f=2)
                t1 = op("act", [tu] + before, lambda e: e.activation(r, pv, ACT.Relu))
                bank_t[b] = [t1]
                t2 = op("act", [t1] + free, lambda e: e.activation(hi, r, ACT.Square))
                t3 = op("dve", [t1], lambda e: e.tensor_tensor(q, r, r, ALU.mult))
                t4 = op("dve", [t2, t3] + free, lambda e: e.tensor_tensor(lo, q, hi.bitcast(F32), ALU.subtract))
                return [t2, t4]
            return mlp("w_down", 16, up, post, lower_bounds), post_t

        y, t_post = relu_stage(y, t_bc)
        t_y = y[0]
        t_lb, t_c4 = t_bound

        Q = FF[:, 0:2048].rearrange("p (h t) -> p h t", h=8)
        K = FF[:, 2048:4096].rearrange("p (h t) -> p h t", h=8)
        E0 = FF[:, 4096:6144]
        E1 = FF[:, 6144:7168]
        V = FF[:, 7168:9216].rearrange("p (t n) -> p t n", t=2)
        G = FF[:, 9216:11264].rearrange("p (t n) -> p t n", t=2)
        AC = FF[:, 11264:13312].rearrange("p (h t) -> p h t", h=8)
        XC = FF[:, 4096:5120].rearrange("p (h t) -> p h t", h=8)
        sg = [FF[:, 13312 + 256 * i:13568 + 256 * i] for i in range(2)]
        E = E0.rearrange("p (h t) -> p h t", h=8)
        h_pair = lambda h: [("hgrn_w_in", h), ("hgrn_w_in", 8 + h)]
        h_bank = lambda h: 4 + h % 4
        h_outs = lambda h: [ps[:, h_bank(h), 0:256], ps[:, h_bank(h), 256:512]]
        t_v = []
        t_a2, t_bc = between(y, t_post, R_MIX0, R_HNORM, "hgrn_w_in", 2048,
                             copier(t_v, lambda tok: V[:, tok, 0:512], (6, 7), 512, t_y))
        t_a = t_a2[0] + t_a2[1]
        t_z = op("pool", t_y, lambda e: e.memset(AC, 0.0))
        sg_t = [[], []]
        t_hd = []
        for h in range(8):
            b = h_bank(h)
            tu = s_mm(h_pair(h), act, h_outs(h), t_a + bank_t[b])
            qv, fv = ps[:, b, 0:256], ps[:, b, 256:512]
            s = sg[h % 2]
            c = slice(h, h + 1)
            t1 = op("act", [tu] + sg_t[h % 2], lambda e, s=s, qv=qv: e.activation(s, qv, ACT.Sigmoid))
            t2 = op("act", [], lambda e, h=h, fv=fv: e.activation(E[:, h, :], fv, ACT.Sigmoid))
            t3 = op("act", [], lambda e, h=h, fv=fv: e.activation(K[:, h, :], fv, ACT.Sigmoid, scale=-1.0))
            t4 = op("dve", [t3], lambda e, h=h, s=s, qv=qv: e.tensor_tensor(Q[:, h, :], qv, s, ALU.mult))
            bank_t[b] = [t3, t4]
            sg_t[h % 2] = [t4]
            t5 = op("dve", [t2, t_lb], lambda e, h=h, c=c:
                    e.tensor_scalar(E[:, h, :], E[:, h, :], om[:, c], lb[:, c], ALU.mult, ALU.add))
            t6 = op("dve", [t3, t_lb], lambda e, h=h, c=c:
                    e.tensor_scalar(K[:, h, :], K[:, h, :], om[:, c], None, ALU.mult))
            t_hd.append([t4, t5, t6])

        t_gg = []
        fill = []
        for n in range(1, 4):
            banks = (2, 3) if n % 2 else (0, 1)
            if n < 2:
                end = copier(t_v, lambda tok, n=n: V[:, tok, 512 * n:512 * n + 512], banks, 512, t_y)
            else:
                def end(tok, t, n=n, banks=banks):
                    d = G[:, tok, 512 * n - 1024:512 * n - 512]
                    b = banks[tok]
                    t1 = op("act", [t], lambda e: e.activation(d, ps[:, b, :], ACT.Sigmoid))
                    t2 = op("dve", [t1], lambda e: e.tensor_tensor(d, ps[:, b, :], d, ALU.mult))
                    bank_t[b] = [t2]
                    t_gg.append(op("dve", [t2, t_bc], lambda e:
                                   e.tensor_tensor(d, d, bc[:, 512 * n - 1024:512 * n - 512], ALU.mult)))
            fill += a_pieces("hgrn_w_in", 2048 + 512 * n, 512, 8, 4, act, banks, t_a2, end, by_chunk=True)

        rd_t = [[], []]
        up_t = [t_hd[0] + t_hd[1] + t_hd[2] + t_hd[3], t_hd[4] + t_hd[5] + t_hd[6] + t_hd[7]]
        ac_t = [[t_z], [t_z]]
        e_t = [[], []]
        cur = [[E0[:, 1024 * g:1024 * g + 1024] for g in range(2)], [E1[:, 512 * g:512 * g + 512] for g in range(2)]]

        def level(g):
            b0 = 4 + 2 * g

            def go(eng):
                for h in range(4):
                    for blk in range(2):
                        s = TOK[blk]
                        c = 256 * (h % 2) + 128 * blk
                        last = eng.matmul(ps[:, b0 + h // 2, c:c + 128], K[:, 4 * g + h, s], Q[:, 4 * g + h, s],
                                          start=True, stop=True)
                return last
            t = op("pe", up_t[g] + bank_t[b0] + bank_t[b0 + 1], go)
            rd_t[g] = [t]

        def gather(g, lev, hs):
            b0 = 4 + 2 * g
            d = AC[:, 4 * g:4 * g + 4, :].rearrange("p h (b t) -> p (h b) t", t=128)
            m = hmask[:, lev, :].unsqueeze(1).to_broadcast([128, 8, 128])
            src = ps[:, b0:b0 + 2, :].rearrange("p b (c t) -> p (b c) t", t=128)
            if hs:
                d = d.rearrange("p b (n w s) -> p b n w s", w=2, s=hs)[:, :, :, 1, :]
                m = m.rearrange("p b (n w s) -> p b n w s", w=2, s=hs)[:, :, :, 1, :]
                src = src.rearrange("p b (n w s) -> p b n w s", w=2, s=hs)[:, :, :, 1, :]
            tc = op("dve", rd_t[g] + ac_t[g], lambda e: e.copy_predicated(d, m, src))
            bank_t[b0] = bank_t[b0 + 1] = [tc]
            ac_t[g] = [tc]

        def grow(g, hs):
            if hs == 0:
                qg, eg = Q[:, 4 * g:4 * g + 4, :], E[:, 4 * g:4 * g + 4, :]
                t = op("dve", rd_t[g] + up_t[g], lambda e: e.tensor_tensor(qg, qg, eg, ALU.mult))
                up_t[g] = up_t[g] + [t]
                return
            n = 1024 // (2 * hs)
            e2 = cur[0][g][:, 0:2 * n].rearrange("p (n w) -> p n w", w=2)
            q2 = FF[:, 1024 * g:1024 * g + 1024].rearrange("p (n w s) -> p n w s", w=2, s=hs)[:, :, 1, :]
            k2 = FF[:, 2048 + 1024 * g:3072 + 1024 * g].rearrange("p (n w s) -> p n w s", w=2, s=hs)[:, :, 0, :]
            f0 = e2[:, :, 0:1].to_broadcast([128, n, hs])
            f1 = e2[:, :, 1:2].to_broadcast([128, n, hs])
            nx = cur[1][g][:, 0:n]
            t1 = op("dve", rd_t[g] + up_t[g] + e_t[g], lambda e: e.tensor_tensor(q2, q2, f0, ALU.mult))
            t2 = op("pool", rd_t[g] + up_t[g] + e_t[g], lambda e: e.tensor_tensor(k2, k2, f1, ALU.mult))
            if hs < 64:
                e_t[g] = [op("pool", up_t[g] + e_t[g], lambda e:
                             e.tensor_tensor(nx, e2[:, :, 0], e2[:, :, 1], ALU.mult))]
            up_t[g] = [t1, t2]

        hs = 0
        for lev in range(8):
            for g in range(2):
                level(g)
                if len(fill) > 1:
                    fill.pop(0)()
                grow(g, hs)
                gather(g, lev, hs)
            if hs:
                cur.reverse()
            hs = max(1, 2 * hs)
        fill.pop(0)()
        t_oh, t_xc = [], []

        def mix_v(tok):
            for g in range(2):
                def go(eng, g=g):
                    for h in range(4 * g, 4 * g + 4):
                        o = ps[:, 2 * tok + g, 128 * (h % 4):128 * (h % 4) + 128]
                        c = slice(128 * h, 128 * h + 128)
                        if tok:
                            eng.matmul(o, XC[:, h, :], V[:, 0, c], start=True, stop=False)
                        last = eng.matmul(o, AC[:, h, TOK[tok]], V[:, tok, c], start=not tok, stop=True)
                    return last
                t_oh.append(op("pe", (t_xc if tok else []) + ac_t[g] + t_v + bank_t[2 * tok + g], go))
        mix_v(0)
        for g in range(2):
            b0 = 4 + 2 * g

            def go(eng, g=g, b0=b0):
                for h in range(4):
                    last = eng.matmul(ps[:, b0, 128 * h:128 * h + 128], K[:, 4 * g + h, 0:128], Q[:, 4 * g + h, 128:256],
                                      start=True, stop=True)
                return last
            t = op("pe", up_t[g] + bank_t[b0], go)
            d = XC[:, 4 * g:4 * g + 4, :].rearrange("p h t -> p (h t)")
            te = op("act", [t] + up_t[0] + up_t[1] + e_t[0] + e_t[1], lambda e, d=d, b0=b0:
                    e.activation(d, ps[:, b0, :], ACT.Copy))
            bank_t[b0] = [te]
            t_xc.append(te)
        mix_v(1)
        t_mt = [[], []]

        def head_norm(tok):
            y = ps[:, 2 * tok:2 * tok + 2, :]
            d = xn[:, tok, :].rearrange("p (b n) -> p b n", b=2)
            t1 = op("act", [t_oh[2 * tok + 1]], lambda e: e.activation(d, y, ACT.Square))
            ss = stats(8)
            t2 = op("dve", [t1], lambda e:
                    e.tensor_reduce(ss, xn[:, tok, :].rearrange("p (h n) -> p h n", h=8), AX, ALU.add))
            rs, tp = power(ss, 8, 1.0 / 128, [t2])
            t3 = op("dve", t_gg + [t2], lambda e:
                    e.tensor_tensor(d, y, G[:, tok, :].rearrange("p (b n) -> p b n", b=2), ALU.mult))
            bank_t[2 * tok] = bank_t[2 * tok + 1] = [t3]
            v = xn[:, tok, :].rearrange("p (h n) -> p h n", h=8)
            return [[op("dve", [t3, tp], lambda e, c=c:
                        e.tensor_tensor(v[:, c:c + 4, :], v[:, c:c + 4, :],
                                        rs[:, c:c + 4].unsqueeze(2).to_broadcast([128, 4, 128]), ALU.mult))]
                    for c in (0, 4)]

        def flip_heads(tok, halves):
            t_mt[tok] += flip_tok(lambda k: xn[:, tok, 128 * k:128 * k + 128], 8,
                                  (4 + 2 * tok, 5 + 2 * tok), act, tok, halves, [])
        halves = head_norm(0)
        flip_heads(0, halves)
        halves = head_norm(1)
        y = project("hgrn_w_out", t_mt, lambda: flip_heads(1, halves))

        def swiglu(layer, row, y, post_row=None):
            def pair(f):
                return [(f"ffn_in{layer}", f), (f"ffn_in{layer}", 22 + f)]

            def outs(f):
                b = 4 + f % 4
                return [ps[:, b, 0:256], ps[:, b, 256:512]]
            turns = []
            o = outs(0) + outs(1)
            t_a, post_t = between(y, None, row, post_row, f"ffn_first{layer}", 0,
                                  turned([o[0], o[2], o[1], o[3]], (4, 5), turns))
            t_a = t_a[0] + t_a[1]

            def up(j):
                if j == 0:
                    s_mm(pair(2), act, outs(2), t_a + bank_t[6])
                    return [turn() for turn in turns][1]
                for f in (2 * j, 2 * j + 1):
                    if f > 2:
                        t = s_mm(pair(f), act, outs(f), t_a + bank_t[4 + f % 4])
                return t

            def post(j, tu, free, before):
                b = 4 + 2 * (j % 2)
                gv, uv = ps[:, b:b + 2, 0:256], ps[:, b:b + 2, 256:512]
                s, q = htmp[j % 2][:, 0], htmp[j % 2][:, 1]
                hi, lo = hid[j % 4]
                t1 = op("act", [tu] + before, lambda e: e.activation(s, gv, ACT.Sigmoid))
                t2 = op("dve", [t1], lambda e: e.tensor_tensor(s, gv, s, ALU.mult))
                t3 = op("dve", [t2], lambda e: e.tensor_tensor(q, uv, s, ALU.mult))
                bank_t[b] = bank_t[b + 1] = [t3]
                t4 = op("act", [t3] + free, lambda e: e.activation(hi, q, ACT.Copy))
                t5 = op("dve", [t4], lambda e: e.tensor_tensor(lo, q, hi.bitcast(F32), ALU.subtract))
                return [t4, t5]
            return mlp(f"ffn_out{layer}", 11, up, post), post_t

        y, _ = swiglu(0, R_FFN0, y)
        t_y = y[0]

        l_pair = lambda f: [("lru_w_in", f), ("lru_w_in", 8 + f)]
        l_bank = lambda f: (0 if f // 2 == 1 else 4) + f % 2
        l_outs = lambda f: [ps[:, l_bank(f), 0:256], ps[:, l_bank(f), 256:512]]
        turns = []
        o = l_outs(0) + l_outs(1)
        t_a, _ = between(y, None, R_MIX1, None, "lru_first", 0, turned([o[0], o[2], o[1], o[3]], (4, 5), turns))
        t_a = t_a[0] + t_a[1]

        def buf(off, width, count):
            return [FF[:, off + 2 * width * i:off + 2 * width * (i + 1)].rearrange("p (f t) -> p f t", f=2)
                    for i in range(count)]
        Y, U, UC = buf(0, 256, 4), buf(2048, 260, 4), buf(4128, 256, 4)
        RG, IG, VV, SQ = buf(6176, 256, 2), buf(7200, 256, 2), buf(8224, 256, 2), buf(9248, 256, 2)
        WW, QQ = buf(10272, 256, 2), buf(11296, 256, 2)
        uP = [tuple(RR[:, (2 * j + i) * 512:(2 * j + i + 1) * 512].rearrange("p (f t) -> p f t", f=2)
                    for i in range(2)) for j in range(2)]
        hP = [tuple(RR[:, 2048 + (2 * j + i) * 512:2048 + (2 * j + i + 1) * 512].rearrange("p (f t) -> p f t", f=2)
                    for i in range(2)) for j in range(2)]
        t_p = [op("pool", t_y, lambda e, i=i: e.memset(U[i][:, :, 0:3], 0.0)) for i in range(4)]
        unit = [{} for _ in range(4)]

        def lru_in(f):
            t = s_mm(l_pair(f), act, l_outs(f), t_a + bank_t[l_bank(f)])
            unit[f // 2]["in"] = [t]

        def lru_conv(n):
            b = l_bank(2 * n)
            unit[n]["y"] = op("act", unit[n]["in"] + t_y, lambda e:
                              e.activation(Y[n], ps[:, b:b + 2, 0:256], ACT.Gelu_apprx_tanh))
            t2 = op("act", [], lambda e: e.activation(U[n][:, :, 3:259], ps[:, b:b + 2, 256:512], ACT.Copy))
            bank_t[b] = bank_t[b + 1] = [t2]
            t3 = [None, None]
            for tap in range(4):
                for c in range(2):
                    w = C_CONVW + 8 * tap + 2 * n + c
                    wc = cols[:, w:w + 1]
                    if tap == 0:
                        cb = cols[:, C_CONVB + 2 * n + c:C_CONVB + 2 * n + c + 1]
                        t3[c] = op("dve", [t2, t_p[n], t_in], lambda e, c=c, wc=wc, cb=cb:
                                   e.tensor_scalar(UC[n][:, c, :], U[n][:, c, 0:256], wc, cb, ALU.mult, ALU.add))
                    else:
                        t3[c] = op("dve", [t3[c]], lambda e, c=c, tap=tap, wc=wc: e.scalar_tensor_tensor(
                            UC[n][:, c, :], U[n][:, c, tap:tap + 256], wc, UC[n][:, c, :], ALU.mult, ALU.add))
            unit[n]["conv"] = t3

        def lru_split(n):
            hi, lo = uP[n % 2]
            old = unit[n - 2]["gate"] if n >= 2 else []
            th = op("act", unit[n]["conv"] + old, lambda e: e.activation(hi, UC[n], ACT.Copy))
            tl = op("dve", [th], lambda e: e.tensor_tensor(lo, UC[n], hi.bitcast(F32), ALU.subtract))
            unit[n]["u"] = [th, tl]

        def lru_gate(n, upto):
            i = n % 2
            h, l, wt = take(("g", n), upto=upto)
            hi, lo = uP[i]

            def go(eng):
                for m in range(2):
                    for fo in range(2):
                        for k in range(2):
                            w0 = (2 * m + k) * 256 + 128 * fo
                            w = slice(w0, w0 + 128)
                            last = mm3(eng, ps[:, 6 + m, 256 * fo:256 * fo + 256], (h[:, w], l[:, w]),
                                       (hi[:, k, :], lo[:, k, :]), k == 0, k == 1)
                return last
            t = op("pe", wt + unit[n]["u"] + bank_t[6] + bank_t[7], go)
            done_t.append(t)
            unit[n]["gate"] = [t]
            old = [unit[n - 2]["w"]] if n >= 2 else []
            for m, (dst, col) in enumerate(((RG, C_BA), (IG, C_BX))):
                for fo in range(2):
                    f = 2 * n + fo
                    te = op("act", [t] + old, lambda e, dst=dst, col=col, f=f, fo=fo, bb=6 + m:
                            e.activation(dst[i][:, fo, :], ps[:, bb, 256 * fo:256 * fo + 256], ACT.Sigmoid,
                                         bias=cols[:, col + f:col + f + 1]))
                bank_t[6 + m] = [te]
            unit[n]["sig"] = te
            unit[n]["x"] = op("pool", [te], lambda e: e.tensor_tensor(IG[i], IG[i], UC[n], ALU.mult))

        def lru_scan(n):
            i, te = n % 2, unit[n]["sig"]
            for fo in range(2):
                tv = op("act", [te, t_c4], lambda e, fo=fo, f=2 * n + fo:
                        e.activation(VV[i][:, fo, :], RG[i][:, fo, :], ACT.Tanh, scale=c4[:, f:f + 1]))
            for fo in range(2):
                ta = op("act", [te], lambda e, fo=fo, f=2 * n + fo:
                        e.activation(QQ[i][:, fo, :], RG[i][:, fo, :], ACT.Exp, scale=c8[:, f:f + 1]))
            ts = op("act", [tv], lambda e: e.activation(SQ[i], VV[i], ACT.Sqrt))
            flat = lambda x: x.rearrange("p f t -> p (f t)")
            t2 = op("dve", [ta, tv], lambda e: e.scalar_tensor_tensor(
                flat(RG[i]), flat(QQ[i]), 1.0, flat(VV[i]), ALU.add, ALU.mult))
            t3 = op("dve", [t2], lambda e: e.tensor_scalar(RG[i], RG[i], -1.0, 1.0, ALU.mult, ALU.add))
            t4 = op("dve", [ts], lambda e: e.scalar_tensor_tensor(
                flat(SQ[i]), flat(QQ[i]), 1.0, flat(SQ[i]), ALU.add, ALU.mult))
            t5 = op("dve", [t4, unit[n]["x"]], lambda e: e.tensor_tensor(SQ[i], SQ[i], IG[i], ALU.mult))
            old = unit[n - 2]["end"] if n >= 2 else []
            for fo in range(2):
                t6 = op("dve", [t5, t3] + old, lambda e, fo=fo: e.tensor_tensor_scan(
                    WW[i][:, fo, :], RG[i][:, fo, :], SQ[i][:, fo, :], 0.0, ALU.mult, ALU.add))
            unit[n]["w"] = op("dve", [t6, unit[n]["y"]], lambda e: e.tensor_tensor(WW[i], WW[i], Y[n], ALU.mult))

        def lru_hidden(n):
            i, t7 = n % 2, unit[n]["w"]
            ho, lw_ = hP[i]
            free = unit[n - 2]["down"] if n >= 2 else []
            t8 = op("act", [t7] + free, lambda e: e.activation(ho, WW[i], ACT.Copy))
            t9 = op("dve", [t8], lambda e: e.tensor_tensor(lw_, WW[i], ho.bitcast(F32), ALU.subtract))
            unit[n]["end"] = [t8, t9]

        def lru_down(n, upto):
            part = take(("d", "lru_w_out", n), upto=upto)
            out = [d_part(part, tok, hP[n % 2], 0, n == 0, n == 3, unit[n]["end"]) for tok in range(2)]
            done_t.append(out[1])
            unit[n]["down"] = [out[1]]

        every = len(chunks)
        upto = chunks.index((("d", "lru_w_out", 3), 2048)) + 1
        lru_in(2)
        unit[0]["in"] = [[turn() for turn in turns][1]]
        lru_conv(0)
        lru_split(0)
        lru_in(3)
        lru_conv(1)
        lru_in(4)
        lru_gate(0, every)
        lru_split(1)
        lru_in(5)
        lru_conv(2)
        lru_scan(0)
        lru_split(2)
        lru_gate(1, every)
        lru_in(6)
        lru_hidden(0)
        lru_scan(1)
        lru_in(7)
        lru_conv(3)
        lru_gate(2, every)
        lru_split(3)
        lru_hidden(1)
        lru_down(0, upto)
        lru_scan(2)
        lru_gate(3, upto)
        lru_down(1, upto)
        lru_hidden(2)
        lru_scan(3)
        lru_down(2, upto)
        lru_hidden(3)
        pump(upto + 2)
        end = unit[3]["end"]
        y = d_group("lru_w_out", (3,), (hP[1],), (0,), False, ((end, end),), upto + 2)
        y, t_b = swiglu(1, R_FFN1, y, R_FINAL)

        t_y, rest = y
        for tok in range(2):
            if tok:
                rest(lambda: None)
            t = residual(tok, t_y[tok], None)
            halves = norm_tok(tok, xr[:, tok, :], 1024, xn[:, tok, :], bc[:, :], t_b, [t])
            for c in range(2):
                t_out = dma("out", halves[c], out_d[128 * tok:128 * tok + 128, 512 * c:512 * c + 512],
                            xn[:, tok, 512 * c:512 * c + 512])
        wait("sp", [t_out])
        assert len(done_t) == len(chunks)

        block = ctx.enter_context(nc.Block())

        @block.sync
        def _(eng):
            for f in queue["sp"]:
                f(eng)

        @block.gpsimd
        def _(eng):
            for f in queue["pool"]:
                f(eng)

        @block.scalar
        def _(eng):
            for f in queue["act"]:
                f(eng)

        @block.vector
        def _(eng):
            for f in queue["dve"]:
                f(eng)

        @block.tensor
        def _(eng):
            for f in queue["pe"]:
                f(eng)


def kernel(**inputs):
    import concourse.bacc as bacc
    from concourse.bass_utils import run_bass_kernel_spmd

    a = {k: np.asarray(v) for k, v in inputs.items()}
    w = {
        "w_in": a["w_in"][0], "w_uq": a["w_uq"][0], "w_ukv": a["w_ukv"][0],
        "w_branch_a": a["w_branch_a"][0], "w_branch_b": a["w_branch_b"][0], "w_out": a["w_out"][0],
        "w_up": a["w_up"][0], "w_down": a["w_down"][0],
        "hgrn_w_in": a["hgrn_w_in_2"][0], "hgrn_w_out": a["hgrn_w_out_2"][0],
        "lru_w_in": a["lru_w_in_2"][0], "lru_w_out": a["lru_w_out_2"][0],
        "w_ukv_v": a["w_ukv"][0].reshape(256, 8, 128)[:, :, 64:].reshape(256, 512),
        "ffn_first0": np.concatenate([a["ffn_w_in_2"][0][:, c:c + 256] for c in (0, 2816)], axis=1),
        "ffn_first1": np.concatenate([a["ffn_w_in_2"][1][:, c:c + 256] for c in (0, 2816)], axis=1),
        "lru_first": np.concatenate([a["lru_w_in_2"][0][:, c:c + 256] for c in (0, 1024)], axis=1),
        "lru_wa": a["lru_wa_2"][0], "lru_wx": a["lru_wx_2"][0],
        "ffn_in0": a["ffn_w_in_2"][0], "ffn_in1": a["ffn_w_in_2"][1],
        "ffn_out0": a["ffn_w_out_2"][0], "ffn_out1": a["ffn_w_out_2"][1],
    }
    stream = np.concatenate([np.ascontiguousarray(lay_chunk(w, key)).reshape(-1) for key, _ in chunk_list()])

    def col(v):
        return v.reshape(-1, 128).T

    cols = np.ascontiguousarray(np.concatenate(
        [col(a["hgrn_lb_2"][0]), col(a["hgrn_lb_2"][1]), col(a["lru_conv_b_2"][0]), col(a["lru_ba_2"][0]),
         col(a["lru_bx_2"][0]), col(a["lru_lambda_2"][0])] + [col(a["lru_conv_w_2"][0][t]) for t in range(4)], axis=1))
    rows = np.concatenate([
        a["g_pre_mix"][0], a["g_post_mix"][0], a["g_pre_mlp"][0], a["g_post_mlp"][0],
        a["norm_mix_2"][0], a["norm_mix_2"][1], a["norm_ffn_2"][0], a["norm_ffn_2"][1], a["norm_final_2"],
        a["b_gate"][0], np.tile(a["hgrn_norm_2"][0], 8), a["g_q_norm"][0], a["g_kv_norm"][0]])

    def inv_freq(r):
        return np.power(np.float32(500000.0), -np.arange(r // 2, dtype=np.float32) * np.float32(2.0 / r))

    const = np.zeros((128, 1560), np.float32)
    const[:, 0:128] = np.eye(128)
    tri = np.where(np.arange(128)[None, :] <= np.arange(128)[:, None], 0.0, -1e38)
    const[:, 128:256] = tri
    const[:, 384:512] = tri
    const[:, 512:520] = inv_freq(16)
    const[:, 520:536] = inv_freq(32)
    s, t = np.arange(128)[:, None], np.arange(128)[None, :]
    mask = np.zeros((128, 8, 128), np.float32)
    mask[:, 0] = s == t
    for n in range(7):
        h = 1 << n
        mask[:, n + 1] = ((t // h) % 2 == 1) & (s // h == t // h - 1)

    const[:, 536:] = mask.reshape(128, 1024)

    arrays = {
        "x_in": np.ascontiguousarray(a["x"][0]),
        "pos_in": np.ascontiguousarray(a["positions"].reshape(2, 128).T.astype(np.int32)),
        "w_stream": stream, "cols_in": cols, "rows_in": rows, "const_in": const,
    }
    nc = bacc.Bacc("TRN2", target_bir_lowering=False, num_devices=1)
    args = [nc.dram_tensor(k, v.shape, mybir.dt.from_np(v.dtype), kind="ExternalInput").ap()
            for k, v in arrays.items()]
    args.append(nc.dram_tensor("out_0", (256, 1024), F32, kind="ExternalOutput").ap())
    program(nc, *args)
    r = run_bass_kernel_spmd(nc, [arrays], core_ids=[0])
    return r.results[0]["out_0"].reshape(1, 256, 1024)
```
